# Optimizing a Trainium2 kernel written in Bass

```python
import math
import jax, jax.numpy as jnp
from jax import lax
import numpy as np

D_MODEL = 1024
BATCH = 1
SEQ = 512
DEPTH = 2

MLA_HEADS = 4
MLA_Q_LORA = 256
MLA_KV_LORA = 128
MLA_D_NOPE = 128
MLA_D_ROPE = 64
MLA_D_V = 128
ROPE_THETA = 10000.0

DIFF_HEADS = 4
DIFF_D_QK = 64
DIFF_D_V = 2 * DIFF_D_QK

SSD_HEADS = 16
SSD_HEAD_DIM = 64
SSD_D_INNER = SSD_HEADS * SSD_HEAD_DIM
SSD_GROUPS = 4
SSD_STATE = 128
SSD_CONV = 4
SSD_CHUNK = 128
SSD_CONV_DIM = SSD_D_INNER + 2 * SSD_GROUPS * SSD_STATE

D_MIX = MLA_HEADS * MLA_D_V + DIFF_HEADS * DIFF_D_V + SSD_D_INNER

IN_SIZES = (MLA_Q_LORA, MLA_KV_LORA, MLA_D_ROPE,
            DIFF_HEADS * 2 * DIFF_D_QK, DIFF_HEADS * 2 * DIFF_D_QK, DIFF_HEADS * DIFF_D_V,
            SSD_D_INNER, SSD_CONV_DIM, SSD_HEADS)
N_IN = sum(IN_SIZES)

MOE_GROUPS = 4
MOE_EXPERTS_PER_GROUP = 8
N_EXPERTS = MOE_GROUPS * MOE_EXPERTS_PER_GROUP
MOE_TOP_K = 2
D_EXPERT = 512
MOE_BLOCK = 128

Q_BLOCK = 128
NORM_EPS = 1e-6
SUBLN_EPS = 1e-5

kernel_name = 'hybrid_mla_diff_ssd_hmoe'

def rmsnorm(x, w, eps=NORM_EPS):
    xf = x.astype(jnp.float32)
    y = xf * lax.rsqrt(jnp.mean(xf * xf, axis=-1, keepdims=True) + eps)
    return (y * w.astype(jnp.float32)).astype(x.dtype)

def modulate(h, shift, scale):
    return h * (1 + scale[:, None, :]) + shift[:, None, :]

def rope_tables(positions, dim, dtype):
    inv = 1.0 / (ROPE_THETA ** (jnp.arange(0, dim, 2, dtype=jnp.float32) / dim))
    ang = positions.astype(jnp.float32)[..., None] * inv
    ang = jnp.concatenate([ang, ang], axis=-1)
    return jnp.cos(ang).astype(dtype), jnp.sin(ang).astype(dtype)

def apply_rope(t, cos, sin):
    half = t.shape[-1] // 2
    rot = jnp.concatenate([-t[..., half:], t[..., :half]], axis=-1)
    return t * cos + rot * sin

def to_query_blocks(t):
    nb = t.shape[1] // Q_BLOCK
    return t.reshape(t.shape[0], nb, Q_BLOCK, *t.shape[2:]).swapaxes(0, 1)

def from_query_blocks(t):
    t = t.swapaxes(0, 1)
    return t.reshape(t.shape[0], t.shape[1] * t.shape[2], *t.shape[3:])

def causal_block_mask(i, s):
    q_idx = i * Q_BLOCK + jnp.arange(Q_BLOCK)
    return q_idx[:, None] >= jnp.arange(s)[None, :]

def mla_group(cq, ckv, k_pe, positions, q_norm_w, w_uq, kv_norm_w, w_ukv):
    bsz, s, _ = cq.shape
    q = (rmsnorm(cq, q_norm_w) @ w_uq).reshape(bsz, s, MLA_HEADS, MLA_D_NOPE + MLA_D_ROPE)
    kv = (rmsnorm(ckv, kv_norm_w) @ w_ukv).reshape(bsz, s, MLA_HEADS, MLA_D_NOPE + MLA_D_V)
    q_nope, q_pe = q[..., :MLA_D_NOPE], q[..., MLA_D_NOPE:]
    k_nope, v = kv[..., :MLA_D_NOPE], kv[..., MLA_D_NOPE:]
    cos, sin = rope_tables(positions, MLA_D_ROPE, cq.dtype)
    q_pe = apply_rope(q_pe, cos[:, :, None], sin[:, :, None])
    k_pe = apply_rope(k_pe, cos, sin)
    scale = (MLA_D_NOPE + MLA_D_ROPE) ** -0.5

    def block(args):
        qn, qp, i = args
        sc = (jnp.einsum('bqhd,bkhd->bhqk', qn, k_nope)
              + jnp.einsum('bqhd,bkd->bhqk', qp, k_pe)).astype(jnp.float32) * scale
        sc = jnp.where(causal_block_mask(i, s), sc, -jnp.inf)
        p = jax.nn.softmax(sc, axis=-1).astype(v.dtype)
        return jnp.einsum('bhqk,bkhd->bqhd', p, v)

    nb = s // Q_BLOCK
    out = lax.map(block, (to_query_blocks(q_nope), to_query_blocks(q_pe), jnp.arange(nb)))
    return from_query_blocks(out).reshape(bsz, s, MLA_HEADS * MLA_D_V)

def diff_group(q, k, v, positions, lambdas, subln_w, layer_idx):
    bsz, s, _ = q.shape
    q = q.reshape(bsz, s, DIFF_HEADS, 2, DIFF_D_QK)
    k = k.reshape(bsz, s, DIFF_HEADS, 2, DIFF_D_QK)
    v = v.reshape(bsz, s, DIFF_HEADS, DIFF_D_V)
    lam_init = 0.8 - 0.6 * math.exp(-0.3 * layer_idx)
    lf = lambdas.astype(jnp.float32)
    lam = jnp.exp(jnp.sum(lf[0] * lf[1])) - jnp.exp(jnp.sum(lf[2] * lf[3])) + lam_init
    slopes = jnp.exp2(-8.0 / DIFF_HEADS * jnp.arange(1, DIFF_HEADS + 1, dtype=jnp.float32))
    pos_k = positions.astype(jnp.float32)
    scale = DIFF_D_QK ** -0.5

    def block(args):
        qb, pq, i = args
        sc = jnp.einsum('bqhmd,bkhmd->bhmqk', qb, k).astype(jnp.float32) * scale
        dist = jnp.abs(pq.astype(jnp.float32)[:, :, None] - pos_k[:, None, :])
        sc = sc - slopes[None, :, None, None, None] * dist[:, None, None]
        sc = jnp.where(causal_block_mask(i, s), sc, -jnp.inf)
        p = jax.nn.softmax(sc, axis=-1)
        attn = (p[:, :, 0] - lam * p[:, :, 1]).astype(v.dtype)
        return jnp.einsum('bhqk,bkhe->bqhe', attn, v)

    nb = s // Q_BLOCK
    out = from_query_blocks(lax.map(block, (to_query_blocks(q), to_query_blocks(positions), jnp.arange(nb))))
    out = rmsnorm(out, subln_w, SUBLN_EPS) * (1.0 - lam_init)
    return out.reshape(bsz, s, DIFF_HEADS * DIFF_D_V)

def causal_depthwise_conv(u, w, b):
    y = lax.conv_general_dilated(u, w[:, None, :], window_strides=(1,), padding=[(SSD_CONV - 1, 0)],
                                 dimension_numbers=('NWC', 'WIO', 'NWC'), feature_group_count=u.shape[-1])
    return y + b

def ssd_chunked(x, dt, a, bm, cm):
    bsz, s, nh, p = x.shape
    nc = s // SSD_CHUNK
    r = nh // SSD_GROUPS
    xdt = (x * dt[..., None].astype(x.dtype)).reshape(bsz, nc, SSD_CHUNK, SSD_GROUPS, r, p)
    adt = (dt * a).reshape(bsz, nc, SSD_CHUNK, SSD_GROUPS, r).transpose(0, 3, 4, 1, 2)
    bc = bm.reshape(bsz, nc, SSD_CHUNK, SSD_GROUPS, SSD_STATE)
    cc = cm.reshape(bsz, nc, SSD_CHUNK, SSD_GROUPS, SSD_STATE)
    a_cs = jnp.cumsum(adt, axis=-1)
    tril = jnp.tril(jnp.ones((SSD_CHUNK, SSD_CHUNK), dtype=bool))
    seg = a_cs[..., :, None] - a_cs[..., None, :]
    decay_in = jnp.exp(jnp.where(tril, seg, -jnp.inf)).astype(x.dtype)
    cb = jnp.einsum('bclgn,bcsgn->bcgls', cc, bc)
    y_diag = jnp.einsum('bcgls,bgrcls,bcsgrp->bclgrp', cb, decay_in, xdt)
    decay_to_end = jnp.exp(a_cs[..., -1:] - a_cs).astype(x.dtype)
    states = jnp.einsum('bclgn,bgrcl,bclgrp->bcgrpn', bc, decay_to_end, xdt)
    chunk_tot = jnp.pad(a_cs[..., -1], ((0, 0), (0, 0), (0, 0), (1, 0)))
    ccs = jnp.cumsum(chunk_tot, axis=-1)
    trilc = jnp.tril(jnp.ones((nc + 1, nc + 1), dtype=bool))
    decay_chunk = jnp.exp(jnp.where(trilc, ccs[..., :, None] - ccs[..., None, :], -jnp.inf)).astype(x.dtype)
    states = jnp.concatenate([jnp.zeros_like(states[:, :1]), states], axis=1)
    entering = jnp.einsum('bgrzk,bkgrpn->bzgrpn', decay_chunk, states)[:, :-1]
    y_off = jnp.einsum('bclgn,bcgrpn,bgrcl->bclgrp', cc, entering, jnp.exp(a_cs).astype(x.dtype))
    return (y_diag + y_off).reshape(bsz, s, nh, p)

def ssd_group(z, xbc, dt_raw, conv_w, conv_b, dt_bias, a_log, d_skip, norm_w):
    bsz, s, _ = z.shape
    xbc = jax.nn.silu(causal_depthwise_conv(xbc, conv_w, conv_b))
    xs, bm, cm = jnp.split(xbc, [SSD_D_INNER, SSD_D_INNER + SSD_GROUPS * SSD_STATE], axis=-1)
    xs = xs.reshape(bsz, s, SSD_HEADS, SSD_HEAD_DIM)
    bm = bm.reshape(bsz, s, SSD_GROUPS, SSD_STATE)
    cm = cm.reshape(bsz, s, SSD_GROUPS, SSD_STATE)
    dt = jax.nn.softplus(dt_raw.astype(jnp.float32) + dt_bias.astype(jnp.float32))
    a = -jnp.exp(a_log.astype(jnp.float32))
    y = ssd_chunked(xs, dt, a, bm, cm) + xs * d_skip[:, None]
    y = (y.reshape(bsz, s, SSD_D_INNER) * jax.nn.silu(z)).reshape(bsz, s, SSD_GROUPS, SSD_D_INNER // SSD_GROUPS)
    y = rmsnorm(y, norm_w.reshape(SSD_GROUPS, SSD_D_INNER // SSD_GROUPS))
    return y.reshape(bsz, s, SSD_D_INNER)

def hybrid_mixer(h, positions, layer_idx, w_in, mla_q_norm_w, mla_w_uq, mla_kv_norm_w, mla_w_ukv,
                 diff_lambda, diff_subln_w, ssd_conv_w, ssd_conv_b, ssd_dt_bias, ssd_a_log, ssd_d,
                 ssd_norm_w, w_out):
    proj = h @ w_in
    split_at = [int(o) for o in np.cumsum(IN_SIZES)[:-1]]
    cq, ckv, k_pe, dq, dk, dv, z, xbc, dt = jnp.split(proj, split_at, axis=-1)
    y_mla = mla_group(cq, ckv, k_pe, positions, mla_q_norm_w, mla_w_uq, mla_kv_norm_w, mla_w_ukv)
    y_diff = diff_group(dq, dk, dv, positions, diff_lambda, diff_subln_w, layer_idx)
    y_ssd = ssd_group(z, xbc, dt, ssd_conv_w, ssd_conv_b, ssd_dt_bias, ssd_a_log, ssd_d, ssd_norm_w)
    return jnp.concatenate([y_mla, y_diff, y_ssd], axis=-1) @ w_out

def hier_moe(h, w_group, b_group, w_expert, b_expert, w_gate, w_up, w_down):
    bsz, s, d = h.shape
    t = bsz * s
    hf = h.reshape(t, d)
    pg = jax.nn.softmax((hf @ w_group + b_group).astype(jnp.float32), axis=-1)
    pg_top, g_sel = lax.top_k(pg, 1)
    le = (hf @ w_expert + b_expert).astype(jnp.float32).reshape(t, MOE_GROUPS, MOE_EXPERTS_PER_GROUP)
    le_sel = jnp.take_along_axis(le, g_sel[:, :, None], axis=1)[:, 0]
    pe_top, e_top = lax.top_k(jax.nn.softmax(le_sel, axis=-1), MOE_TOP_K)
    gate_w = pg_top * pe_top / jnp.sum(pe_top, axis=-1, keepdims=True)
    eid = g_sel * MOE_EXPERTS_PER_GROUP + e_top
    flat_e = eid.reshape(-1)
    flat_w = gate_w.reshape(-1)
    flat_tok = jnp.repeat(jnp.arange(t, dtype=jnp.int32), MOE_TOP_K)
    order = jnp.argsort(flat_e)
    se, stok, sw = flat_e[order], flat_tok[order], flat_w[order]
    counts = jnp.bincount(flat_e, length=N_EXPERTS)
    pcounts = (counts + MOE_BLOCK - 1) // MOE_BLOCK * MOE_BLOCK
    pend = jnp.cumsum(pcounts)
    pstart = pend - pcounts
    start = jnp.cumsum(counts) - counts
    dest = pstart[se] + jnp.arange(t * MOE_TOP_K) - start[se]
    cap = t * MOE_TOP_K + N_EXPERTS * MOE_BLOCK
    nb = cap // MOE_BLOCK
    btok = jnp.zeros((cap,), jnp.int32).at[dest].set(stok)
    bw = jnp.zeros((cap,), jnp.float32).at[dest].set(sw)
    bexp = jnp.clip(jnp.searchsorted(pend, jnp.arange(nb) * MOE_BLOCK, side='right'), 0, N_EXPERTS - 1)
    xb = hf[btok].reshape(nb, MOE_BLOCK, d)

    def expert_block(args):
        xblk, e = args
        return (jax.nn.silu(xblk @ w_gate[e]) * (xblk @ w_up[e])) @ w_down[e]

    yb = lax.map(expert_block, (xb, bexp)).reshape(cap, d)
    y = jnp.zeros_like(hf).at[btok].add(yb * bw[:, None].astype(yb.dtype))
    return y.reshape(bsz, s, d)

def setup_inputs(seed: int = 0) -> dict:
    key = jax.random.key(seed)
    ks = jax.random.split(key, 32)
    L = DEPTH

    def nrm(k, shape, scale):
        return jax.random.normal(k, shape, jnp.float32) * scale

    def gain(k, shape):
        return 1.0 + 0.05 * jax.random.normal(k, shape, jnp.float32)

    dt0 = jnp.exp(jax.random.uniform(ks[16], (L, SSD_HEADS), jnp.float32, math.log(1e-3), math.log(1e-1)))
    return {
        'x': nrm(ks[0], (BATCH, SEQ, D_MODEL), 1.0),
        'c': nrm(ks[1], (BATCH, D_MODEL), 1.0),
        'positions': jnp.broadcast_to(jnp.arange(SEQ, dtype=jnp.int32), (BATCH, SEQ)),
        'w_ada': nrm(ks[2], (L, D_MODEL, 6 * D_MODEL), D_MODEL ** -0.5),
        'b_ada': nrm(ks[3], (L, 6 * D_MODEL), 0.02),
        'norm1_w': gain(ks[4], (L, D_MODEL)),
        'w_in': nrm(ks[5], (L, D_MODEL, N_IN), D_MODEL ** -0.5),
        'mla_q_norm_w': gain(ks[6], (L, MLA_Q_LORA)),
        'mla_w_uq': nrm(ks[7], (L, MLA_Q_LORA, MLA_HEADS * (MLA_D_NOPE + MLA_D_ROPE)), MLA_Q_LORA ** -0.5),
        'mla_kv_norm_w': gain(ks[8], (L, MLA_KV_LORA)),
        'mla_w_ukv': nrm(ks[9], (L, MLA_KV_LORA, MLA_HEADS * (MLA_D_NOPE + MLA_D_V)), MLA_KV_LORA ** -0.5),
        'diff_lambda': nrm(ks[10], (L, 4, DIFF_D_QK), 0.1),
        'diff_subln_w': gain(ks[11], (L, DIFF_D_V)),
        'ssd_conv_w': nrm(ks[12], (L, SSD_CONV, SSD_CONV_DIM), SSD_CONV ** -0.5),
        'ssd_conv_b': nrm(ks[13], (L, SSD_CONV_DIM), 0.02),
        'ssd_dt_bias': dt0 + jnp.log(-jnp.expm1(-dt0)),
        'ssd_a_log': jnp.log(jax.random.uniform(ks[14], (L, SSD_HEADS), jnp.float32, 1.0, 16.0)),
        'ssd_d': gain(ks[15], (L, SSD_HEADS)),
        'ssd_norm_w': gain(ks[17], (L, SSD_D_INNER)),
        'w_out': nrm(ks[18], (L, D_MIX, D_MODEL), D_MIX ** -0.5),
        'norm2_w': gain(ks[19], (L, D_MODEL)),
        'router_w_group': nrm(ks[20], (L, D_MODEL, MOE_GROUPS), D_MODEL ** -0.5),
        'router_b_group': nrm(ks[21], (L, MOE_GROUPS), 0.01),
        'router_w_expert': nrm(ks[22], (L, D_MODEL, N_EXPERTS), D_MODEL ** -0.5),
        'router_b_expert': nrm(ks[23], (L, N_EXPERTS), 0.01),
        'exp_w_gate': nrm(ks[24], (L, N_EXPERTS, D_MODEL, D_EXPERT), D_MODEL ** -0.5),
        'exp_w_up': nrm(ks[25], (L, N_EXPERTS, D_MODEL, D_EXPERT), D_MODEL ** -0.5),
        'exp_w_down': nrm(ks[26], (L, N_EXPERTS, D_EXPERT, D_MODEL), D_EXPERT ** -0.5),
        'final_norm_w': gain(ks[27], (D_MODEL,)),
    }

def reference(x, c, positions, w_ada, b_ada, norm1_w, w_in, mla_q_norm_w, mla_w_uq, mla_kv_norm_w, mla_w_ukv,
              diff_lambda, diff_subln_w, ssd_conv_w, ssd_conv_b, ssd_dt_bias, ssd_a_log, ssd_d, ssd_norm_w,
              w_out, norm2_w, router_w_group, router_b_group, router_w_expert, router_b_expert,
              exp_w_gate, exp_w_up, exp_w_down, final_norm_w):
    cond = jax.nn.silu(c)
    for l in range(DEPTH):
        mod = cond @ w_ada[l] + b_ada[l]
        sh1, sc1, g1, sh2, sc2, g2 = jnp.split(mod, 6, axis=-1)
        h = modulate(rmsnorm(x, norm1_w[l]), sh1, sc1)
        y = hybrid_mixer(h, positions, l, w_in[l], mla_q_norm_w[l], mla_w_uq[l], mla_kv_norm_w[l], mla_w_ukv[l],
                         diff_lambda[l], diff_subln_w[l], ssd_conv_w[l], ssd_conv_b[l], ssd_dt_bias[l],
                         ssd_a_log[l], ssd_d[l], ssd_norm_w[l], w_out[l])
        x = x + g1[:, None, :] * y
        h = modulate(rmsnorm(x, norm2_w[l]), sh2, sc2)
        y = hier_moe(h, router_w_group[l], router_b_group[l], router_w_expert[l], router_b_expert[l],
                     exp_w_gate[l], exp_w_up[l], exp_w_down[l])
        x = x + g2[:, None, :] * y
    return rmsnorm(x, final_norm_w)


_drawn_inputs = setup_inputs


def setup_inputs(seed=0):
    import zlib

    import numpy as np

    out = dict(_drawn_inputs(seed))
    spreads = {}
    factors = {'mla_q_norm_w': 5.082, 'router_b_group': 4.014}
    for name, (base, spread) in spreads.items():
        noise = np.random.default_rng([zlib.crc32(name.encode()), seed]).standard_normal(out[name].shape)
        drawn = base * np.exp(spread * noise) if base else spread * noise
        out[name] = __import__('jax').numpy.asarray(drawn.astype(out[name].dtype))
    for name, factor in factors.items():
        out[name] = (out[name] * factor).astype(out[name].dtype)
    return out
```

```python
import math
from contextlib import ExitStack

import numpy as np
import concourse.bass as bass
from concourse import mybir

F32 = mybir.dt.float32
BF16 = mybir.dt.bfloat16
I32 = mybir.dt.int32
U32 = mybir.dt.uint32
ALU = mybir.AluOpType
ACT = mybir.ActivationFunctionType
AX = mybir.AxisListType.X

P = 128
T, D, L = 512, 1024, 2
TT, KT = T // P, D // P
NH = 4
MQ, MKV, DN, DR, DV = 256, 128, 128, 64, 128
DQK = 64
SH, SP_, SG, SN_, SC = 16, 64, 4, 128, 4
DI = SH * SP_
NG, NE_G = 4, 8
NE = NG * NE_G
FE = 512
O_CQ, O_CKV, O_KPE, O_DQ, O_DK, O_DV, O_Z, O_XBC, O_DT = 0, 256, 384, 448, 960, 1472, 1984, 3008, 5056
N_IN = 5072
EPS, SUBEPS = 1e-6, 1e-5
NEG = -1.0e30
MLA_SCALE = (DN + DR) ** -0.5
DIFF_SCALE = DQK ** -0.5
SLOPES = [2.0 ** (-8.0 / NH * (h + 1)) for h in range(NH)]
NB_MAX = 42
PAIRS_MAX = 20
CH = 512
CHE = KT * CH

C_ID, C_U, C_SU, C_ONE, C_CM = 0, 128, 256, 384, 512
C_D4, C_D32, C_E32, C_K8, C_INV, C_PH, C_HALF = 1024, 1028, 1060, 1092, 1100, 1101, 1102
C_N = 1104 + 2
B_DTB, B_ALOG, B_D, B_RB, B_LAM, B_LI = 0, 16, 32, 48, 84, 340
B_N = 342
R_CW, R_CB, R_QN, R_KN, R_SUB, R_N = 0, 64, 80, 82, 83, 84


def shape_constants():
    c = np.zeros((P, C_N), np.float32)
    i = np.arange(P)
    c[:, C_ID:C_ID + P] = np.eye(P)
    c[:, C_U:C_U + P] = i[:, None] <= i[None, :]
    c[:, C_SU:C_SU + P] = i[:, None] < i[None, :]
    c[:, C_ONE:C_ONE + P] = 1.0
    c[:, C_CM + 384:C_CM + 512] = np.where(i[:, None] >= i[None, :], 0.0, NEG)
    c[:, C_D4:C_D4 + 4] = 4.0 - np.arange(4)
    c[:, C_D32:C_D32 + 32] = 32.0 - np.arange(32)
    c[:, C_E32:C_E32 + 32] = np.arange(32)
    c[:, C_K8:C_K8 + 8] = np.arange(8)
    inv = (1.0 / (np.float32(10000.0) ** (np.arange(0, DR, 2, dtype=np.float32) / np.float32(DR)))).astype(np.float32)
    c[:, C_INV] = np.tile(inv, 4)
    c[0:64, C_PH], c[64:96, C_PH], c[96:128, C_PH] = 0.25, 0.5, 0.0
    c[:, C_HALF] = -0.5
    pay = np.zeros((P, TT, 2, 4), np.int32)
    tok = np.arange(TT)[None, :] * P + i[:, None]
    for s in range(2):
        pay[:, :, s, 0] = tok
        pay[:, :, s, 1] = 2 * tok + s
    table = np.zeros((P, NB_MAX, 4), np.int32)
    table[:, :, 0:2] = 1 << 20
    lam = np.array([[0.8 - 0.6 * math.exp(-0.3 * l), 1.0 - (0.8 - 0.6 * math.exp(-0.3 * l))] for l in range(L)], np.float32)
    eids = np.tile(np.arange(48, dtype=np.int32)[None, :] % 32, (1, 1))
    return {"k_const": c, "k_pay": pay.reshape(P, -1), "k_table": table.reshape(P, -1), "k_lam": lam, "k_eid": eids}


def numbered(names):
    return {n: k for k, n in enumerate(names)}


ACC = numbered(
    [("A", j) for j in range(4)] + [("X", m) for m in range(16)] + [("Z", m) for m in range(8)] + ["DT", "AC"]
    + [("R", c, g) for c in range(TT) for g in range(SG)]
    + [(n, m) for n in ("DQ", "DK", "DV") for m in range(4)] + [("DS", h) for h in range(NH)]
    + [("C", m) for m in range(4)] + ["SQ", "SK"]
    + [("QN", h) for h in range(NH)] + [("QP", h) for h in range(NH)] + [("KN", h) for h in range(NH)]
    + [("V", t) for t in range(TT)] + [("A", j) for j in range(4, 12)])
TRN = numbered(["P"] + [("H", t, q) for t in range(TT) for q in range(2)] + [("T", m) for m in range(12)] + ["AT"]
               + [("Y", c, q) for c in range(TT) for q in range(2)])
CHUNKS = [("A", j) for j in range(4)] + [("I", j) for j in range(10)] + ["U"] + [("A", j) for j in range(4, 12)] \
    + [("O", j) for j in range(4)]
CHN = numbered(CHUNKS)
NCH = len(CHUNKS)
CHUNK_DMAS = {("I", 9): 3, "U": 7}
IN_COLS = [O_XBC, O_XBC + 512, O_XBC + 1024, O_XBC + 1536, O_Z, O_Z + 512, O_DQ, O_DK, O_DV, O_CQ]


def slot_count(n):
    return sum(16 * CHUNK_DMAS.get(CHUNKS[m], 1) for m in range(n % 2, n + 1, 2))


SLOT_BASE = [slot_count(NCH - 1 if (NCH - 1) % 2 == s else NCH - 2) for s in range(2)] + [0] * 4


def hybrid_kernel(nc, x, c, positions, w_ada, b_ada, norm1_w, w_in, mla_q_norm_w, mla_w_uq, mla_kv_norm_w, mla_w_ukv,
                  diff_lambda, diff_subln_w, ssd_conv_w, ssd_conv_b, ssd_dt_bias, ssd_a_log, ssd_d, ssd_norm_w,
                  w_out, norm2_w, router_w_group, router_b_group, router_w_expert, router_b_expert,
                  exp_w_gate, exp_w_up, exp_w_down, final_norm_w,
                  k_const, k_pay, k_table, k_lam, k_eid, out, h2_rows, expert_rows, slot_table):
    with ExitStack() as ctx:
        def sb(name, shape, dt=F32):
            return ctx.enter_context(nc.sbuf_tensor(name, shape, dt))

        def sem(name):
            s = ctx.enter_context(nc.semaphore(name))
            layer_sems.append(s)
            return s

        def kept_sem(name):
            return ctx.enter_context(nc.semaphore(name))

        layer_sems = []

        RING = sb("ring", [P, 2, CHE])
        OV = sb("ov", [P, 4 * CHE])
        X = sb("x_sb", [P, TT, D])
        HT = sb("ht", [P, KT, T])
        MOD = sb("mod", [P, 6, D])
        YA = sb("ya", [P, 2, NH, T])
        F = sb("f_area", [P, 6144])
        TRIG = sb("trig", [P, T])
        CON = sb("con", [P, C_N])
        IDB = sb("ident_bf", [P, P], BF16)
        CMB = sb("causal_bf", [P, P], BF16)
        BC = sb("bc", [P, B_N])
        COLS = sb("cols", [P, R_N])
        COND = sb("cond", [P, KT])
        SM = sb("small", [P, 832])
        WDT = sb("w_dt", [P, KT, SH])
        WR = sb("w_router", [P, KT, NG + NE])
        PAY = sb("pay", [P, TT, 2, 4], I32)
        TBL = sb("tbl", [P, NB_MAX, 4], I32)
        EID = sb("eid", [1, 48], I32)
        ROWI = sb("row_idx", [P, 8], U32)
        GIDX = [sb(f"gidx{s}", [P, 1], U32) for s in range(2)]
        SIDX = [sb(f"sidx{s}", [P, 4], U32) for s in range(2)]
        SLOT = [RING[:, 0, :], RING[:, 1, :]] + [OV[:, j * CHE:(j + 1) * CHE] for j in range(4)]

        def ov(at, *shape):
            n = int(np.prod(shape))
            v = OV[:, at:at + n]
            return v if len(shape) == 1 else v.rearrange("p (a b) -> p a b", a=shape[0])

        def fa(at, *shape):
            n = int(np.prod(shape))
            v = F[:, at:at + n]
            return v if len(shape) == 1 else v.rearrange("p (a b) -> p a b", a=shape[0])

        XS, Z, BTOK, BT, CT = ov(0, TT, DI), ov(4096, TT, DI), ov(8192, TT, T), ov(10240, SG, T), ov(12288, SG, T)
        CV = [ov(14336, T), ov(14848, T)]
        SX = [ov(15360, T), ov(15872, T)]
        ST, XW, XD = fa(0, DI), fa(1024, DI), fa(2048, DI)
        MT = [fa(3072, 4, P), fa(3584, 4, P)]
        DQT, DKT = fa(4096, NH, T), ov(14336, NH, T)
        DVT = YA[:, 0]
        CQT, CKVT, KPE, QN, QP, KN, VT = ov(0, 2, T), ov(1024, T), ov(1536, T), ov(2048, NH, T), ov(4096, NH, T), \
            ov(6144, NH, T), ov(8192, TT, T)
        PB = [ov(10240 + 512 * j, T) for j in range(4)]
        PT = ov(12288, TT, T)
        YT1, YT2, JSS = fa(4096, 512), fa(4608, 512), fa(5120, 256)
        ROT = fa(3072, T)
        DIST = fa(0, TT, T)
        SQB, RSB = fa(2048, T), fa(2560, T)
        POSR = ov(10240, T)
        NW1, HR = fa(0, D), [fa(1024, D), fa(2048, D)]
        JUNK1 = fa(3072, D)
        H2T, H2R = fa(0, KT, T), [fa(4096, D), fa(5120, D)]
        JUNK2 = MOD[:, 0]
        NW2, SNW = MOD[:, 0], MOD[:, 1]
        yaf = YA[:, :, :, :].rearrange("p a h t -> p (a h t)")
        htf = HT[:, :, :].rearrange("p k t -> p (k t)")
        XG = [yaf[:, 0:1024], yaf[:, 1024:2048]]
        XGT = [yaf[:, 2048 + 1024 * s:3072 + 1024 * s].rearrange("p (k j) -> p k j", k=KT) for s in range(2)]
        YB = [htf[:, 0:1024], htf[:, 1024:2048]]
        HHT = [htf[:, a:a + 512].rearrange("p (k j) -> p k j", k=4) for a in (2048, 3584)]
        GS, HH = htf[:, 2560:3072], htf[:, 3072:3584]
        CB = [yaf[:, 0:2048], yaf[:, 2048:4096], htf[:, 0:2048], htf[:, 2048:4096]]

        ID, UU, SU, ONE = (CON[:, a:a + P] for a in (C_ID, C_U, C_SU, C_ONE))

        def sm(at, *shape):
            n = int(np.prod(shape))
            v = SM[:, at:at + n]
            if len(shape) == 2:
                v = v.rearrange("p (a b) -> p a b", a=shape[0])
            return v
        SS, MS, RS = sm(0, TT), sm(4, TT), sm(8, TT)
        DTT, ADT, ACS, NACS, EACS, DEND, ETOT, STMP = (sm(16 + 64 * k, TT, SH) for k in range(8))
        ANEG = sm(528, SH)
        MX, NB_, SE, RR = sm(544, 4), sm(548, 4), sm(552, 4), sm(556, 4)
        LAM, LT, SUBW = sm(560, 1), sm(561, 2), sm(563, 1)
        SSG, MSG, RSG = (sm(768 + 16 * k, TT, SG) for k in range(3))
        POSQ = sm(816, TT)
        ACST = F[0:TT * SH, 5376:5504]
        LPR = F[:, 5120:5248]
        ROWS = F[0:R_N, 5504:5632]
        CROW = F[0:KT, 4096:4224]
        RM, RV, RP_, RW, R1, R2, R3, R4 = (sm(576 + 4 * k, TT) for k in range(8))
        GL, GE, PEN = sm(608, TT, NG), sm(624, TT, NG), sm(640, TT, NG)
        EL, LM, OH1, OH2, MM, POS, BLK, TMPE, ROWF = (YA[:, 1, k // 4, 128 * (k % 4):128 * (k % 4) + 128]
                                                      .rearrange("p (t e) -> p t e", t=TT) for k in range(9))
        OVS, OVE = (YA[:, 1, 3, 32 * k:32 * k + 32] for k in range(2))
        OVR = YA[0:32, 1, 3, 128:256]
        OVT = YA[0:32, 1, 3, 256:260]
        NPF = YA[0:1, 1, 3, 264:280]
        KCMP = YA[0:1, 1, 2, 256:512].rearrange("p (k e) -> p k e", k=8)

        PS = [ctx.enter_context(nc.psum_tensor(f"bank{b}", [P, 512], F32)) for b in range(8)]

        s_load = [sem(f"s_load{j}") for j in range(6)]
        s_par = sem("s_par")
        s_bada = sem("s_bada")
        s_late = sem("s_late")
        s_n1done = sem("s_n1done")
        s_tblini = sem("s_tblini")
        s_acc = sem("s_acc")
        s_accf = [sem("s_accf0"), sem("s_accf1")]
        s_tr = sem("s_tr")
        s_trf = [sem("s_trf0"), sem("s_trf1")]
        s_dch = sem("s_dch")
        s_ach = sem("s_ach")
        s_pch = sem("s_pch")
        s_ss1 = sem("s_ss1")
        s_ms = sem("s_ms")
        s_rs = sem("s_rs")
        s_hr = sem("s_hr")
        s_conv = sem("s_conv")
        s_sx = sem("s_sx")
        s_dt1 = sem("s_dt1")
        s_dt2 = sem("s_dt2")
        s_lam = sem("s_lam")
        s_adt = sem("s_adt")
        s_acs = sem("s_acs")
        s_dec = sem("s_dec")
        s_xw = sem("s_xw")
        s_cb = sem("s_cb")
        s_mx = sem("s_mx")
        s_mt = sem("s_mt")
        s_yd = sem("s_yd")
        s_st = sem("s_st")
        s_ydf = sem("s_ydf")
        s_ste = sem("s_ste")
        s_yn = sem("s_yn")
        s_ssg = sem("s_ssg")
        s_msg = sem("s_msg")
        s_rsg = sem("s_rsg")
        s_ynn = sem("s_ynn")
        s_pos = sem("s_pos")
        s_sc = sem("s_sc")
        s_scf = sem("s_scf")
        s_nb = sem("s_nb")
        s_ex = sem("s_ex")
        s_at = sem("s_at")
        s_tp = sem("s_tp")
        s_pt = sem("s_pt")
        s_pv = sem("s_pv")
        s_sq = sem("s_sq")
        s_rst = sem("s_rst")
        s_ya = sem("s_ya")
        s_csq = sem("s_csq")
        s_crs = sem("s_crs")
        s_cn = sem("s_cn")
        s_kpe = sem("s_kpe")
        s_qpr = sem("s_qpr")
        s_oc = sem("s_oc")
        s_o = sem("s_o")
        s_xr = sem("s_xr")
        s_ss2 = sem("s_ss2")
        s_h2 = sem("s_h2")
        s_h2st = sem("s_h2st")
        s_nt = sem("s_nt")
        s_ntf = sem("s_ntf")
        s_lg = sem("s_lg")
        s_ge = sem("s_ge")
        s_gf = sem("s_gf")
        s_oh = sem("s_oh")
        s_pp = sem("s_pp")
        s_ovt = sem("s_ovt")
        s_ov2 = sem("s_ov2")
        s_eid = sem("s_eid")
        s_row = sem("s_row")
        s_tbl = sem("s_tbl")
        s_xt = sem("s_xt")
        s_xte = [sem("s_xte_a"), sem("s_xte_d")]
        s_g = sem("s_g")
        s_u = sem("s_u")
        s_gs = sem("s_gs")
        s_hh = sem("s_hh")
        s_htp = sem("s_htp")
        s_hte = sem("s_hte")
        s_y = [sem("s_y0"), sem("s_y1")]
        s_ye = [sem("s_ye_d"), sem("s_ye_a")]
        s_slot = [sem("s_slot0"), sem("s_slot1")]
        s_all = sem("s_all")
        s_cmb = [sem(f"s_cmb{t}") for t in range(TT)]
        s_gd = [kept_sem("s_gd0"), kept_sem("s_gd1")]
        s_sd = [kept_sem("s_sd0"), kept_sem("s_sd1")]
        s_disp = [kept_sem(f"s_disp{k}") for k in range(8)]
        s_end = kept_sem("s_end")
        s_clr = kept_sem("s_clr")
        s_seq = kept_sem("s_seq")
        s_con = kept_sem("s_con")
        s_x0 = kept_sem("s_x0")
        s_pro = kept_sem("s_pro")
        s_proa = kept_sem("s_proa")
        s_prod = kept_sem("s_prod")
        s_prot = kept_sem("s_prot")
        s_prov = kept_sem("s_prov")
        s_fss = kept_sem("s_fss")
        s_fin = kept_sem("s_fin")
        s_finr = kept_sem("s_finr")
        s_fout = kept_sem("s_fout")
        s_fw = kept_sem("s_fw")
        s_fst = kept_sem("s_fst")
        s_tick = kept_sem("s_tick")

        block = ctx.enter_context(nc.Block())

        N_PAR = 16 * 16

        def acc_bank(name):
            n = ACC[name]
            return PS[n % 2], s_accf[n % 2], n // 2 + 1

        def tr_bank(name):
            n = TRN[name]
            return PS[2 + n % 2], s_trf[n % 2], n // 2 + 1

        def evacuated(eng, name):
            _, free, k = acc_bank(name)
            eng.wait_ge(free, k)

        def turned_out(eng, name):
            _, free, k = tr_bank(name)
            eng.wait_ge(free, k)

        def flat(v):
            return v.rearrange("p a b -> p (a b)")

        def last_group(n):
            name = CHUNKS[n]
            if name == "U":
                return s_acc, ACC[("V", 3)] + 1
            if name[0] == "A":
                return s_acc, ACC[name] + 1
            if name[0] == "O":
                return (s_oc, name[1] + 1) if name[1] < 3 else (s_o, TT)
            j = name[1]
            tile = (("X", 4 * j + 3) if j < 4 else ("Z", 4 * j - 13) if j < 6 else
                    (("DQ", "DK", "DV")[j - 6], 3) if j < 9 else ("C", 3))
            return s_acc, ACC[tile] + 1

        def pairs(eng):
            eng.wait_ge(s_eid, 1)
            return eng.value_load(EID[0:1, 40:41], min_val=16, max_val=PAIRS_MAX)

        @block.sync
        def _(sp):
            sp.dma_start(CON[:, :], k_const).then_inc(s_con, 16)
            sp.dma_start(CROW, c.rearrange("a (k p) -> (a k) p", p=P)).then_inc(s_con, 16)
            sp.dma_start(EID[:, :], k_eid).then_inc(s_con, 16)
            sp.dma_start(PAY[:, :, :, :].rearrange("p t s w -> p (t s w)"), k_pay).then_inc(s_con, 16)
            sp.dma_start(SM[:, 0:512].bitcast(I32), positions.partition_broadcast(P)).then_inc(s_con, 16)
            sp.dma_start(X[:, :, :], x.rearrange("a (t p) d -> p (a t) d", p=P)).then_inc(s_x0, 16)
            sp.wait_ge(s_prod, 1)

            with sp.Fori(0, L) as l:
                def rows(w, o, n):
                    return w[bass.ds(l, 1), :, o:o + n].rearrange("a (k p) n -> p (a k) n", p=P)

                def load_chunk(n):
                    name, dst, landed = CHUNKS[n], SLOT[n % 2], s_load[n % 2]
                    if n >= 2:
                        sp.wait_ge(*last_group(n - 2))
                    tiles = dst.rearrange("p (k n) -> p k n", k=KT)
                    if name[0] == "A":
                        sp.dma_start(tiles, rows(w_ada, name[1] * CH, CH)).then_inc(landed, 16)
                    elif name == ("I", 9):
                        for a, b, o in ((0, 448, 0), (448, 480, 416), (480, 512, 384)):
                            sp.dma_start(tiles[:, :, a:b], rows(w_in, o, b - a)).then_inc(landed, 16)
                    elif name[0] == "I":
                        sp.dma_start(tiles, rows(w_in, IN_COLS[name[1]], CH)).then_inc(landed, 16)
                    elif name == "U":
                        uq = dst[:, 0:2048].rearrange("p (k h n) -> p k h n", k=2, h=NH)
                        for k in range(2):
                            src = mla_w_uq[bass.ds(l, 1), k * P:(k + 1) * P, :].rearrange("a p (h n) -> (a p) h n", h=NH)
                            for a, b, o in ((0, 192, 0), (192, 224, 160), (224, 256, 128)):
                                sp.dma_start(uq[:, k, :, a:b], src[:, :, o:o + b - a]).then_inc(landed, 16)
                        sp.dma_start(dst[:, 2048:3072],
                                     mla_w_ukv[bass.ds(l, 1)].rearrange("a p n -> (a p) n")).then_inc(landed, 16)
                    else:
                        j = name[1]
                        sp.dma_start(dst.rearrange("p (f n) -> p f n", f=4),
                                     w_out[bass.ds(l, 1), j * 512:(j + 1) * 512, :]
                                     .rearrange("a (f p) n -> p (a f) n", p=P)).then_inc(landed, 16)

                small = [(NW1, norm1_w[bass.ds(l, 1)].partition_broadcast(P)),
                         (ROWS[R_CW:R_CW + 64, :], ssd_conv_w[bass.ds(l, 1)].rearrange("a k (m p) -> (a k m) p", p=P)),
                         (ROWS[R_CB:R_CB + 16, :], ssd_conv_b[bass.ds(l, 1)].rearrange("a (m p) -> (a m) p", p=P)),
                         (ROWS[R_QN:R_QN + 2, :], mla_q_norm_w[bass.ds(l, 1)].rearrange("a (m p) -> (a m) p", p=P)),
                         (ROWS[R_KN:R_KN + 1, :], mla_kv_norm_w[bass.ds(l, 1)]),
                         (ROWS[R_SUB:R_SUB + 1, :], diff_subln_w[bass.ds(l, 1)]),
                         (BC[:, B_LAM:B_LAM + 256], diff_lambda[bass.ds(l, 1)].rearrange("a k d -> a (k d)").partition_broadcast(P)),
                         (WDT[:, :, :], rows(w_in, O_DT, SH)),
                         (WR[:, :, 0:NG], rows(router_w_group, 0, NG)),
                         (WR[:, :, NG:], rows(router_w_expert, 0, NE))]
                for at, n, w in ((B_DTB, SH, ssd_dt_bias), (B_ALOG, SH, ssd_a_log), (B_D, SH, ssd_d),
                                 (B_RB, NG, router_b_group), (B_RB + NG, NE, router_b_expert), (B_LI, 2, k_lam)):
                    small.append((BC[:, at:at + n], w[bass.ds(l, 1)].partition_broadcast(P)))
                assert 16 * len(small) == N_PAR
                for dst, src in small:
                    sp.dma_start(dst, src).then_inc(s_par, 16)
                sp.dma_start(MOD[:, :, :].rearrange("p a n -> p (a n)"), b_ada[bass.ds(l, 1)].partition_broadcast(P)).then_inc(s_bada, 16)
                for n in range(4):
                    load_chunk(n)
                sp.dma_start(TBL[:, :, :].rearrange("p k w -> p (k w)"), k_table).then_inc(s_tblini, 16)
                sp.wait_ge(s_tblini, 16)
                sp.dma_start(slot_table.rearrange("(p k) w -> p (k w)", p=P),
                             TBL[:, :, :].rearrange("p k w -> p (k w)")).then_inc(s_tblini, 16)
                for n in range(4, 8):
                    load_chunk(n)
                sp.wait_ge(s_n1done, 1)
                sp.dma_start(NW2, norm2_w[bass.ds(l, 1)].partition_broadcast(P)).then_inc(s_late, 16)
                sp.dma_start(SNW, ssd_norm_w[bass.ds(l, 1)].partition_broadcast(P)).then_inc(s_late, 16)
                for n in range(8, NCH):
                    load_chunk(n)
                    if n == CHN[("I", 7)]:
                        sp.wait_ge(s_st, 8)
                        sp.dma_start(POSR.bitcast(I32), positions.partition_broadcast(P)).then_inc(s_pos, 16)

                def load_expert(m, e):
                    slot, kind = (m + 2) % 6, (0, 1, 0, 1, 2, 2)[m]
                    w = (exp_w_gate, exp_w_up, exp_w_down)[kind][bass.ds(l, 1), bass.ds(e, 1)]
                    sp.dma_start(SLOT[slot].rearrange("p (k n) -> p k n", k=4 if kind == 2 else KT),
                                 w.rearrange("a b (k p) n -> p (a b k) n", p=P)).then_inc(s_load[slot], 16)

                sp.wait_ge(s_ya, 2 * NH)
                for m in range(6):
                    if m >= 4:
                        sp.wait_ge(*last_group(NCH - 1 if m == 4 else NCH - 2))
                    load_expert(m, (0, 0, 1, 1, 0, 1)[m])
                for t in range(TT):
                    sp.wait_ge(s_h2, t + 1)
                    sp.dma_start(h2_rows[t * P:(t + 1) * P, :], H2R[t % 2]).then_inc(s_h2st, 16)
                    sp.wait_ge(s_h2st, 16 * (t + 1))
                for q in s_disp:
                    sp.wait_ge(q, 16)
                sp.dma_start(TBL[:, :, :].rearrange("p k w -> p (k w)"),
                             slot_table.rearrange("(p k) w -> p (k w)", p=P)).then_inc(s_tbl, 16)
                n_pairs = pairs(sp)
                more = sp.value_load(EID[0:1, 41:42], min_val=15, max_val=PAIRS_MAX - 1)
                with sp.Fori(0, more) as i:
                    e = [sp.value_load(EID[0:1, bass.ds(i * 2 + (2 + s), 1)], min_val=0, max_val=NE - 1) for s in range(2)]
                    for m in range(6):
                        s = (0, 0, 1, 1, 0, 1)[m]
                        sp.wait_ge((s_g, s_u, s_g, s_u, s_y[1], s_y[1])[m], i * 2 + (s + 1))
                        load_expert(m, e[s])
                sp.wait_ge(s_all, 1)
                for q in s_xte:
                    sp.wait_ge(q, n_pairs * 2 + 1)
                    sp.sem_inc(s_tick, 1)
                for t in range(TT):
                    sp.dma_start(CB[t], expert_rows[t * 2 * P:(t + 1) * 2 * P, :].rearrange("(p s) d -> p (s d)", s=2)).then_inc(s_cmb[t], 16)
                sp.sem_inc(s_end, 1)
                sp.wait_ge(s_end, l * 5 + 5)
                sp.sem_inc(s_seq, 1)
                for q in layer_sems:
                    sp.sem_clear(q)
                sp.sem_inc(s_clr, 1)
            sp.dma_start(MOD[:, 0], final_norm_w.rearrange("(a d) -> a d", a=1).partition_broadcast(P)).then_inc(s_fw, 16)
            for t in range(TT):
                sp.wait_ge(s_fout, t + 1)
                sp.dma_start(out[0, t * P:(t + 1) * P, :], X[:, t, :]).then_inc(s_fst, 16)
            sp.wait_ge(s_fst, 16 * TT)

        @block.gpsimd
        def _(pool):
            pool.wait_ge(s_con, 80)
            half = CON[:, C_HALF:C_HALF + 1]

            def rstd(dst, src, n, done):
                pool.tensor_tensor(dst, src, half.broadcast_to([P, n]), ALU.pow).then_inc(done, 1)

            with pool.Fori(0, L) as l:
                pool.wait_ge(s_ms, 1)
                rstd(RS, MS, TT, s_rs)
                for cc in range(TT):
                    pool.wait_ge(s_msg, cc + 1)
                    rstd(RSG[:, cc, :], MSG[:, cc, :], SG, s_rsg)
                for t in range(TT):
                    pool.wait_ge(s_ms, t + 2)
                    rstd(RS[:, t:t + 1], MS[:, t:t + 1], 1, s_rs)
                pool.wait_ge(s_tblini, 32)
                pool.wait_ge(s_row, 1)
                for t in range(TT):
                    for s in range(2):
                        k = 2 * t + s
                        pool.indirect_dma_start(slot_table, bass.IndirectOffsetOnAxis(ap=ROWI[:, k:k + 1], axis=0), PAY[:, t, s, :], None,
                                                bounds_check=P * NB_MAX - 1, oob_is_err=False).then_inc(s_disp[k], 16)
                for s in range(2):
                    pool.memset(XG[s], 0.0).then_inc(s_pch, 1)
                pool.wait_ge(s_pch, 2)
                pool.wait_ge(s_tbl, 16)
                pool.wait_ge(s_h2st, 16 * TT)

                def gather(s):
                    pool.indirect_dma_start(XG[s], None, h2_rows, bass.IndirectOffsetOnAxis(ap=GIDX[s][:, 0:1], axis=0),
                                            bounds_check=T - 1, oob_is_err=False).then_inc(s_gd[s], 16)

                for s in range(2):
                    pool.tensor_copy(GIDX[s][:, :], TBL[:, s, 0:1].bitcast(U32)).then_inc(s_pch, 1)
                    pool.tensor_copy(SIDX[s][:, 0:3], TBL[:, s, 0:3].bitcast(U32)).then_inc(s_slot[s], 1)
                for s in range(2):
                    pool.wait_ge(s_pch, 3 + s)
                    gather(s)
                n_pairs = pairs(pool)

                def after(q, value):
                    pool.wait_ge(q, value)
                    pool.sem_inc(s_tick, 1)

                with pool.Fori(0, n_pairs) as i:
                    for s in range(2):
                        after(s_xt, i * 2 + (s + 1))
                        pool.tensor_copy(GIDX[s][:, :], TBL[:, bass.ds(i * 2 + (2 + s), 1), 0:1]
                                         .rearrange("p a b -> p (a b)").bitcast(U32)).then_inc(s_pch, 1)
                        after(s_pch, i * 2 + (5 + s))
                        gather(s)
                        after(s_ye[0], i * 2 + (s + 2))
                        after(s_ye[1], i * 2 + (s + 2))
                        pool.indirect_dma_start(expert_rows, bass.IndirectOffsetOnAxis(ap=SIDX[s][:, 1:2], axis=0), YB[s], None,
                                                bounds_check=2 * T - 1, oob_is_err=False).then_inc(s_sd[s], 16)
                        after(s_sd[s], i * 16 + 16)
                        pool.tensor_copy(SIDX[s][:, 0:3], TBL[:, bass.ds(i * 2 + (2 + s), 1), 0:3]
                                         .rearrange("p a b -> p (a b)").bitcast(U32)).then_inc(s_slot[s], 1)
                for s in range(2):
                    after(s_gd[s], n_pairs * 16 + 16)
                pool.sem_inc(s_all, 1)
                for q in (*s_gd, *s_sd, *s_disp):
                    pool.dma_reset(range(q.num, q.num + 1))
                    pool.sem_clear(q)
                pool.sem_inc(s_end, 1)
                after(s_clr, l + 1)
            pool.wait_ge(s_fin, 1)
            rstd(RS, MS, TT, s_finr)

        @block.scalar
        def _(act):
            act.wait_ge(s_pro, 1)
            act.activation(COND[:, :], PS[2][:, 0:KT], ACT.Silu).then_inc(s_proa, 1)
            act.wait_ge(s_prod, 1)
            act.activation(TRIG[:, :], TRIG[:, :], ACT.Sin).then_inc(s_proa, 1)

            with act.Fori(0, L) as l:
                chain = [0]

                def link(ins):
                    chain[0] += 1
                    ins.then_inc(s_ach, 1)
                    act.wait_ge(s_ach, chain[0])

                def acc_ready(name):
                    act.wait_ge(s_acc, ACC[name] + 1)
                    return acc_bank(name)

                def tr_ready(name):
                    act.wait_ge(s_tr, TRN[name] + 1)
                    return tr_bank(name)

                act.wait_ge(s_x0, 16)
                for t in range(TT):
                    link(act.activation(JUNK1, X[:, t, :], ACT.Square, accum_out=SS[:, t:t + 1]))
                act.sem_inc(s_ss1, 1)
                bank, free, _ = tr_ready("P")
                act.activation(COLS[:, :], bank[:, 0:R_N], ACT.Copy).then_inc(free, 1)
                for t in range(TT):
                    for q in range(2):
                        bank, free, _ = tr_ready(("H", t, q))
                        act.activation(HT[:, 4 * q:4 * q + 4, t * P:(t + 1) * P],
                                       bank[:, :].rearrange("p (k t) -> p k t", k=4), ACT.Copy).then_inc(free, 1)

                for m in range(16):
                    if 1 <= m <= 12:
                        bank, free, _ = tr_ready(("T", m - 1))
                        dst = XS[:, :, (m - 1) * P:m * P] if m <= 8 else BTOK[:, :, (m - 9) * P:(m - 8) * P]
                        act.activation(dst, bank[:, :].rearrange("p (t n) -> p t n", t=TT), ACT.Copy).then_inc(free, 1)
                    act.wait_ge(s_conv, m + 1)
                    dst = SX[m % 2] if m < 8 else (BT, CT)[m // 12][:, m % 4, :]
                    act.activation(dst, CV[m % 2], ACT.Silu).then_inc(s_sx, 1)
                for m in range(8):
                    bank, free, _ = acc_ready(("Z", m))
                    act.activation(Z[:, m % 4, (m // 4) * CH:(m // 4 + 1) * CH], bank[:, :], ACT.Silu).then_inc(free, 1)
                act.preload_act_table_set("natural_log_exp_and_others")
                act.wait_ge(s_dt1, 1)
                act.activation(ANEG, BC[:, B_ALOG:B_ALOG + SH], ACT.Exp)
                link(act.activation(flat(ACS), flat(DTT), ACT.Abs))
                link(act.activation(flat(NACS), flat(ACS), ACT.Exp, scale=-1.0))
                act.activation(flat(EACS), flat(NACS), ACT.Ln, bias=1.0).then_inc(s_dt2, 1)
                act.wait_ge(s_lam, 1)
                act.activation(LT, LT, ACT.Exp).then_inc(s_dt2, 1)
                act.wait_ge(s_acs, 1)
                act.activation(flat(EACS), flat(ACS), ACT.Exp)
                act.activation(flat(DEND), flat(STMP), ACT.Exp)
                act.activation(flat(ETOT), flat(ETOT), ACT.Exp).then_inc(s_dec, 1)
                bank, free, _ = tr_ready("AT")
                act.activation(ACST, bank[0:TT * SH, 0:P], ACT.Copy).then_inc(free, 1)

                def squares(cc, hf):
                    act.wait_ge(s_yn, 2 * cc + hf + 1)
                    for q in range(2):
                        g = 2 * hf + q
                        link(act.activation(JSS, Z[:, cc, 256 * g:256 * g + 256], ACT.Square, accum_out=SSG[:, cc, g:g + 1]))
                    act.sem_inc(s_ssg, 1)

                for cc in range(TT):
                    for g in range(SG):
                        n = 4 * cc + g
                        bank, free, k = acc_ready(("R", cc, g))
                        if n >= 2:
                            act.wait_ge(s_yd, n - 1)
                        for h in range(4):
                            ins = act.activation(MT[g % 2][:, h, :], bank[:, h * P:(h + 1) * P], ACT.Exp,
                                                 bias=NACS[:, cc, 4 * g + h:4 * g + h + 1])
                        ins.then_inc(free, 1)
                        act.wait_ge(free, k)
                        act.sem_inc(s_mx, 1)
                        if n >= 2 and g == 3:
                            squares(cc, 0)
                        if cc >= 1 and g == 1:
                            squares(cc - 1, 1)
                squares(TT - 1, 1)
                for name, dst in (("DQ", DQT), ("DK", DKT), ("DV", DVT)):
                    for m in range(4):
                        bank, free, _ = acc_ready((name, m))
                        act.activation(dst[:, m, :], bank[:, :], ACT.Copy).then_inc(free, 1)

                def exps(base, u, width, scale):
                    for m in range(width):
                        b, n = (width * u + m) % 4, (u % 4 + 1) * P
                        act.wait_ge(s_nb, base + width * u + m + 1)
                        link(act.activation(PB[b][:, 0:n], PB[b][:, 0:n], ACT.Exp, bias=NB_[:, b:b + 1], scale=scale,
                                            accum_out=SE[:, b:b + 1]))
                        act.sem_inc(s_ex, 1)

                def turned(k):
                    i = k % 4
                    act.wait_ge(s_tp, k + 1)
                    if i == 0 and k >= 4:
                        act.wait_ge(s_pv, k // 4)
                    act.activation(PT[:, 0:i + 1, i * P:(i + 1) * P],
                                   PS[6][:, 0:(i + 1) * P].rearrange("p (j q) -> p j q", j=i + 1), ACT.Copy).then_inc(s_pt, 1)

                def rms_rows(name, n, eps, done):
                    bank, free, k = acc_ready(name)
                    act.activation(RSB, bank[:, :], ACT.Ln, scale=1.0 / n, bias=eps).then_inc(free, 1)
                    act.wait_ge(free, k)
                    act.activation(RSB, RSB, ACT.Exp, scale=-0.5).then_inc(done, 1)

                for u in range(18):
                    if u < 16:
                        exps(0, u, 2, DIFF_SCALE)
                    if u >= 2:
                        turned(u - 2)
                        if u % 4 == 1:
                            h = (u - 2) // 4
                            act.wait_ge(s_pv, h + 1)
                            act.activation(SQB, PS[7][:, :], ACT.Square).then_inc(s_sq, 1)
                            if h >= 1:
                                act.wait_ge(s_ya, h)
                            rms_rows(("DS", h), DV, SUBEPS, s_rst)
                act.wait_ge(s_ya, NH)
                for m, dst in ((0, SQB), (1, PB[0])):
                    evacuated(act, ("C", m))
                    act.activation(dst, CQT[:, m, :], ACT.Square).then_inc(s_csq, 1)
                rms_rows("SQ", MQ, EPS, s_crs)
                evacuated(act, ("C", 2))
                act.activation(SQB, CKVT, ACT.Square).then_inc(s_csq, 1)
                act.wait_ge(s_cn, 1)
                rms_rows("SK", MKV, EPS, s_crs)
                for cc in range(TT):
                    for q in range(2):
                        bank, free, _ = tr_ready(("Y", cc, q))
                        act.activation(HT[:, 4 * q:4 * q + 4, cc * P:(cc + 1) * P],
                                       bank[:, :].rearrange("p (k t) -> p k t", k=4), ACT.Copy).then_inc(free, 1)
                for name, dst in (("QN", QN), ("KN", KN), ("V", VT)):
                    for m in range(4):
                        bank, free, _ = acc_ready((name, m))
                        act.activation(dst[:, m, :], bank[:, :], ACT.Copy).then_inc(free, 1)
                for u in range(18):
                    if u < 16:
                        exps(32, u, 1, MLA_SCALE)
                    if u >= 2:
                        turned(16 + u - 2)
                def feature_major2(t):
                    act.wait_ge(s_nt, t + 1)
                    for q in range(2):
                        ins = act.activation(H2T[:, 4 * q:4 * q + 4, t * P:(t + 1) * P],
                                             PS[2 * t + q][:, :].rearrange("p (k t) -> p k t", k=4), ACT.Copy)
                    ins.then_inc(s_ntf, 1)

                for t in range(TT):
                    act.wait_ge(s_xr, t + 1)
                    link(act.activation(JUNK2, X[:, t, :], ACT.Square, accum_out=SS[:, t:t + 1]))
                    act.sem_inc(s_ss2, 1)
                    if t >= 1:
                        feature_major2(t - 1)
                feature_major2(TT - 1)
                act.wait_ge(s_ge, 1)
                act.activation(flat(GE), flat(GE), ACT.Exp).then_inc(s_gf, 1)
                act.wait_ge(s_ge, 2)
                act.activation(RW, RW, ACT.Exp).then_inc(s_gf, 1)
                n_pairs = pairs(act)
                act.sem_inc(s_ye[1], 1)

                def rows_turned(s, count):
                    act.wait_ge(s_xt, count)
                    act.activation(XGT[s][:, 0:4, :], PS[0][:, :].rearrange("p (k j) -> p k j", k=4), ACT.Copy).then_inc(s_xte[0], 1)

                def hidden_turned(s, count):
                    act.wait_ge(s_htp, count)
                    act.activation(HHT[s][:, :, :], PS[4][:, :].rearrange("p (k j) -> p k j", k=4), ACT.Copy).then_inc(s_hte, 1)

                def gate(i, s):
                    act.wait_ge(s_g, i * 2 + (s + 1))
                    act.activation(GS, PS[2][:, :], ACT.Silu).then_inc(s_gs, 1)

                def output_half(i, s):
                    act.wait_ge(s_slot[s], i + 1)
                    act.wait_ge(s_y[1], i * 2 + (s + 1))
                    act.activation(YB[s][:, CH:D], PS[6][:, :], ACT.Copy).then_inc(s_ye[1], 1)

                rows_turned(0, 1)
                with act.Fori(0, n_pairs) as i:
                    gate(i, 0)
                    rows_turned(1, i * 2 + 2)
                    hidden_turned(0, i * 2 + 1)
                    gate(i, 1)
                    hidden_turned(1, i * 2 + 2)
                    output_half(i, 0)
                    rows_turned(0, i * 2 + 3)
                    output_half(i, 1)
                act.sem_inc(s_end, 1)
                act.wait_ge(s_clr, l + 1)
                act.sem_inc(s_seq, 1)
            act.wait_ge(s_fss, 1)
            for t in range(TT):
                if t:
                    act.wait_ge(s_prot, t)
                act.activation(F[:, 0:D], X[:, t, :], ACT.Square, accum_out=SS[:, t:t + 1]).then_inc(s_prot, 1)

        @block.vector
        def _(dve):
            own = [0]

            def olink(ins):
                own[0] += 1
                ins.then_inc(s_prov, 1)
                dve.wait_ge(s_prov, own[0])

            dve.wait_ge(s_con, 80)
            dve.tensor_copy(IDB[:, :], ID)
            dve.tensor_scalar(CMB[:, :], UU, -1.0, -NEG, ALU.add, ALU.mult)
            angle, turns, posf = F[:, 0:T], F[:, T:2 * T], F[:, 2 * T:3 * T]
            olink(dve.tensor_copy(posf, SM[:, 0:512].bitcast(I32)))
            for t in range(TT):
                dve.tensor_tensor(F[:, 3 * T + t * P:3 * T + (t + 1) * P], posf[:, t * P:(t + 1) * P], ID, ALU.mult)
            olink(dve.tensor_scalar(angle, posf, CON[:, C_INV:C_INV + 1], None, ALU.mult))
            dve.tensor_reduce(POSQ, F[:, 3 * T:4 * T].rearrange("p (t q) -> p t q", t=TT), AX, ALU.add)
            olink(dve.tensor_scalar(turns, angle, 1.0 / (2 * math.pi), CON[:, C_PH:C_PH + 1], ALU.mult, ALU.add))
            olink(dve.tensor_scalar(turns, turns, 12582912.0, None, ALU.add))
            olink(dve.tensor_scalar(turns, turns, -12582912.0, None, ALU.add))
            c1 = 6.28125
            c2 = float(np.float32(np.round((2 * math.pi - c1) * 2 ** 22) / 2 ** 22))
            c3 = 2 * math.pi - c1 - c2
            for part in (c1, c2, c3):
                olink(dve.scalar_tensor_tensor(angle, turns, -part, angle, ALU.mult, ALU.add))
            olink(dve.tensor_scalar(turns[:, 0:1], CON[:, C_PH:C_PH + 1], 2 * math.pi, None, ALU.mult))
            olink(dve.tensor_scalar(angle, angle, turns[:, 0:1], 3.1415925, ALU.add, ALU.min))
            olink(dve.tensor_scalar(TRIG[:, :], angle, -3.1415925, None, ALU.max))
            dve.sem_inc(s_prod, 1)

            with dve.Fori(0, L) as l:
                chain = [0]

                def link(ins):
                    chain[0] += 1
                    ins.then_inc(s_dch, 1)
                    dve.wait_ge(s_dch, chain[0])

                def signal(ins, q, n=1):
                    link(ins)
                    dve.sem_inc(q, n)

                def acc_ready(name):
                    dve.wait_ge(s_acc, ACC[name] + 1)
                    return acc_bank(name)

                dve.wait_ge(s_ss1, 1)
                signal(dve.tensor_scalar(MS, SS, 1.0 / D, EPS, ALU.mult, ALU.add), s_ms)
                dve.wait_ge(s_bada, 16)
                for j in range(4):
                    bank, free, _ = acc_ready(("A", j))
                    row = MOD[:, j // 2, (j % 2) * CH:(j % 2 + 1) * CH]
                    signal(dve.tensor_tensor(row, bank[:, :], row, ALU.add), free)
                dve.wait_ge(s_par, N_PAR)
                link(dve.scalar_tensor_tensor(MOD[:, 1], MOD[:, 1], 1.0, NW1, ALU.add, ALU.mult))
                dve.wait_ge(s_rs, 1)
                for t in range(TT):
                    if t >= 2:
                        dve.wait_ge(s_tr, TRN[("H", t - 2, 1)] + 1)
                    link(dve.scalar_tensor_tensor(HR[t % 2], X[:, t, :], RS[:, t:t + 1], MOD[:, 1], ALU.mult, ALU.mult))
                    signal(dve.tensor_tensor(HR[t % 2], HR[t % 2], MOD[:, 0], ALU.add), s_hr)
                dve.sem_inc(s_n1done, 1)
                lam = BC[:, B_LAM:B_LAM + 256]
                for k in range(2):
                    link(dve.tensor_tensor(LPR[:, 64 * k:64 * k + 64], lam[:, 128 * k:128 * k + 64], lam[:, 128 * k + 64:128 * k + 128], ALU.mult))
                signal(dve.tensor_reduce(LT, LPR.rearrange("p (k d) -> p k d", k=2), AX, ALU.add), s_lam)
                turned_out(dve, "P")
                for m in range(16):
                    bank, free, _ = acc_ready(("X", m))
                    if m >= 2:
                        dve.wait_ge(s_sx, m - 1)
                    w = lambda k: COLS[:, R_CW + 16 * k + m:R_CW + 16 * k + m + 1]
                    link(dve.tensor_scalar(CV[m % 2], bank[:, :], w(SC - 1), COLS[:, R_CB + m:R_CB + m + 1], ALU.mult, ALU.add))
                    for back in range(1, SC):
                        ins = dve.scalar_tensor_tensor(CV[m % 2][:, back:], bank[:, 0:T - back], w(SC - 1 - back), CV[m % 2][:, back:],
                                                       ALU.mult, ALU.add)
                        link(ins)
                    dve.sem_inc(free, 1)
                    dve.sem_inc(s_conv, 1)
                def per_chunk(v):
                    return v.rearrange("p (a h) -> p a h", a=1).broadcast_to([P, TT, SH])

                bank, free, _ = acc_ready("DT")
                signal(dve.tensor_tensor(DTT, bank[:, 0:TT * SH].rearrange("p (t h) -> p t h", t=TT), per_chunk(BC[:, B_DTB:B_DTB + SH]), ALU.add), free)
                dve.sem_inc(s_dt1, 1)
                dve.wait_ge(s_dt2, 1)
                link(dve.scalar_tensor_tensor(flat(DTT), flat(DTT), 0.0, flat(EACS), ALU.max, ALU.add))
                signal(dve.scalar_tensor_tensor(ADT, DTT, -1.0, per_chunk(ANEG), ALU.mult, ALU.mult), s_adt)
                dve.wait_ge(s_dt2, 2)
                link(dve.tensor_tensor(LAM, LT[:, 0:1], LT[:, 1:2], ALU.subtract))
                link(dve.tensor_tensor(LAM, LAM, BC[:, B_LI:B_LI + 1], ALU.add))
                link(dve.tensor_tensor(SUBW, COLS[:, R_SUB:R_SUB + 1], BC[:, B_LI + 1:B_LI + 2], ALU.mult))
                bank, free, _ = acc_ready("AC")
                cs, tot = bank[:, 0:TT * SH], bank[:, TT * SH:2 * TT * SH]
                link(dve.tensor_copy(flat(ACS), cs))
                dve.tensor_scalar(flat(NACS), cs, -1.0, None, ALU.mult)
                dve.tensor_tensor(flat(STMP), tot, flat(ACS), ALU.subtract)
                signal(dve.tensor_copy(flat(ETOT), tot), free)
                dve.sem_inc(s_acs, 1)
                dve.wait_ge(s_dec, 1)
                turned_out(dve, ("T", 10))
                turned_out(dve, ("T", 11))
                dve.wait_ge(s_late, 32)

                def heads(v, n=SH):
                    return v.rearrange("p (h d) -> p h d", h=n)

                def each(v, n):
                    return v.rearrange("p (h a) -> p h a", a=1).broadcast_to([P, n, SP_])

                def norm_chunk(cc):
                    dve.wait_ge(s_ssg, 2 * cc + 2)
                    signal(dve.tensor_scalar(MSG[:, cc, :], SSG[:, cc, :], 1.0 / 256, EPS, ALU.mult, ALU.add), s_msg)
                    dve.wait_ge(s_rsg, cc + 1)
                    for g in range(SG):
                        zg = Z[:, cc, 256 * g:256 * g + 256]
                        ins = dve.scalar_tensor_tensor(zg, zg, RSG[:, cc, g:g + 1], SNW[:, 256 * g:256 * g + 256], ALU.mult, ALU.mult)
                    signal(ins, s_ynn)

                for cc in range(TT):
                    if cc >= 1:
                        dve.wait_ge(s_st, 2 * cc)
                    link(dve.tensor_tensor(heads(XW), heads(XS[:, cc, :]), each(DTT[:, cc, :], SH), ALU.mult))
                    if cc < TT - 1:
                        link(dve.tensor_tensor(heads(XD), heads(XW), each(DEND[:, cc, :], SH), ALU.mult))
                    dve.sem_inc(s_xw, 1)
                    for g in range(SG):
                        dve.wait_ge(s_cb, cc + 1)
                        dve.wait_ge(s_mx, 4 * cc + g + 1)
                        cb = PS[4][:, g * P:(g + 1) * P].rearrange("p (a l) -> p a l", a=1).broadcast_to([P, 4, P])
                        signal(dve.tensor_tensor(MT[g % 2], MT[g % 2], cb, ALU.mult), s_mt)
                        if g % 2 == 0:
                            continue
                        hf, hs = g // 2, slice(8 * (g // 2), 8 * (g // 2) + 8)
                        cols = slice(512 * hf, 512 * hf + 512)
                        link(dve.tensor_tensor(heads(YT2, 8), heads(XS[:, cc, cols], 8), each(BC[:, B_D + 8 * hf:B_D + 8 * hf + 8], 8), ALU.mult))
                        dve.wait_ge(s_st, 2 * cc + hf + 1)
                        if cc:
                            link(dve.tensor_tensor(heads(YT1, 8), heads(PS[6][:, :], 8), each(EACS[:, cc, hs], 8), ALU.mult))
                            link(dve.tensor_tensor(YT1, YT1, PS[5][:, :], ALU.add))
                        else:
                            link(dve.tensor_copy(YT1, PS[5][:, :]))
                        dve.sem_inc(s_ydf, 1)
                        link(dve.tensor_tensor(YT1, YT1, YT2, ALU.add))
                        signal(dve.tensor_tensor(Z[:, cc, cols], YT1, Z[:, cc, cols], ALU.mult), s_yn)
                        if cc < TT - 1:
                            if cc:
                                link(dve.tensor_tensor(heads(ST[:, cols], 8), heads(ST[:, cols], 8), each(ETOT[:, cc, hs], 8), ALU.mult))
                                link(dve.tensor_tensor(ST[:, cols], ST[:, cols], PS[7][:, :], ALU.add))
                            else:
                                link(dve.tensor_copy(ST[:, cols], PS[7][:, :]))
                            dve.sem_inc(s_ste, 1)
                        if hf == 0 and cc >= 1:
                            norm_chunk(cc - 1)
                norm_chunk(TT - 1)

                dve.wait_ge(s_pos, 16)
                posf = PB[1]
                link(dve.tensor_copy(posf, POSR.bitcast(I32)))
                for i in range(TT):
                    n = (i + 1) * P
                    link(dve.tensor_scalar(DIST[:, i, 0:n], posf[:, 0:n], POSQ[:, i:i + 1], None, ALU.subtract))
                    link(dve.scalar_tensor_tensor(DIST[:, i, 0:n], DIST[:, i, 0:n], -1.0, DIST[:, i, 0:n], ALU.mult, ALU.max))
                    link(dve.tensor_tensor(DIST[:, i, 0:n], DIST[:, i, 0:n], CON[:, C_CM + 512 - n:C_CM + 512], ALU.subtract))

                def maxima(b, n, scale, count):
                    link(dve.tensor_reduce(MX[:, b:b + 1], PB[b][:, 0:n], AX, ALU.max))
                    signal(dve.tensor_scalar(NB_[:, b:b + 1], MX[:, b:b + 1], -scale, None, ALU.mult), s_nb)

                def diff_scores(u):
                    h, i = u // 4, u % 4
                    n = (i + 1) * P
                    if u >= 2:
                        dve.wait_ge(s_tp, u - 1)
                    for m in range(2):
                        b = (2 * u + m) % 4
                        dve.wait_ge(s_sc, 2 * u + m + 1)
                        signal(dve.scalar_tensor_tensor(PB[b][:, 0:n], DIST[:, i, 0:n], -SLOPES[h] / DIFF_SCALE, PS[2 + b][:, 0:n],
                                                        ALU.mult, ALU.add), s_scf)
                        maxima(b, n, DIFF_SCALE, 2 * u + m)

                def diff_probs(u):
                    i, b = u % 4, 2 * (u % 2)
                    n = (i + 1) * P
                    dve.wait_ge(s_ex, 2 * u + 2)
                    link(dve.reciprocal(RR[:, b:b + 2], SE[:, b:b + 2]))
                    link(dve.tensor_tensor(RR[:, b + 1:b + 2], RR[:, b + 1:b + 2], LAM, ALU.mult))
                    link(dve.tensor_scalar(PB[b + 1][:, 0:n], PB[b + 1][:, 0:n], RR[:, b + 1:b + 2], None, ALU.mult))
                    signal(dve.scalar_tensor_tensor(PB[b][:, 0:n], PB[b][:, 0:n], RR[:, b:b + 1], PB[b + 1][:, 0:n], ALU.mult, ALU.subtract), s_at)

                for u in range(19):
                    if u >= 6 and (u - 6) % 4 == 0:
                        h = (u - 6) // 4
                        dve.wait_ge(s_rst, h + 1)
                        signal(dve.scalar_tensor_tensor(YA[:, 1, h, :], PS[7][:, :], SUBW, RSB, ALU.mult, ALU.mult), s_ya)
                    if u < 16:
                        diff_scores(u)
                    if 1 <= u <= 16:
                        diff_probs(u - 1)

                for m in range(3):
                    bank, free, _ = acc_ready(("C", m))
                    signal(dve.tensor_copy(CQT[:, m, :] if m < 2 else CKVT, bank[:, :]), free)

                def rotate(dst, bank, free, done):
                    link(dve.tensor_tensor(dst, bank[0:64, :], TRIG[0:64, :], ALU.mult))
                    signal(dve.tensor_tensor(ROT[0:64, :], bank[64:128, :], TRIG[64:128, :], ALU.mult), free)
                    signal(dve.tensor_tensor(dst, dst, ROT[0:64, :], ALU.add), done)

                bank, free, _ = acc_ready(("C", 3))
                rotate(KPE[0:64, :], bank, free, s_kpe)
                dve.wait_ge(s_crs, 1)
                for m in range(2):
                    link(dve.scalar_tensor_tensor(CQT[:, m, :], CQT[:, m, :], COLS[:, R_QN + m:R_QN + m + 1], RSB, ALU.mult, ALU.mult))
                dve.sem_inc(s_cn, 1)
                dve.wait_ge(s_crs, 2)
                signal(dve.scalar_tensor_tensor(CKVT, CKVT, COLS[:, R_KN:R_KN + 1], RSB, ALU.mult, ALU.mult), s_cn)
                for h in range(NH):
                    bank, free, _ = acc_ready(("QP", h))
                    rotate(QP[0:64, h, :], bank, free, s_qpr)

                def mla_scores(u):
                    b, n = u % 4, (u % 4 + 1) * P
                    if u >= 4:
                        dve.wait_ge(s_tp, 16 + u - 3)
                    dve.wait_ge(s_sc, 32 + u + 1)
                    signal(dve.tensor_tensor(PB[b][:, 0:n], PS[2 + b][:, 0:n], CON[:, C_CM + 512 - n:C_CM + 512], ALU.add), s_scf)
                    maxima(b, n, MLA_SCALE, 32 + u)

                def mla_probs(u):
                    b, n = u % 4, (u % 4 + 1) * P
                    dve.wait_ge(s_ex, 32 + u + 1)
                    link(dve.reciprocal(RR[:, b:b + 1], SE[:, b:b + 1]))
                    signal(dve.tensor_scalar(PB[b][:, 0:n], PB[b][:, 0:n], RR[:, b:b + 1], None, ALU.mult), s_at)

                for u in range(19):
                    if u >= 6 and (u - 6) % 4 == 0:
                        h = (u - 6) // 4
                        dve.wait_ge(s_pv, NH + h + 1)
                        signal(dve.tensor_copy(YA[:, 0, h, :], PS[7][:, :]), s_ya)
                    if u < 16:
                        mla_scores(u)
                    if 1 <= u <= 16:
                        mla_probs(u - 1)

                for j in range(4, 12):
                    bank, free, _ = acc_ready(("A", j))
                    row = MOD[:, j // 2, (j % 2) * CH:(j % 2 + 1) * CH]
                    signal(dve.tensor_tensor(row, bank[:, :], row, ALU.add), free)
                link(dve.scalar_tensor_tensor(MOD[:, 4], MOD[:, 4], 1.0, NW2, ALU.add, ALU.mult))

                def residual(t):
                    if t >= 2:
                        dve.wait_ge(s_nt, t - 1)
                        dve.wait_ge(s_h2st, 16 * (t - 1))
                    dve.wait_ge(s_o, t + 1)
                    for q in range(2):
                        cols = slice(q * CH, (q + 1) * CH)
                        link(dve.tensor_tensor(H2R[t % 2][:, cols], PS[2 * t + q][:, :], MOD[:, 2, cols], ALU.mult))
                    signal(dve.tensor_tensor(X[:, t, :], X[:, t, :], H2R[t % 2], ALU.add), s_xr)

                def norm2(t):
                    dve.wait_ge(s_ss2, t + 1)
                    signal(dve.tensor_scalar(MS[:, t:t + 1], SS[:, t:t + 1], 1.0 / D, EPS, ALU.mult, ALU.add), s_ms)
                    dve.wait_ge(s_rs, t + 2)
                    link(dve.scalar_tensor_tensor(H2R[t % 2], X[:, t, :], RS[:, t:t + 1], MOD[:, 4], ALU.mult, ALU.mult))
                    signal(dve.tensor_tensor(H2R[t % 2], H2R[t % 2], MOD[:, 3], ALU.add), s_h2)

                residual(0)
                for t in range(TT):
                    norm2(t)
                    if t + 1 < TT:
                        residual(t + 1)

                for t in range(TT):
                    dve.wait_ge(s_lg, t + 1)
                    dve.tensor_tensor(GL[:, t, :], PS[2 * t][:, 0:NG], BC[:, B_RB:B_RB + NG], ALU.add)
                    link(dve.tensor_tensor(EL[:, t, :], PS[2 * t][:, NG:NG + NE], BC[:, B_RB + NG:B_RB + NG + NE], ALU.add))

                def per_token(v, n):
                    return v.rearrange("p (t a) -> p t a", a=1).broadcast_to([P, TT, n])

                def per_entry(v, n):
                    return v.rearrange("p (a e) -> p a e", a=1).broadcast_to([P, TT, n])

                def first_of_max(oh, v, best, order, n):
                    link(dve.tensor_reduce(best, v, AX, ALU.max))
                    link(dve.tensor_tensor(oh, v, per_token(best, n), ALU.is_equal))
                    link(dve.tensor_tensor(oh, oh, per_entry(order, n), ALU.mult))
                    link(dve.tensor_reduce(RV, oh, AX, ALU.max))
                    link(dve.tensor_tensor(oh, oh, per_token(RV, n), ALU.is_equal))

                first_of_max(PEN, GL, RM, CON[:, C_D4:C_D4 + 4], NG)
                signal(dve.tensor_tensor(GE, GL, per_token(RM, NG), ALU.subtract), s_ge)
                link(dve.tensor_scalar(flat(PEN), flat(PEN), -1.0, -NEG, ALU.add, ALU.mult))
                by_group = lambda v: v.rearrange("p t (g e) -> p (t g) e", g=NG)
                link(dve.tensor_tensor(by_group(LM), by_group(EL),
                                       flat(PEN).rearrange("p (a b) -> p a b", b=1).broadcast_to([P, TT * NG, NE_G]), ALU.add))
                first_of_max(OH1, LM, R1, CON[:, C_D32:C_D32 + 32], NE)
                link(dve.scalar_tensor_tensor(flat(LM), flat(OH1), 2 * NEG, flat(LM), ALU.mult, ALU.add))
                first_of_max(OH2, LM, R2, CON[:, C_D32:C_D32 + 32], NE)
                signal(dve.tensor_tensor(RW, R2, R1, ALU.subtract), s_ge)
                signal(dve.tensor_tensor(MM, OH1, OH2, ALU.add), s_oh)
                dve.wait_ge(s_gf, 2)
                link(dve.tensor_reduce(R3, GE, AX, ALU.add))
                link(dve.reciprocal(R3, R3))
                link(dve.tensor_scalar(R4, RW, 1.0, None, ALU.add))
                link(dve.reciprocal(R4, R4))
                link(dve.tensor_tensor(R3, R3, R4, ALU.mult))
                weight = PAY[:, :, :, :].bitcast(F32)
                link(dve.tensor_copy(weight[:, :, 0, 2], R3))
                link(dve.tensor_tensor(weight[:, :, 1, 2], R3, RW, ALU.mult))
                dve.wait_ge(s_pp, 1)
                cnt = PS[1][0:NE, 64:65]
                for k, limit in enumerate((P, 2 * P, 3 * P)):
                    link(dve.tensor_scalar(OVT[:, k:k + 1], cnt, float(limit), None, ALU.is_gt))
                link(dve.tensor_tensor(OVT[:, 0:1], OVT[:, 0:1], OVT[:, 1:2], ALU.add))
                link(dve.tensor_tensor(OVT[:, 0:1], OVT[:, 0:1], OVT[:, 2:3], ALU.add))
                signal(dve.tensor_scalar(OVR, ONE[0:NE, :], OVT[:, 0:1], None, ALU.mult), s_ovt)
                link(dve.tensor_copy(flat(POS), PS[0][:, 0:TT * NE]))
                link(dve.tensor_scalar(flat(BLK), flat(POS), float(P), None, ALU.is_ge))
                for limit in (2 * P, 3 * P):
                    link(dve.scalar_tensor_tensor(flat(BLK), flat(POS), float(limit), flat(BLK), ALU.is_ge, ALU.add))
                link(dve.scalar_tensor_tensor(flat(ROWF), flat(BLK), -float(P), flat(POS), ALU.mult, ALU.add))
                dve.wait_ge(s_ov2, 1)
                link(dve.tensor_copy(OVS, PS[2][:, 0:NE]))
                link(dve.tensor_copy(OVE, PS[2][:, 64:64 + NE]))
                row0 = lambda v, n: v.rearrange("p (a e) -> p a e", a=1).broadcast_to([1, 8, n])
                link(dve.tensor_tensor(KCMP, row0(OVE[0:1, :], NE),
                                       CON[0:1, C_K8:C_K8 + 8].rearrange("p (k a) -> p k a", a=1).broadcast_to([1, 8, NE]), ALU.is_le))
                link(dve.tensor_reduce(NPF[:, 0:8], KCMP, AX, ALU.add))
                link(dve.tensor_scalar(EID[0:1, 32:40], NPF[:, 0:8], float(NE - 1), None, ALU.min))
                over = PS[2][0:1, 128:129]
                link(dve.tensor_scalar(NPF[:, 8:9], over, 0.0, 16.0, ALU.is_gt, ALU.add))
                for limit in (2.0, 4.0, 6.0):
                    link(dve.scalar_tensor_tensor(NPF[:, 8:9], over, limit, NPF[:, 8:9], ALU.is_gt, ALU.add))
                link(dve.tensor_copy(EID[0:1, 40:41], NPF[:, 8:9]))
                signal(dve.tensor_scalar(EID[0:1, 41:42], NPF[:, 8:9], -1.0, None, ALU.add), s_eid)
                link(dve.tensor_tensor(TMPE, BLK, per_entry(OVS, NE), ALU.add))
                link(dve.tensor_scalar(flat(TMPE), flat(TMPE), float(NE - 1), None, ALU.add))
                e32 = per_entry(CON[:, C_E32:C_E32 + 32], NE)
                link(dve.tensor_tensor(TMPE, TMPE, e32, ALU.subtract))
                link(dve.scalar_tensor_tensor(flat(TMPE), flat(BLK), 0.0, flat(TMPE), ALU.is_gt, ALU.mult))
                link(dve.tensor_tensor(TMPE, TMPE, e32, ALU.add))
                link(dve.scalar_tensor_tensor(flat(ROWF), flat(ROWF), float(NB_MAX), flat(TMPE), ALU.mult, ALU.add))
                for s, oh in enumerate((OH1, OH2)):
                    link(dve.tensor_tensor(TMPE, oh, ROWF, ALU.mult))
                    link(dve.tensor_reduce(RV, TMPE, AX, ALU.add))
                    link(dve.tensor_copy(ROWI[:, s:8:2], RV))
                dve.sem_inc(s_row, 1)

                n_pairs = pairs(dve)
                dve.sem_inc(s_ye[0], 1)

                def rows_turned(s, count):
                    dve.wait_ge(s_xt, count)
                    dve.tensor_copy(XGT[s][:, 4:8, :], PS[1][:, :].rearrange("p (k j) -> p k j", k=4)).then_inc(s_xte[1], 1)

                def hidden(i, s):
                    dve.wait_ge(s_slot[s], i + 1)
                    dve.wait_ge(s_gs, i * 2 + (s + 1))
                    dve.wait_ge(s_u, i * 2 + (s + 1))
                    dve.scalar_tensor_tensor(HH, PS[3][:, :], SIDX[s][:, 2:3].bitcast(F32), GS, ALU.mult, ALU.mult).then_inc(s_hh, 1)

                def output_half(i, s):
                    dve.wait_ge(s_y[0], i * 2 + (s + 1))
                    dve.tensor_copy(YB[s][:, 0:CH], PS[5][:, :]).then_inc(s_ye[0], 1)

                rows_turned(0, 1)
                with dve.Fori(0, n_pairs) as i:
                    hidden(i, 0)
                    rows_turned(1, i * 2 + 2)
                    hidden(i, 1)
                    output_half(i, 0)
                    output_half(i, 1)
                    rows_turned(0, i * 2 + 3)
                for t in range(TT):
                    dve.wait_ge(s_cmb[t], 16)
                    link(dve.tensor_tensor(CB[t][:, 0:D], CB[t][:, 0:D], CB[t][:, D:2 * D], ALU.add))
                    link(dve.tensor_tensor(CB[t][:, 0:D], CB[t][:, 0:D], MOD[:, 5], ALU.mult))
                    link(dve.tensor_tensor(X[:, t, :], X[:, t, :], CB[t][:, 0:D], ALU.add))
                dve.sem_inc(s_end, 1)
                dve.wait_ge(s_clr, l + 1)
                dve.sem_inc(s_seq, 1)
            dve.sem_inc(s_fss, 1)
            dve.wait_ge(s_prot, TT)
            olink(dve.tensor_scalar(MS, SS, 1.0 / D, EPS, ALU.mult, ALU.add))
            dve.sem_inc(s_fin, 1)
            dve.wait_ge(s_finr, 1)
            dve.wait_ge(s_fw, 16)
            for t in range(TT):
                dve.scalar_tensor_tensor(X[:, t, :], X[:, t, :], RS[:, t:t + 1], MOD[:, 0], ALU.mult, ALU.mult).then_inc(s_fout, 1)

        @block.tensor
        def _(pe):
            pe.wait_ge(s_con, 80)
            pe.transpose(PS[2][:, 0:KT], CROW, ID[0:KT, 0:KT]).then_inc(s_pro, 1)
            pe.wait_ge(s_proa, 2)
            ln = dict(start=True, stop=True)

            with pe.Fori(0, L) as l:
                def begin(name):
                    bank, free, k = acc_bank(name)
                    if k >= 2:
                        pe.wait_ge(free, k - 1)
                    return bank

                def begin_tr(name):
                    bank, free, k = tr_bank(name)
                    if k >= 2:
                        pe.wait_ge(free, k - 1)
                    return bank

                def chunk(name):
                    n = CHN[name]
                    pe.wait_ge(s_load[n % 2], slot_count(n))
                    return SLOT[n % 2]

                def tile_of(v, t):
                    return v[:, t * P:(t + 1) * P]

                def turn(bank, blocks, done):
                    for j, v in enumerate(blocks):
                        ins = pe.transpose(bank[:, j * P:(j + 1) * P], v, ID)
                    ins.then_inc(done, 1)

                def ada(j):
                    w = chunk(("A", j)).rearrange("p (k n) -> p k n", k=KT)
                    bank = begin(("A", j))
                    for k in range(KT):
                        ins = pe.matmul(bank[:, :], COND[:, k:k + 1].broadcast_to([P, P]), w[:, k, :], start=(k == 0), stop=(k == KT - 1))
                    ins.then_inc(s_acc, 1)

                def project(name, lhs, rhs):
                    bank = begin(name)
                    n = len(lhs)
                    for k in range(n):
                        ins = pe.matmul(bank[:, :], lhs[k], rhs[k], start=(k == 0), stop=(k == n - 1))
                    ins.then_inc(s_acc, 1)

                def in_feature(name, j, m):
                    w = chunk(("I", j)).rearrange("p (k n) -> p k n", k=KT)
                    project(name, [tile_of(w[:, k, :], m) for k in range(KT)], [HT[:, k, :] for k in range(KT)])

                def in_token(name, j, t):
                    w = chunk(("I", j)).rearrange("p (k n) -> p k n", k=KT)
                    project(name, [tile_of(HT[:, k, :], t) for k in range(KT)], [w[:, k, :] for k in range(KT)])

                pe.wait_ge(s_par, N_PAR)
                bank = begin_tr("P")
                pe.transpose(bank[:, 0:R_N], ROWS, ID[0:R_N, 0:R_N]).then_inc(s_tr, 1)
                for j in range(4):
                    ada(j)
                for t in range(TT):
                    pe.wait_ge(s_hr, t + 1)
                    for q in range(2):
                        turn(begin_tr(("H", t, q)), [tile_of(HR[t % 2], 4 * q + k) for k in range(4)], s_tr)
                turned_out(pe, ("H", 3, 0))
                turned_out(pe, ("H", 3, 1))
                def token_major(m):
                    bank = begin_tr(("T", m))
                    pe.wait_ge(s_sx, m + 1)
                    src = SX[m % 2] if m < 8 else BT[:, m - 8, :]
                    turn(bank, [tile_of(src, t) for t in range(TT)], s_tr)

                for m in range(16):
                    in_feature(("X", m), m // 4, m % 4)
                    if 1 <= m <= 12:
                        token_major(m - 1)
                for m in range(8):
                    in_token(("Z", m), 4 + m // 4, m % 4)
                bank = begin("DT")
                for t in range(TT):
                    for k in range(KT):
                        ins = pe.matmul(bank[:, t * SH:(t + 1) * SH], tile_of(HT[:, k, :], t), WDT[:, k, :], start=(k == 0), stop=(k == KT - 1))
                ins.then_inc(s_acc, 1)
                bank = begin("AC")
                pe.wait_ge(s_adt, 1)
                pe.matmul(bank[:, 0:TT * SH], UU, flat(ADT), **ln)
                pe.matmul(bank[:, TT * SH:2 * TT * SH], ONE, flat(ADT), **ln).then_inc(s_acc, 1)
                bank = begin_tr("AT")
                pe.wait_ge(s_acs, 1)
                pe.transpose(bank[0:TT * SH, 0:P], flat(ACS), ID).then_inc(s_tr, 1)
                turned_out(pe, "AT")
                pe.wait_ge(s_sx, 16)

                def decay_rows(cc, g):
                    bank = begin(("R", cc, g))
                    pe.matmul(bank[:, :], IDB[:, :], CMB[:, :].rearrange("p (a l) -> p a l", a=1).broadcast_to([P, 4, P]), start=True, stop=False)
                    for h in range(4):
                        j = cc * SH + 4 * g + h
                        ins = pe.matmul(tile_of(bank, h), ID[0:TT * SH, j:j + 1].broadcast_to([TT * SH, P]), ACST,
                                        start=False, stop=(h == 3))
                    ins.then_inc(s_acc, 1)

                def ssd_group(cc, g):
                    hf = g // 2
                    pe.wait_ge(s_mt, 4 * cc + g + 1)
                    if g % 2 == 0 and cc + hf:
                        pe.wait_ge(s_ydf, 2 * cc + hf)
                    for h in range(4):
                        at = (4 * (g % 2) + h) * SP_
                        ins = pe.matmul(PS[5][:, at:at + SP_], MT[g % 2][:, h, :], XW[:, (4 * g + h) * SP_:(4 * g + h + 1) * SP_], **ln)
                    ins.then_inc(s_yd, 1)
                    half = slice((g % 2) * 256, (g % 2) * 256 + 256)
                    cols = slice(g * 256, g * 256 + 256)
                    last = g % 2 == 1
                    if cc:
                        if g % 2 == 0:
                            pe.wait_ge(s_ste, 2 * (cc - 1) + hf + 1)
                        ins = pe.matmul(PS[6][:, half], tile_of(CT[:, g, :], cc), ST[:, cols], **ln)
                        if last and cc == TT - 1:
                            ins.then_inc(s_st, 1)
                    if cc < TT - 1:
                        if g % 2 == 0 and cc + hf:
                            pe.wait_ge(s_ste, 2 * cc + hf)
                        ins = pe.matmul(PS[7][:, half], tile_of(BTOK[:, cc, :], g), XD[:, cols], **ln)
                        if last:
                            ins.then_inc(s_st, 1)

                for cc in range(TT):
                    if cc:
                        pe.wait_ge(s_mt, 4 * cc)
                    for g in range(SG):
                        ins = pe.matmul(tile_of(PS[4], g), tile_of(BT[:, g, :], cc), tile_of(CT[:, g, :], cc), **ln)
                    ins.then_inc(s_cb, 1)
                    decay_rows(cc, 0)
                    decay_rows(cc, 1)
                    pe.wait_ge(s_xw, cc + 1)
                    for g in range(SG):
                        ssd_group(cc, g)
                        if g < 2:
                            decay_rows(cc, g + 2)
                for m in range(4):
                    in_feature(("DQ", m), 6, m)
                for m in range(4):
                    in_feature(("DK", m), 7, m)
                for m in range(4):
                    in_token(("DV", m), 8, m)

                def transposed(k, buf):
                    pe.wait_ge(s_at, k + 1)
                    if k:
                        pe.wait_ge(s_pt, k)
                    turn(PS[6], [tile_of(buf, j) for j in range(k % 4 + 1)], s_tp)

                def values(h, v):
                    pe.wait_ge(s_pt, 4 * h + 4)
                    if h:
                        pe.wait_ge(s_ya, h)
                    for j in range(TT):
                        ins = pe.matmul(PS[7][:, j * P:T], v[j], PT[:, j, j * P:T], start=(j == 0), stop=(j == TT - 1))
                    ins.then_inc(s_pv, 1)

                def diff_scores(u):
                    h, i = u // 4, u % 4
                    for m in range(2):
                        k = 2 * u + m
                        b, rows = k % 4, slice(64 * m, 64 * m + 64)
                        if k >= 4:
                            pe.wait_ge(s_scf, k - 3)
                        pe.matmul(PS[2 + b][:, 0:(i + 1) * P], DQT[rows, h, i * P:(i + 1) * P], DKT[rows, h, 0:(i + 1) * P], **ln).then_inc(s_sc, 1)

                evacuated(pe, ("DV", 2))
                evacuated(pe, ("DV", 3))
                pe.wait_ge(s_ydf, 8)
                pe.wait_ge(s_ste, 6)
                for u in range(19):
                    if u < 16:
                        diff_scores(u)
                    if u >= 6 and (u - 6) % 4 == 0:
                        h = (u - 6) // 4
                        bank = begin(("DS", h))
                        pe.wait_ge(s_sq, h + 1)
                        pe.matmul(bank[:, :], ONE, SQB, **ln).then_inc(s_acc, 1)
                    if 2 <= u <= 17:
                        transposed(u - 2, PB[2 * (u % 2)])
                        if u % 4 == 1:
                            h = (u - 2) // 4
                            values(h, [DVT[:, j, h * P:(h + 1) * P] for j in range(TT)])
                for m in range(4):
                    in_feature(("C", m), 9, m)
                bank = begin("SQ")
                pe.wait_ge(s_csq, 2)
                pe.matmul(bank[:, :], ONE, SQB, start=True, stop=False)
                pe.matmul(bank[:, :], ONE, PB[0], start=False, stop=True).then_inc(s_acc, 1)
                bank = begin("SK")
                pe.wait_ge(s_csq, 3)
                pe.matmul(bank[:, :], ONE, SQB, **ln).then_inc(s_acc, 1)
                pe.wait_ge(s_scf, 32)
                for cc in range(TT):
                    pe.wait_ge(s_ynn, cc + 1)
                    for q in range(2):
                        turn(begin_tr(("Y", cc, q)), [tile_of(Z[:, cc, :], 4 * q + k) for k in range(4)], s_tr)
                w = chunk("U")
                uq = w[:, 0:2048].rearrange("p (k h n) -> p k h n", k=2, h=NH)
                ukv = w[:, 2048:3072].rearrange("p (h n) -> p h n", h=NH)
                pe.wait_ge(s_cn, 1)
                for h in range(NH):
                    project(("QN", h), [uq[:, k, h, 0:P] for k in range(2)], [CQT[:, k, :] for k in range(2)])
                for h in range(NH):
                    project(("QP", h), [uq[:, k, h, P:2 * P] for k in range(2)], [CQT[:, k, :] for k in range(2)])
                pe.wait_ge(s_cn, 2)
                for h in range(NH):
                    project(("KN", h), [ukv[:, h, 0:P]], [CKVT])
                for t in range(TT):
                    bank = begin(("V", t))
                    pe.matmul(bank[:, :].rearrange("p (h n) -> p h n", h=NH), tile_of(CKVT, t), ukv[:, :, P:2 * P], **ln).then_inc(s_acc, 1)

                def mla_scores(u):
                    h, i, b = u // 4, u % 4, u % 4
                    if u >= 4:
                        pe.wait_ge(s_scf, 32 + u - 3)
                    out_, n = PS[2 + b], (i + 1) * P
                    pe.matmul(out_[:, 0:n], tile_of(QN[:, h, :], i), KN[:, h, 0:n], start=True, stop=False)
                    pe.matmul(out_[:, 0:n], tile_of(QP[0:64, h, :], i), KPE[0:64, 0:n], start=False, stop=True).then_inc(s_sc, 1)

                turned_out(pe, ("Y", 3, 0))
                turned_out(pe, ("Y", 3, 1))
                evacuated(pe, ("V", 2))
                evacuated(pe, ("V", 3))
                pe.wait_ge(s_kpe, 1)
                pe.wait_ge(s_qpr, NH)
                for u in range(18):
                    if u < 16:
                        mla_scores(u)
                    if u >= 2:
                        transposed(16 + u - 2, PB[(u - 2) % 4])
                        if u % 4 == 1:
                            h = (u - 2) // 4
                            values(NH + h, [VT[:, j, h * P:(h + 1) * P] for j in range(TT)])
                for j in range(4, 12):
                    ada(j)
                evacuated(pe, ("A", 10))
                evacuated(pe, ("A", 11))
                pe.wait_ge(s_scf, 48)
                pe.wait_ge(s_pt, 32)
                pe.wait_ge(s_ya, 2 * NH)
                for j in range(4):
                    w = chunk(("O", j)).rearrange("p (f n) -> p f n", f=4)
                    src = (YA[:, 0], YA[:, 1], HT[:, 0:4], HT[:, 4:8])[j]
                    for t in range(TT):
                        for q in range(2):
                            for f in range(4):
                                ins = pe.matmul(PS[2 * t + q][:, :], tile_of(src[:, f, :], t), w[:, f, q * CH:(q + 1) * CH],
                                                start=(j == 0 and f == 0), stop=(j == 3 and f == 3))
                        if j == 3:
                            ins.then_inc(s_o, 1)
                    if j < 3:
                        ins.then_inc(s_oc, 1)
                def logits(t):
                    pe.wait_ge(s_ntf, t + 1)
                    for k in range(KT):
                        ins = pe.matmul(PS[2 * t][:, 0:NG + NE], tile_of(H2T[:, k, :], t), WR[:, k, :], start=(k == 0), stop=(k == KT - 1))
                    ins.then_inc(s_lg, 1)

                for t in range(TT):
                    pe.wait_ge(s_h2, t + 1)
                    for q in range(2):
                        for k in range(4):
                            ins = pe.transpose(tile_of(PS[2 * t + q], k), tile_of(H2R[t % 2], 4 * q + k), ID)
                    ins.then_inc(s_nt, 1)
                    if t:
                        logits(t - 1)
                logits(TT - 1)
                pe.wait_ge(s_oh, 1)
                for t in range(TT):
                    for before in range(t):
                        pe.matmul(PS[0][:, t * NE:(t + 1) * NE], ONE, MM[:, before, :], start=(before == 0), stop=False)
                    pe.matmul(PS[0][:, t * NE:(t + 1) * NE], SU, MM[:, t, :], start=(t == 0), stop=True)
                for t in range(TT):
                    ins = pe.matmul(PS[1][0:NE, 64:65], MM[:, t, :], ONE[:, 0:1], start=(t == 0), stop=(t == TT - 1))
                ins.then_inc(s_pp, 1)
                pe.wait_ge(s_ovt, 1)
                pe.matmul(PS[2][:, 0:NE], OVR, SU[0:NE, 0:NE], **ln)
                pe.matmul(PS[2][:, 64:64 + NE], OVR, UU[0:NE, 0:NE], **ln)
                pe.matmul(PS[2][:, 128:129], OVR, ONE[0:NE, 0:1], **ln).then_inc(s_ov2, 1)

                n_pairs = pairs(pe)

                def landed(i, m):
                    slot = (m + 2) % 6
                    pe.wait_ge(s_load[slot], i * 16 + (SLOT_BASE[slot] + 16))
                    return SLOT[slot]

                def turn_rows(s):
                    for q in range(2):
                        for k in range(4):
                            ins = pe.transpose(tile_of(PS[q], k), tile_of(XG[s], 4 * q + k), ID)
                    ins.then_inc(s_xt, 1)

                def hidden_in(i, s, m, bank, done):
                    w = landed(i, m).rearrange("p (k n) -> p k n", k=KT)
                    for k in range(KT):
                        ins = pe.matmul(PS[bank][:, :], XGT[s][:, k, :], w[:, k, :], start=(k == 0), stop=(k == KT - 1))
                    ins.then_inc(done, 1)

                def gate_up(i, s):
                    for q in s_xte:
                        pe.wait_ge(q, i * 2 + (s + 1))
                    hidden_in(i, s, 2 * s, 2, s_g)
                    hidden_in(i, s, 2 * s + 1, 3, s_u)

                def turn_hidden(i, s):
                    pe.wait_ge(s_hh, i * 2 + (s + 1))
                    for k in range(4):
                        ins = pe.transpose(tile_of(PS[4], k), tile_of(HH, k), ID)
                    ins.then_inc(s_htp, 1)

                def down(i, s, q):
                    w = landed(i, 4 + s).rearrange("p (k n) -> p k n", k=4)
                    pe.wait_ge(s_hte, i * 2 + (s + 1))
                    pe.wait_ge(s_ye[q], i * 2 + (s + 1))
                    for k in range(4):
                        ins = pe.matmul(PS[5 + q][:, :], HHT[s][:, k, :], w[:, k, q * CH:(q + 1) * CH], start=(k == 0), stop=(k == 3))
                    ins.then_inc(s_y[q], 1)

                pe.wait_ge(s_gd[0], 16)
                turn_rows(0)
                with pe.Fori(0, n_pairs) as i:
                    gate_up(i, 0)
                    pe.wait_ge(s_gd[1], i * 16 + 16)
                    turn_rows(1)
                    turn_hidden(i, 0)
                    gate_up(i, 1)
                    down(i, 0, 0)
                    turn_hidden(i, 1)
                    down(i, 0, 1)
                    down(i, 1, 0)
                    pe.wait_ge(s_gd[0], i * 16 + 32)
                    turn_rows(0)
                    down(i, 1, 1)
                pe.sem_inc(s_end, 1)
                pe.wait_ge(s_clr, l + 1)
                pe.sem_inc(s_seq, 1)


INS = ["x", "c", "positions", "w_ada", "b_ada", "norm1_w", "w_in", "mla_q_norm_w", "mla_w_uq", "mla_kv_norm_w", "mla_w_ukv",
       "diff_lambda", "diff_subln_w", "ssd_conv_w", "ssd_conv_b", "ssd_dt_bias", "ssd_a_log", "ssd_d", "ssd_norm_w",
       "w_out", "norm2_w", "router_w_group", "router_b_group", "router_w_expert", "router_b_expert",
       "exp_w_gate", "exp_w_up", "exp_w_down", "final_norm_w"]


def kernel(**inputs):
    import concourse.bacc as bacc
    from concourse.bass_utils import run_bass_kernel_spmd

    nc = bacc.Bacc("TRN2", target_bir_lowering=False, num_devices=1)
    arrays = {f"in_{name}": np.ascontiguousarray(inputs[name]) for name in INS}
    arrays.update({f"in_{name}": a for name, a in shape_constants().items()})
    args = [nc.dram_tensor(n, a.shape, mybir.dt.from_np(a.dtype), kind="ExternalInput").ap() for n, a in arrays.items()]
    out = nc.dram_tensor("out", (1, T, D), F32, kind="ExternalOutput").ap()
    h2_rows = nc.dram_tensor("h2_rows", (T, D), F32, kind="Internal").ap()
    expert_rows = nc.dram_tensor("expert_rows", (2 * T, D), F32, kind="Internal").ap()
    slot_table = nc.dram_tensor("slot_table", (P * NB_MAX, 4), I32, kind="Internal").ap()
    hybrid_kernel(nc, *args, out, h2_rows, expert_rows, slot_table)
    r = run_bass_kernel_spmd(nc, [arrays], core_ids=[0])
    return r.results[0]["out"]
```

```python
import math
from contextlib import ExitStack

import numpy as np
import concourse.bass as bass
from concourse import mybir

F32 = mybir.dt.float32
F32R = mybir.dt.float32r
BF16 = mybir.dt.bfloat16
I32 = mybir.dt.int32
U32 = mybir.dt.uint32
ALU = mybir.AluOpType
ACT = mybir.ActivationFunctionType
AX = mybir.AxisListType.X

P = 128
T, D, L = 512, 1024, 2
TT, KT = T // P, D // P
NH = 4
MQ, MKV, DN, DR, DV = 256, 128, 128, 64, 128
DQK = 64
SH, SP_, SG, SN_, SC = 16, 64, 4, 128, 4
DI = SH * SP_
NG, NE_G = 4, 8
NE = NG * NE_G
FE = 512
O_CQ, O_CKV, O_KPE, O_DQ, O_DK, O_DV, O_Z, O_XBC, O_DT = 0, 256, 384, 448, 960, 1472, 1984, 3008, 5056
N_IN = 5072
EPS, SUBEPS = 1e-6, 1e-5
NEG = -1.0e30
MLA_SCALE = (DN + DR) ** -0.5
DIFF_SCALE = DQK ** -0.5
SLOPES = [2.0 ** (-8.0 / NH * (h + 1)) for h in range(NH)]
NB_MAX = 42
PAIRS_MAX = 20
CH = 512
CHE = KT * CH

C_ID, C_U, C_SU, C_ONE, C_CM = 0, 128, 256, 384, 512
C_D4, C_D32, C_E32, C_K8, C_INV, C_PH, C_HALF = 1024, 1028, 1060, 1092, 1100, 1101, 1102
C_N = 1104 + 2
B_DTB, B_ALOG, B_D, B_RB, B_LAM, B_LI = 0, 16, 32, 48, 84, 340
B_N = 342
R_CW, R_CB, R_QN, R_KN, R_SUB, R_NW1, R_BADA, R_N = 0, 64, 80, 82, 83, 84, 92, 108


def shape_constants():
    c = np.zeros((P, C_N), np.float32)
    i = np.arange(P)
    c[:, C_ID:C_ID + P] = np.eye(P)
    c[:, C_U:C_U + P] = i[:, None] <= i[None, :]
    c[:, C_SU:C_SU + P] = i[:, None] < i[None, :]
    c[:, C_ONE:C_ONE + P] = 1.0
    c[:, C_CM + 384:C_CM + 512] = np.where(i[:, None] >= i[None, :], 0.0, NEG)
    c[:, C_D4:C_D4 + 4] = 4.0 - np.arange(4)
    c[:, C_D32:C_D32 + 32] = 32.0 - np.arange(32)
    c[:, C_E32:C_E32 + 32] = np.arange(32)
    c[:, C_K8:C_K8 + 8] = np.arange(8)
    inv = (1.0 / (np.float32(10000.0) ** (np.arange(0, DR, 2, dtype=np.float32) / np.float32(DR)))).astype(np.float32)
    c[:, C_INV] = np.tile(inv, 4)
    c[0:64, C_PH], c[64:96, C_PH], c[96:128, C_PH] = 0.25, 0.5, 0.0
    c[:, C_HALF] = -0.5
    pay = np.zeros((P, TT, 2, 4), np.int32)
    tok = np.arange(TT)[None, :] * P + i[:, None]
    for s in range(2):
        pay[:, :, s, 0] = tok
        pay[:, :, s, 1] = 2 * tok + s
    table = np.zeros((P, NB_MAX, 4), np.int32)
    table[:, :, 0:2] = 1 << 20
    lam = np.array([[0.8 - 0.6 * math.exp(-0.3 * l), 1.0 - (0.8 - 0.6 * math.exp(-0.3 * l))] for l in range(L)], np.float32)
    eids = np.tile(np.arange(48, dtype=np.int32)[None, :] % 32, (1, 1))
    return {"k_const": c, "k_pay": pay.reshape(P, -1), "k_table": table.reshape(P, -1), "k_lam": lam, "k_eid": eids}


def numbered(names):
    return {n: k for k, n in enumerate(names)}


SSD_FILL = [(n, m) for n in ("DQ", "DK", "DV") for m in range(4)]
DIFF_FILL = {2 * k: n for k, n in enumerate([("C", m) for m in range(4)] + [("A", j) for j in range(4, 9)])}
MLA_FILL = {4 + 4 * k: ("A", 9 + k) for k in range(3)}


def head_ends(u):
    return u >= 6 and (u - 6) % 4 == 0


ACC = numbered(
    [("A", j) for j in range(4)] + [("X", m) for m in range(16)] + [("Z", m) for m in range(16)] + ["DT", "AC"]
    + [n for c in range(TT) for n in (("R", c, 0), ("R", c, 1), SSD_FILL[3 * c], ("R", c, 2), ("R", c, 3), *SSD_FILL[3 * c + 1:3 * c + 3])]
    + [n for u in range(19) for n in ([("DS", (u - 6) // 4)] if head_ends(u) else []) + ([DIFF_FILL[u]] if u in DIFF_FILL else [])]
    + ["SQ", "SK"]
    + [("QN", h) for h in range(NH)] + [("QP", h) for h in range(NH)] + [("KN", h) for h in range(NH)]
    + [("V", t) for t in range(TT)] + list(MLA_FILL.values()))
TRN = numbered([("H", t, q) for t in range(TT) for q in range(2)] + ["P"] + [("T", m) for m in range(12)] + ["AT"]
               + [("Y", c, q) for c in range(TT) for q in range(2)])
IN_UNITS = [("X", 2 * u + 1) for u in range(8)] + [("Z", 4 * u + 3) for u in range(4)]

CHUNKS = [("A", j) for j in range(4)] + [("I", j) for j in range(10)] + [("A", j) for j in range(4, 9)] + ["U"] + [("A", j) for j in range(9, 12)] \
    + [("O", j) for j in range(4)]
CHN = numbered(CHUNKS)
NCH = len(CHUNKS)
CHUNK_DMAS = {("I", 9): 3, "U": 7}
IN_COLS = [O_XBC, O_XBC + 512, O_XBC + 1024, O_XBC + 1536, O_Z, O_Z + 512, O_DQ, O_DK, O_DV, O_CQ]


def chunk_slot(n):
    return n + 2 if n < 4 else n % 2


def slot_count(n):
    return sum(16 * CHUNK_DMAS.get(CHUNKS[m], 1) for m in range(n + 1) if chunk_slot(m) == chunk_slot(n))


UNITS = 12


def unit_matrix(v):
    return (v // 2 + 2) % 6, v % 2, ("in", "out")[v >= 8]


SLOT_BASE = [slot_count(max(m for m in range(NCH) if chunk_slot(m) == s)) for s in range(6)]


def hybrid_kernel(nc, x, c, positions, w_ada, b_ada, norm1_w, w_in, mla_q_norm_w, mla_w_uq, mla_kv_norm_w, mla_w_ukv,
                  diff_lambda, diff_subln_w, ssd_conv_w, ssd_conv_b, ssd_dt_bias, ssd_a_log, ssd_d, ssd_norm_w,
                  w_out, norm2_w, router_w_group, router_b_group, router_w_expert, router_b_expert,
                  exp_w_gate, exp_w_up, exp_w_down, final_norm_w,
                  k_const, k_pay, k_table, k_lam, k_eid, out, h2_rows, expert_rows, slot_table):
    with ExitStack() as ctx:
        at = {}

        def sb(name, shape, dt=F32):
            at[name] = (nc.sbuf_base + 31) // 32 * 32
            return ctx.enter_context(nc.sbuf_tensor(name, shape, dt))

        def sem(name):
            s = ctx.enter_context(nc.semaphore(name))
            layer_sems.append(s)
            return s

        def kept_sem(name):
            return ctx.enter_context(nc.semaphore(name))

        layer_sems = []

        RING = sb("ring", [P, 2, CHE])
        OV = sb("ov", [P, 4 * CHE])
        X = sb("x_sb", [P, TT, D])
        HT = sb("ht", [P, KT, T])
        MOD = sb("mod", [P, 6, D])
        YA = sb("ya", [P, 2, NH, T])
        F = sb("f_area", [P, 6144])
        TRIG = sb("trig", [P, T])
        CON = sb("con", [P, C_N])
        IDB = sb("ident_bf", [P, P], BF16)
        CMB = sb("causal_bf", [P, P], BF16)
        BC = sb("bc", [P, B_N])
        COLS = sb("cols", [P, R_N])
        MCOL = sb("mod_cols", [P, 2 * KT])
        COND = sb("cond", [P, KT])
        SM = sb("small", [P, 832])
        WDT = sb("w_dt", [P, KT, SH])
        WR = sb("w_router", [P, KT, NG + NE])
        PAY = sb("pay", [P, TT, 2, 4], I32)
        TBL = sb("tbl", [P, NB_MAX, 4], I32)
        EID = sb("eid", [1, 48], I32)
        ROWI = sb("row_idx", [P, 8], U32)
        GIDX = [sb(f"gidx{s}", [P, 1], U32) for s in range(2)]
        SIDX = [sb(f"sidx{s}", [P, 4], U32) for s in range(2)]
        SLOT = [RING[:, 0, :], RING[:, 1, :]] + [OV[:, j * CHE:(j + 1) * CHE] for j in range(4)]

        def ov(at, *shape):
            n = int(np.prod(shape))
            v = OV[:, at:at + n]
            return v if len(shape) == 1 else v.rearrange("p (a b) -> p a b", a=shape[0])

        def fa(at, *shape):
            n = int(np.prod(shape))
            v = F[:, at:at + n]
            return v if len(shape) == 1 else v.rearrange("p (a b) -> p a b", a=shape[0])

        XS, Z, BTOK, BT, CT = ov(0, TT, DI), ov(4096, TT, DI), ov(8192, TT, T), ov(10240, SG, T), ov(12288, SG, T)
        CV = [ov(14336, T), ov(14848, T)]
        SX = [ov(15360, T), ov(15872, T)]
        ST, XW, XD = fa(0, DI), fa(1024, DI), fa(2048, DI)
        MT = [fa(3072, 4, P), fa(3584, 4, P)]
        DQT, DKT = YA[:, 1], ov(14336, NH, T)
        DVT = YA[:, 0]
        CQT, CKVT, KPE, QN, QP, KN, VT = ov(0, 2, T), ov(1024, T), ov(1536, T), ov(2048, NH, T), ov(4096, NH, T), \
            ov(6144, NH, T), ov(8192, TT, T)
        PB = [ov(10240 + 512 * j, T) for j in range(4)]
        PT = ov(12288, TT, T)
        YT1, YT2, JSS = fa(4096, 512), fa(4608, 512), fa(5120, 256)
        ROT = fa(3072, T)
        DIST = fa(0, TT, T)
        SQB, RSB = fa(2048, T), fa(2560, T)
        POSR = fa(5632, T)
        HR = [fa(0, D), fa(1024, D), fa(2048, D)]
        JUNK1 = fa(3072, D)
        H2T, H2R = fa(0, KT, T), [fa(4096, D), fa(5120, D), MOD[:, 1]]
        JUNK2 = MOD[:, 0]
        NW2, SNW = MOD[:, 0], MOD[:, 1]
        def rounded(name, region, first, *shape):
            return nc.alloc_sbuf_tensor_at(name, [P, *shape], F32R, offset=at[region] + 4 * first)

        def at_slot(j):
            return ("ring", j * CHE) if j < 2 else ("ov", (j - 2) * CHE)

        W_L = [rounded(f"w_low{j}", *at_slot(j), CHE) for j in range(6)]
        W_H = [rounded(f"w_high{k}", *(("f_area", 2048 * k) if k < 3 else ("mod", 0)), 2048) for k in range(4)]
        yaf = YA[:, :, :, :].rearrange("p a h t -> p (a h t)")
        htf = HT[:, :, :].rearrange("p k t -> p (k t)")
        HN_H, HN_L = rounded("hn_high", "ya", 0, KT, T), rounded("hn_low", "mod", 2 * D, KT, T)
        IN_H = [rounded(f"in_high{k}", "ov", 4096 + 2048 * k, 2048) for k in range(2)] + W_H[0:2]
        XG, YB = [MOD[:, 2], MOD[:, 3]], [htf[:, 3072:4096], MOD[:, 4]]
        GS, HH = htf[:, 2048:2560], htf[:, 2560:3072]
        XG_H, XG_L = ([rounded(f"x_{part}{s}", "ya", 2048 * s + 1024 * k, KT, P) for s in range(2)]
                      for k, part in enumerate(("high", "low")))
        HH_H, HH_L = ([rounded(f"h_{part}{s}", "ht", 1024 * s + 512 * k, 4, P) for s in range(2)]
                      for k, part in enumerate(("high", "low")))
        CB = [yaf[:, 0:2048], yaf[:, 2048:4096], htf[:, 0:2048], htf[:, 2048:4096]]

        ID, UU, SU, ONE = (CON[:, a:a + P] for a in (C_ID, C_U, C_SU, C_ONE))

        def sm(at, *shape):
            n = int(np.prod(shape))
            v = SM[:, at:at + n]
            if len(shape) == 2:
                v = v.rearrange("p (a b) -> p a b", a=shape[0])
            return v
        SS, MS, RS = sm(0, TT), sm(4, TT), sm(8, TT)
        DTT, ADT, ACS, NACS, EACS, DEND, ETOT, STMP = (sm(16 + 64 * k, TT, SH) for k in range(8))
        ANEG = sm(528, SH)
        MX, NB_, SE, RR = sm(544, 4), sm(548, 4), sm(552, 4), sm(556, 4)
        LAM, LT, SUBW = sm(560, 1), sm(561, 2), sm(563, 1)
        SSG, MSG, RSG = (sm(768 + 16 * k, TT, SG) for k in range(3))
        POSQ = sm(816, TT)
        ACST = F[0:TT * SH, 5376:5504]
        LPR = F[:, 5120:5248]
        ROWS = F[0:R_N, 5504:5632]
        CROW = F[0:KT, 4096:4224]
        RM, RV, RP_, RW, R1, R2, R3, R4 = (sm(576 + 4 * k, TT) for k in range(8))
        GL, GE, PEN = sm(608, TT, NG), sm(624, TT, NG), sm(640, TT, NG)
        EL, LM, OH1, OH2, MM, POS, BLK, TMPE, ROWF = (YA[:, 1, k // 4, 128 * (k % 4):128 * (k % 4) + 128]
                                                      .rearrange("p (t e) -> p t e", t=TT) for k in range(9))
        OVS, OVE = (YA[:, 1, 3, 32 * k:32 * k + 32] for k in range(2))
        OVR = YA[0:32, 1, 3, 128:256]
        OVT = YA[0:32, 1, 3, 256:260]
        NPF = YA[0:1, 1, 3, 264:280]
        KCMP = YA[0:1, 1, 2, 256:512].rearrange("p (k e) -> p k e", k=8)

        PS = [ctx.enter_context(nc.psum_tensor(f"bank{b}", [P, 512], F32)) for b in range(8)]

        s_load = [sem(f"s_load{j}") for j in range(6)]
        s_par = sem("s_par")
        s_bada = sem("s_bada")
        s_mrow = sem("s_mrow")
        s_mcol = sem("s_mcol")
        s_hm = sem("s_hm")
        s_hnl = sem("s_hnl")
        s_late = sem("s_late")
        s_tblini = sem("s_tblini")
        s_acc = sem("s_acc")
        s_accf = [sem("s_accf0"), sem("s_accf1")]
        s_tr = sem("s_tr")
        s_trf = [sem("s_trf0"), sem("s_trf1")]
        s_dch = sem("s_dch")
        s_ach = sem("s_ach")
        s_pch = sem("s_pch")
        s_ss1 = sem("s_ss1")
        s_ms = sem("s_ms")
        s_rs = sem("s_rs")
        s_hr = sem("s_hr")
        s_conv = sem("s_conv")
        s_sx = sem("s_sx")
        s_dt1 = sem("s_dt1")
        s_dt2 = sem("s_dt2")
        s_lam = sem("s_lam")
        s_adt = sem("s_adt")
        s_acs = sem("s_acs")
        s_dec = sem("s_dec")
        s_xw = sem("s_xw")
        s_cb = sem("s_cb")
        s_mx = sem("s_mx")
        s_mt = sem("s_mt")
        s_yd = sem("s_yd")
        s_st = sem("s_st")
        s_ydf = sem("s_ydf")
        s_ste = sem("s_ste")
        s_yn = sem("s_yn")
        s_ssg = sem("s_ssg")
        s_msg = sem("s_msg")
        s_rsg = sem("s_rsg")
        s_ynn = sem("s_ynn")
        s_pos = sem("s_pos")
        s_sc = sem("s_sc")
        s_scf = sem("s_scf")
        s_nb = sem("s_nb")
        s_ex = sem("s_ex")
        s_at = sem("s_at")
        s_tp = sem("s_tp")
        s_pt = sem("s_pt")
        s_pv = sem("s_pv")
        s_sq = sem("s_sq")
        s_rst = sem("s_rst")
        s_ya = sem("s_ya")
        s_csq = sem("s_csq")
        s_crs = sem("s_crs")
        s_cn = sem("s_cn")
        s_kpe = sem("s_kpe")
        s_qpr = sem("s_qpr")
        s_oc = sem("s_oc")
        s_o = sem("s_o")
        s_xr = sem("s_xr")
        s_ss2 = sem("s_ss2")
        s_h2 = sem("s_h2")
        s_h2st = sem("s_h2st")
        s_nt = sem("s_nt")
        s_ntf = sem("s_ntf")
        s_lg = sem("s_lg")
        s_ge = sem("s_ge")
        s_gf = sem("s_gf")
        s_oh = sem("s_oh")
        s_pp = sem("s_pp")
        s_ovt = sem("s_ovt")
        s_ov2 = sem("s_ov2")
        s_eid = sem("s_eid")
        s_row = sem("s_row")
        s_tbl = sem("s_tbl")
        s_xt = sem("s_xt")
        s_xh = sem("s_xh")
        s_xl = sem("s_xl")
        s_unit = sem("s_unit")
        s_hi = sem("s_hi")
        s_lo = sem("s_lo")
        s_hnh = sem("s_hnh")
        s_inh = sem("s_inh")
        s_inl = sem("s_inl")
        s_gs = sem("s_gs")
        s_hh = sem("s_hh")
        s_htp = sem("s_htp")
        s_hth = sem("s_hth")
        s_htl = sem("s_htl")
        s_ye = sem("s_ye")
        s_slot = [sem("s_slot0"), sem("s_slot1")]
        s_all = sem("s_all")
        s_cmb = [sem(f"s_cmb{t}") for t in range(TT)]
        s_gd = [kept_sem("s_gd0"), kept_sem("s_gd1")]
        s_sd = [kept_sem("s_sd0"), kept_sem("s_sd1")]
        s_disp = [kept_sem(f"s_disp{k}") for k in range(8)]
        s_end = kept_sem("s_end")
        s_clr = kept_sem("s_clr")
        s_seq = kept_sem("s_seq")
        s_con = kept_sem("s_con")
        s_x0 = kept_sem("s_x0")
        s_pro = kept_sem("s_pro")
        s_proa = kept_sem("s_proa")
        s_prod = kept_sem("s_prod")
        s_prot = kept_sem("s_prot")
        s_prov = kept_sem("s_prov")
        s_fss = kept_sem("s_fss")
        s_fin = kept_sem("s_fin")
        s_finr = kept_sem("s_finr")
        s_fout = kept_sem("s_fout")
        s_fw = kept_sem("s_fw")
        s_fst = kept_sem("s_fst")
        s_tick = kept_sem("s_tick")

        block = ctx.enter_context(nc.Block())

        N_PAR = 16 * 17

        def acc_bank(name):
            n = ACC[name]
            return PS[n % 2], s_accf[n % 2], n // 2 + 1

        def tr_bank(name):
            n = TRN[name]
            return PS[2 + n % 2], s_trf[n % 2], n // 2 + 1

        def evacuated(eng, name):
            _, free, k = acc_bank(name)
            eng.wait_ge(free, k)

        def turned_out(eng, name):
            _, free, k = tr_bank(name)
            eng.wait_ge(free, k)

        def flat(v):
            return v.rearrange("p a b -> p (a b)")

        def last_group(n):
            name = CHUNKS[n]
            if name == "U":
                return s_acc, ACC[("V", 3)] + 1
            if name[0] == "A":
                return s_acc, ACC[name] + 1
            if name[0] == "O":
                return (s_oc, name[1] + 1) if name[1] < 3 else (s_o, TT)
            j = name[1]
            tile = (("X", 4 * j + 3) if j < 4 else ("Z", 8 * j - 25) if j < 6 else
                    (("DQ", "DK", "DV")[j - 6], 3) if j < 9 else ("C", 3))
            return s_acc, ACC[tile] + 1

        def tiles4(bank):
            return bank[:, :].rearrange("p (k j) -> p k j", k=4)

        def unit_of(buf, v, half=None):
            if half is None:
                return buf[:, :].rearrange("p (k n) -> p k n", k=4)
            if v % UNITS < 8:
                return buf[:, half * 2048:(half + 1) * 2048].rearrange("p (k n) -> p k n", k=4)
            return buf[:, :].rearrange("p (k n) -> p k n", k=4)[:, :, half * CH:(half + 1) * CH]

        def in_half(buf, u):
            return buf[:, :].rearrange("p (k n) -> p k n", k=KT)[:, :, (u % 2) * 256:(u % 2) * 256 + 256]

        def in_place(u):
            return IN_H[u % 2 if u < 8 else 2 + u % 2][:, :].rearrange("p (k n) -> p k n", k=KT)

        def in_slot(u):
            return chunk_slot(CHN[("I", u // 2)])

        def down_bank(v):
            return PS[(5, 6, 7, 5)[v - 8]]

        def more_pairs(eng):
            eng.wait_ge(s_eid, 1)
            return eng.value_load(EID[0:1, 41:42], min_val=15, max_val=PAIRS_MAX - 1)

        def pairs(eng):
            eng.wait_ge(s_eid, 1)
            return eng.value_load(EID[0:1, 40:41], min_val=16, max_val=PAIRS_MAX)

        @block.sync
        def _(sp):
            sp.dma_start(CON[:, :], k_const).then_inc(s_con, 16)
            sp.dma_start(CROW, c.rearrange("a (k p) -> (a k) p", p=P)).then_inc(s_con, 16)
            sp.dma_start(EID[:, :], k_eid).then_inc(s_con, 16)
            sp.dma_start(PAY[:, :, :, :].rearrange("p t s w -> p (t s w)"), k_pay).then_inc(s_con, 16)
            sp.dma_start(SM[:, 0:512].bitcast(I32), positions.partition_broadcast(P)).then_inc(s_con, 16)
            sp.dma_start(X[:, :, :], x.rearrange("a (t p) d -> p (a t) d", p=P)).then_inc(s_x0, 16)
            sp.wait_ge(s_prod, 1)

            with sp.Fori(0, L) as l:
                def rows(w, o, n):
                    return w[bass.ds(l, 1), :, o:o + n].rearrange("a (k p) n -> p (a k) n", p=P)

                def load_chunk(n):
                    name, dst, landed = CHUNKS[n], SLOT[chunk_slot(n)], s_load[chunk_slot(n)]
                    if n >= 6:
                        sp.wait_ge(*last_group(n - 2))
                    tiles = dst.rearrange("p (k n) -> p k n", k=KT)
                    if name[0] == "A":
                        sp.dma_start(tiles, rows(w_ada, name[1] * CH, CH)).then_inc(landed, 16)
                    elif name == ("I", 9):
                        for a, b, o in ((0, 448, 0), (448, 480, 416), (480, 512, 384)):
                            sp.dma_start(tiles[:, :, a:b], rows(w_in, o, b - a)).then_inc(landed, 16)
                    elif name[0] == "I":
                        sp.dma_start(tiles, rows(w_in, IN_COLS[name[1]], CH)).then_inc(landed, 16)
                    elif name == "U":
                        uq = dst[:, 0:2048].rearrange("p (k h n) -> p k h n", k=2, h=NH)
                        for k in range(2):
                            src = mla_w_uq[bass.ds(l, 1), k * P:(k + 1) * P, :].rearrange("a p (h n) -> (a p) h n", h=NH)
                            for a, b, o in ((0, 192, 0), (192, 224, 160), (224, 256, 128)):
                                sp.dma_start(uq[:, k, :, a:b], src[:, :, o:o + b - a]).then_inc(landed, 16)
                        sp.dma_start(dst[:, 2048:3072],
                                     mla_w_ukv[bass.ds(l, 1)].rearrange("a p n -> (a p) n")).then_inc(landed, 16)
                    else:
                        j = name[1]
                        sp.dma_start(dst.rearrange("p (f n) -> p f n", f=4),
                                     w_out[bass.ds(l, 1), j * 512:(j + 1) * 512, :]
                                     .rearrange("a (f p) n -> p (a f) n", p=P)).then_inc(landed, 16)

                small = [(ROWS[R_NW1:R_NW1 + 8, :], norm1_w[bass.ds(l, 1)].rearrange("a (m p) -> (a m) p", p=P)),
                         (ROWS[R_BADA:R_BADA + 16, :], b_ada[bass.ds(l, 1), 0:2 * D].rearrange("a (m p) -> (a m) p", p=P)),
                         (ROWS[R_CW:R_CW + 64, :], ssd_conv_w[bass.ds(l, 1)].rearrange("a k (m p) -> (a k m) p", p=P)),
                         (ROWS[R_CB:R_CB + 16, :], ssd_conv_b[bass.ds(l, 1)].rearrange("a (m p) -> (a m) p", p=P)),
                         (ROWS[R_QN:R_QN + 2, :], mla_q_norm_w[bass.ds(l, 1)].rearrange("a (m p) -> (a m) p", p=P)),
                         (ROWS[R_KN:R_KN + 1, :], mla_kv_norm_w[bass.ds(l, 1)]),
                         (ROWS[R_SUB:R_SUB + 1, :], diff_subln_w[bass.ds(l, 1)]),
                         (BC[:, B_LAM:B_LAM + 256], diff_lambda[bass.ds(l, 1)].rearrange("a k d -> a (k d)").partition_broadcast(P)),
                         (WDT[:, :, :], rows(w_in, O_DT, SH)),
                         (WR[:, :, 0:NG], rows(router_w_group, 0, NG)),
                         (WR[:, :, NG:], rows(router_w_expert, 0, NE))]
                for at, n, w in ((B_DTB, SH, ssd_dt_bias), (B_ALOG, SH, ssd_a_log), (B_D, SH, ssd_d),
                                 (B_RB, NG, router_b_group), (B_RB + NG, NE, router_b_expert), (B_LI, 2, k_lam)):
                    small.append((BC[:, at:at + n], w[bass.ds(l, 1)].partition_broadcast(P)))
                assert 16 * len(small) == N_PAR
                load_chunk(0)
                for dst, src in small:
                    sp.dma_start(dst, src).then_inc(s_par, 16)
                def load_bias(a, b):
                    sp.dma_start(MOD[:, a:b, :].rearrange("p a n -> p (a n)"),
                                 b_ada[bass.ds(l, 1), a * D:b * D].partition_broadcast(P)).then_inc(s_bada, 16)

                for n in range(1, 6):
                    load_chunk(n)
                sp.dma_start(POSR.bitcast(I32), positions.partition_broadcast(P)).then_inc(s_pos, 16)
                sp.dma_start(TBL[:, :, :].rearrange("p k w -> p (k w)"), k_table).then_inc(s_tblini, 16)
                sp.wait_ge(s_tblini, 16)
                sp.dma_start(slot_table.rearrange("(p k) w -> p (k w)", p=P),
                             TBL[:, :, :].rearrange("p k w -> p (k w)")).then_inc(s_tblini, 16)
                for n in range(6, 8):
                    load_chunk(n)
                sp.wait_ge(s_mcol, 4)
                sp.dma_start(NW2, norm2_w[bass.ds(l, 1)].partition_broadcast(P)).then_inc(s_late, 16)
                sp.dma_start(SNW, ssd_norm_w[bass.ds(l, 1)].partition_broadcast(P)).then_inc(s_late, 16)
                for n in range(8, NCH):
                    load_chunk(n)
                    if n == CHN[("I", 7)]:
                        load_bias(2, 6)

                def load_expert(m, e):
                    slot, kind = (m + 2) % 6, (0, 1, 0, 1, 2, 2)[m]
                    w = (exp_w_gate, exp_w_up, exp_w_down)[kind][bass.ds(l, 1), bass.ds(e, 1)]
                    sp.dma_start(SLOT[slot].rearrange("p (k n) -> p k n", k=4 if kind == 2 else KT),
                                 w.rearrange("a b (k p) n -> p (a b k) n", p=P)).then_inc(s_load[slot], 16)

                sp.wait_ge(s_ya, 2 * NH)
                for m in range(4):
                    load_expert(m, (0, 0, 1, 1)[m])
                for t in range(TT):
                    sp.wait_ge(s_h2, t + 1)
                    sp.dma_start(h2_rows[t * P:(t + 1) * P, :], H2R[t % 3]).then_inc(s_h2st, 16)
                    sp.wait_ge(s_h2st, 16 * (t + 1))
                for m in (4, 5):
                    sp.wait_ge(*last_group(NCH - 1 if m == 4 else NCH - 2))
                    load_expert(m, m - 4)
                for q in s_disp:
                    sp.wait_ge(q, 16)
                sp.dma_start(TBL[:, :, :].rearrange("p k w -> p (k w)"),
                             slot_table.rearrange("(p k) w -> p (k w)", p=P)).then_inc(s_tbl, 16)
                more = more_pairs(sp)
                with sp.Fori(0, more) as i:
                    e = [sp.value_load(EID[0:1, bass.ds(i * 2 + (2 + s), 1)], min_val=0, max_val=NE - 1) for s in range(2)]
                    for m in range(6):
                        s = (0, 0, 1, 1, 0, 1)[m]
                        sp.wait_ge(s_unit, i * UNITS + (2 * m + 2))
                        load_expert(m, e[s])
                sp.wait_ge(s_all, 1)
                for t in range(TT):
                    sp.dma_start(CB[t], expert_rows[t * 2 * P:(t + 1) * 2 * P, :].rearrange("(p s) d -> p (s d)", s=2)).then_inc(s_cmb[t], 16)
                sp.sem_inc(s_end, 1)
                sp.wait_ge(s_end, l * 5 + 5)
                sp.sem_inc(s_seq, 1)
                for q in layer_sems:
                    sp.sem_clear(q)
                sp.sem_inc(s_clr, 1)
            sp.dma_start(MOD[:, 0], final_norm_w.rearrange("(a d) -> a d", a=1).partition_broadcast(P)).then_inc(s_fw, 16)
            for t in range(TT):
                sp.wait_ge(s_fout, t + 1)
                sp.dma_start(out[0, t * P:(t + 1) * P, :], X[:, t, :]).then_inc(s_fst, 16)
            sp.wait_ge(s_fst, 16 * TT)

        @block.gpsimd
        def _(pool):
            pool.wait_ge(s_con, 80)
            half = CON[:, C_HALF:C_HALF + 1]

            def rstd(dst, src, n, done):
                pool.tensor_tensor(dst, src, half.broadcast_to([P, n]), ALU.pow).then_inc(done, 1)

            with pool.Fori(0, L) as l:
                pool.wait_ge(s_ms, 1)
                rstd(RS, MS, TT, s_rs)
                for cc in range(TT):
                    pool.wait_ge(s_msg, cc + 1)
                    rstd(RSG[:, cc, :], MSG[:, cc, :], SG, s_rsg)
                for t in range(TT):
                    pool.wait_ge(s_ms, t + 2)
                    rstd(RS[:, t:t + 1], MS[:, t:t + 1], 1, s_rs)
                pool.wait_ge(s_tblini, 32)
                pool.wait_ge(s_oh, 1)
                for s in range(2):
                    pool.memset(XG[s], 0.0).then_inc(s_pch, 1)
                pool.wait_ge(s_pch, 2)
                pool.wait_ge(s_row, 1)
                for t in range(TT):
                    for s in range(2):
                        k = 2 * t + s
                        pool.indirect_dma_start(slot_table, bass.IndirectOffsetOnAxis(ap=ROWI[:, k:k + 1], axis=0), PAY[:, t, s, :], None,
                                                bounds_check=P * NB_MAX - 1, oob_is_err=False).then_inc(s_disp[k], 16)
                pool.wait_ge(s_tbl, 16)
                pool.wait_ge(s_h2st, 16 * TT)

                def gather(s):
                    pool.indirect_dma_start(XG[s], None, h2_rows, bass.IndirectOffsetOnAxis(ap=GIDX[s][:, 0:1], axis=0),
                                            bounds_check=T - 1, oob_is_err=False).then_inc(s_gd[s], 16)

                for s in range(2):
                    pool.tensor_copy(GIDX[s][:, :], TBL[:, s, 0:1].bitcast(U32)).then_inc(s_pch, 1)
                    pool.tensor_copy(SIDX[s][:, 0:3], TBL[:, s, 0:3].bitcast(U32)).then_inc(s_slot[s], 1)
                for s in range(2):
                    pool.wait_ge(s_pch, 3 + s)
                    gather(s)
                more = more_pairs(pool)

                def after(q, value):
                    pool.wait_ge(q, value)
                    pool.sem_inc(s_tick, 1)

                def gather_next(s, col, count):
                    pool.tensor_copy(GIDX[s][:, :], TBL[:, bass.ds(col, 1), 0:1].rearrange("p a b -> p (a b)").bitcast(U32)).then_inc(s_pch, 1)
                    after(s_pch, count + 1)
                    gather(s)

                def scatter(i, s):
                    after(s_ye, i * 4 + (2 * s + 3))
                    pool.indirect_dma_start(expert_rows, bass.IndirectOffsetOnAxis(ap=SIDX[s][:, 1:2], axis=0), YB[s], None,
                                            bounds_check=2 * T - 1, oob_is_err=False).then_inc(s_sd[s], 16)

                for s in range(2):
                    pool.wait_ge(s_xt, s + 1)
                    pool.tensor_copy(GIDX[s][:, :], TBL[:, 2 + s, 0:1].bitcast(U32)).then_inc(s_pch, 1)
                    pool.wait_ge(s_pch, 5 + s)
                    gather(s)
                with pool.Fori(0, more) as i:
                    after(s_xt, i * 2 + 3)
                    gather_next(0, i * 2 + 4, i * 2 + 6)
                    scatter(i, 0)
                    scatter(i, 1)
                    after(s_xt, i * 2 + 4)
                    gather_next(1, i * 2 + 5, i * 2 + 7)
                    for s in range(2):
                        after(s_sd[s], i * 16 + 16)
                        pool.tensor_copy(SIDX[s][:, 0:3], TBL[:, bass.ds(i * 2 + (2 + s), 1), 0:3]
                                         .rearrange("p a b -> p (a b)").bitcast(U32)).then_inc(s_slot[s], 1)
                for s in range(2):
                    after(s_slot[s], more + 1)
                    scatter(more, s)
                for s in range(2):
                    after(s_sd[s], more * 16 + 16)
                    after(s_gd[s], more * 16 + 32)
                pool.sem_inc(s_all, 1)
                for q in (*s_gd, *s_sd, *s_disp):
                    pool.dma_reset(range(q.num, q.num + 1))
                    pool.sem_clear(q)
                pool.sem_inc(s_end, 1)
                after(s_clr, l + 1)
            pool.wait_ge(s_fin, 1)
            rstd(RS, MS, TT, s_finr)

        @block.scalar
        def _(act):
            act.wait_ge(s_pro, 1)
            act.activation(COND[:, :], PS[2][:, 0:KT], ACT.Silu).then_inc(s_proa, 1)
            act.wait_ge(s_prod, 1)
            act.activation(TRIG[:, :], TRIG[:, :], ACT.Sin).then_inc(s_proa, 1)

            with act.Fori(0, L) as l:
                chain = [0]

                def link(ins):
                    chain[0] += 1
                    ins.then_inc(s_ach, 1)
                    act.wait_ge(s_ach, chain[0])

                def acc_ready(name):
                    act.wait_ge(s_acc, ACC[name] + 1)
                    return acc_bank(name)

                def tr_ready(name):
                    act.wait_ge(s_tr, TRN[name] + 1)
                    return tr_bank(name)

                act.wait_ge(s_x0, 16)
                for t in range(TT):
                    link(act.activation(JUNK1, X[:, t, :], ACT.Square, accum_out=SS[:, t:t + 1]))
                act.sem_inc(s_ss1, 1)
                for t in range(TT):
                    for q in range(2):
                        bank, free, _ = tr_ready(("H", t, q))
                        act.activation(HT[:, 4 * q:4 * q + 4, t * P:(t + 1) * P], tiles4(bank), ACT.Copy).then_inc(free, 1)
                bank, free, _ = tr_ready("P")
                act.activation(COLS[:, :], bank[:, 0:R_N], ACT.Copy).then_inc(free, 1)
                for j in range(4):
                    bank, free, k = acc_ready(("A", j))
                    act.activation(MOD[:, j // 2, (j % 2) * CH:(j % 2 + 1) * CH], bank[:, :], ACT.Copy).then_inc(free, 1)
                    act.wait_ge(free, k)
                    act.sem_inc(s_mrow, 1)

                def in_high(u):
                    if u % 2 == 0:
                        n = CHN[("I", u // 2)]
                        act.wait_ge(s_load[chunk_slot(n)], slot_count(n))
                    if u >= 2 and u != 8 and u != 9:
                        act.wait_ge(s_acc, ACC[IN_UNITS[u - 2]] + 1)
                    act.activation(in_place(u), in_half(SLOT[in_slot(u)], u), ACT.Copy).then_inc(s_inh, 1)

                in_high(0)
                for k in range(KT):
                    act.wait_ge(s_hm, k + 1)
                    act.activation(HN_H[:, k, :], HT[:, k, :], ACT.Copy).then_inc(s_hnh, 1)
                in_high(1)
                for m in range(16):
                    if 1 <= m <= 12:
                        bank, free, _ = tr_ready(("T", m - 1))
                        dst = XS[:, :, (m - 1) * P:m * P] if m <= 8 else BTOK[:, :, (m - 9) * P:(m - 8) * P]
                        act.activation(dst, bank[:, :].rearrange("p (t n) -> p t n", t=TT), ACT.Copy).then_inc(free, 1)
                    act.wait_ge(s_conv, m + 1)
                    dst = SX[m % 2] if m < 8 else (BT, CT)[m // 12][:, m % 4, :]
                    act.activation(dst, CV[m % 2], ACT.Silu).then_inc(s_sx, 1)
                    if m % 2:
                        in_high(m // 2 + 2)
                for m in range(16):
                    bank, free, _ = acc_ready(("Z", m))
                    act.activation(Z[:, m % 4, (m // 4) * 256:(m // 4 + 1) * 256], bank[:, 0:256], ACT.Silu).then_inc(free, 1)
                    if m in (3, 7):
                        in_high(m // 4 + 10)
                act.preload_act_table_set("natural_log_exp_and_others")
                act.wait_ge(s_dt1, 1)
                act.activation(ANEG, BC[:, B_ALOG:B_ALOG + SH], ACT.Exp)
                link(act.activation(flat(ACS), flat(DTT), ACT.Abs))
                link(act.activation(flat(NACS), flat(ACS), ACT.Exp, scale=-1.0))
                act.activation(flat(EACS), flat(NACS), ACT.Ln, bias=1.0).then_inc(s_dt2, 1)
                act.wait_ge(s_lam, 1)
                act.activation(LT, LT, ACT.Exp).then_inc(s_dt2, 1)
                act.wait_ge(s_acs, 1)
                act.activation(flat(EACS), flat(ACS), ACT.Exp)
                act.activation(flat(DEND), flat(STMP), ACT.Exp)
                act.activation(flat(ETOT), flat(ETOT), ACT.Exp).then_inc(s_dec, 1)
                bank, free, _ = tr_ready("AT")
                act.activation(ACST, bank[0:TT * SH, 0:P], ACT.Copy).then_inc(free, 1)

                def squares(cc, hf):
                    act.wait_ge(s_yn, 2 * cc + hf + 1)
                    for q in range(2):
                        g = 2 * hf + q
                        link(act.activation(JSS, Z[:, cc, 256 * g:256 * g + 256], ACT.Square, accum_out=SSG[:, cc, g:g + 1]))
                    act.sem_inc(s_ssg, 1)

                def fill_out(k):
                    name, m = SSD_FILL[k]
                    bank, free, _ = acc_ready((name, m))
                    act.activation({"DQ": DQT, "DK": DKT, "DV": DVT}[name][:, m, :], bank[:, :], ACT.Copy).then_inc(free, 1)

                for cc in range(TT):
                    for g in range(SG):
                        n = 4 * cc + g
                        bank, free, k = acc_ready(("R", cc, g))
                        if n >= 2:
                            act.wait_ge(s_yd, n - 1)
                        for h in range(4):
                            ins = act.activation(MT[g % 2][:, h, :], bank[:, h * P:(h + 1) * P], ACT.Exp,
                                                 bias=NACS[:, cc, 4 * g + h:4 * g + h + 1])
                        ins.then_inc(free, 1)
                        act.wait_ge(free, k)
                        act.sem_inc(s_mx, 1)
                        if g in (1, 3):
                            fill_out(3 * cc + g // 2)
                        if n >= 2 and g == 3:
                            squares(cc, 0)
                        if cc >= 1 and g == 1:
                            squares(cc - 1, 1)
                    fill_out(3 * cc + 2)
                squares(TT - 1, 1)

                def exps(base, u, width, scale):
                    for m in range(width):
                        b, n = (width * u + m) % 4, (u % 4 + 1) * P
                        act.wait_ge(s_nb, base + width * u + m + 1)
                        link(act.activation(PB[b][:, 0:n], PB[b][:, 0:n], ACT.Exp, bias=NB_[:, b:b + 1], scale=scale,
                                            accum_out=SE[:, b:b + 1]))
                        act.sem_inc(s_ex, 1)

                def turned(k):
                    i = k % 4
                    act.wait_ge(s_tp, k + 1)
                    if i == 0 and k >= 4:
                        act.wait_ge(s_pv, k // 4)
                    act.activation(PT[:, 0:i + 1, i * P:(i + 1) * P],
                                   PS[6][:, 0:(i + 1) * P].rearrange("p (j q) -> p j q", j=i + 1), ACT.Copy).then_inc(s_pt, 1)

                def rms_rows(name, n, eps, done):
                    bank, free, k = acc_ready(name)
                    act.activation(RSB, bank[:, :], ACT.Ln, scale=1.0 / n, bias=eps).then_inc(free, 1)
                    act.wait_ge(free, k)
                    act.activation(RSB, RSB, ACT.Exp, scale=-0.5).then_inc(done, 1)

                for u in range(18):
                    if u < 16:
                        exps(0, u, 2, DIFF_SCALE)
                    if u >= 2:
                        turned(u - 2)
                        if u % 4 == 1:
                            h = (u - 2) // 4
                            act.wait_ge(s_pv, h + 1)
                            act.activation(SQB, PS[7][:, :], ACT.Square).then_inc(s_sq, 1)
                            if h >= 1:
                                act.wait_ge(s_ya, h)
                            rms_rows(("DS", h), DV, SUBEPS, s_rst)
                act.wait_ge(s_ya, NH)
                for m, dst in ((0, SQB), (1, PB[0])):
                    evacuated(act, ("C", m))
                    act.activation(dst, CQT[:, m, :], ACT.Square).then_inc(s_csq, 1)
                rms_rows("SQ", MQ, EPS, s_crs)
                evacuated(act, ("C", 2))
                act.activation(SQB, CKVT, ACT.Square).then_inc(s_csq, 1)
                act.wait_ge(s_cn, 1)
                rms_rows("SK", MKV, EPS, s_crs)
                for cc in range(TT):
                    for q in range(2):
                        bank, free, _ = tr_ready(("Y", cc, q))
                        act.activation(HT[:, 4 * q:4 * q + 4, cc * P:(cc + 1) * P],
                                       bank[:, :].rearrange("p (k t) -> p k t", k=4), ACT.Copy).then_inc(free, 1)
                for name, dst in (("QN", QN), ("KN", KN), ("V", VT)):
                    for m in range(4):
                        bank, free, _ = acc_ready((name, m))
                        act.activation(dst[:, m, :], bank[:, :], ACT.Copy).then_inc(free, 1)
                for u in range(18):
                    if u < 16:
                        exps(32, u, 1, MLA_SCALE)
                    if u >= 2:
                        turned(16 + u - 2)
                def feature_major2(t):
                    act.wait_ge(s_nt, t + 1)
                    for q in range(2):
                        ins = act.activation(H2T[:, 4 * q:4 * q + 4, t * P:(t + 1) * P],
                                             PS[2 * t + q][:, :].rearrange("p (k t) -> p k t", k=4), ACT.Copy)
                    ins.then_inc(s_ntf, 1)

                for t in range(TT):
                    act.wait_ge(s_xr, t + 1)
                    link(act.activation(JUNK2, X[:, t, :], ACT.Square, accum_out=SS[:, t:t + 1]))
                    act.sem_inc(s_ss2, 1)
                    if t >= 1:
                        feature_major2(t - 1)
                feature_major2(TT - 1)
                act.wait_ge(s_ge, 1)
                act.activation(flat(GE), flat(GE), ACT.Exp).then_inc(s_gf, 1)
                act.wait_ge(s_ge, 2)
                act.activation(RW, RW, ACT.Exp).then_inc(s_gf, 1)
                more = more_pairs(act)

                def high(i, v):
                    slot, half, kind = unit_matrix(v % UNITS)
                    if half == 0:
                        act.wait_ge(s_load[slot], i * 16 + (SLOT_BASE[slot] + 16 * (1 + v // UNITS)))
                    if v >= 4:
                        act.wait_ge(s_unit, i * UNITS + (v - 3))
                    act.activation(unit_of(W_H[v % 4], v), unit_of(SLOT[slot], v, half), ACT.Copy).then_inc(s_hi, 1)

                def rows_high(s, count):
                    act.wait_ge(s_xt, count)
                    act.activation(XG_H[s][:, 0:4, :], tiles4(PS[0]), ACT.Copy)
                    act.activation(XG_H[s][:, 4:8, :], tiles4(PS[1]), ACT.Copy).then_inc(s_xh, 1)

                def hidden_high(s, count):
                    act.wait_ge(s_htp, count)
                    act.activation(HH_H[s][:, :, :], tiles4(PS[4]), ACT.Copy).then_inc(s_hth, 1)

                def gate(i, s):
                    act.wait_ge(s_unit, i * UNITS + (4 * s + 2))
                    act.activation(GS, PS[2][:, :], ACT.Silu).then_inc(s_gs, 1)

                def pair(i, ahead):
                    high(i, 4)
                    gate(i, 0)
                    rows_high(1, i * 2 + 2)
                    for v in (5, 6, 7, 8):
                        high(i, v)
                    hidden_high(0, i * 2 + 1)
                    gate(i, 1)
                    for v in (9, 10, 11):
                        high(i, v)
                    hidden_high(1, i * 2 + 2)
                    if ahead:
                        high(i, 12)
                        rows_high(0, i * 2 + 3)
                        for v in (13, 14, 15):
                            high(i, v)

                act.wait_ge(s_h2st, 16 * TT)
                for v in range(4):
                    high(0, v)
                rows_high(0, 1)
                with act.Fori(0, more) as i:
                    pair(i, True)
                pair(more, False)
                act.sem_inc(s_end, 1)
                act.wait_ge(s_clr, l + 1)
                act.sem_inc(s_seq, 1)
            act.wait_ge(s_fss, 1)
            for t in range(TT):
                if t:
                    act.wait_ge(s_prot, t)
                act.activation(F[:, 0:D], X[:, t, :], ACT.Square, accum_out=SS[:, t:t + 1]).then_inc(s_prot, 1)

        @block.vector
        def _(dve):
            own = [0]

            def olink(ins):
                own[0] += 1
                ins.then_inc(s_prov, 1)
                dve.wait_ge(s_prov, own[0])

            dve.wait_ge(s_con, 80)
            dve.tensor_copy(IDB[:, :], ID)
            dve.tensor_scalar(CMB[:, :], UU, -1.0, -NEG, ALU.add, ALU.mult)
            angle, turns, posf = F[:, 0:T], F[:, T:2 * T], F[:, 2 * T:3 * T]
            olink(dve.tensor_copy(posf, SM[:, 0:512].bitcast(I32)))
            for t in range(TT):
                dve.tensor_tensor(F[:, 3 * T + t * P:3 * T + (t + 1) * P], posf[:, t * P:(t + 1) * P], ID, ALU.mult)
            olink(dve.tensor_scalar(angle, posf, CON[:, C_INV:C_INV + 1], None, ALU.mult))
            dve.tensor_reduce(POSQ, F[:, 3 * T:4 * T].rearrange("p (t q) -> p t q", t=TT), AX, ALU.add)
            olink(dve.tensor_scalar(turns, angle, 1.0 / (2 * math.pi), CON[:, C_PH:C_PH + 1], ALU.mult, ALU.add))
            olink(dve.tensor_scalar(turns, turns, 12582912.0, None, ALU.add))
            olink(dve.tensor_scalar(turns, turns, -12582912.0, None, ALU.add))
            c1 = 6.28125
            c2 = float(np.float32(np.round((2 * math.pi - c1) * 2 ** 22) / 2 ** 22))
            c3 = 2 * math.pi - c1 - c2
            for part in (c1, c2, c3):
                olink(dve.scalar_tensor_tensor(angle, turns, -part, angle, ALU.mult, ALU.add))
            olink(dve.tensor_scalar(turns[:, 0:1], CON[:, C_PH:C_PH + 1], 2 * math.pi, None, ALU.mult))
            olink(dve.tensor_scalar(angle, angle, turns[:, 0:1], 3.1415925, ALU.add, ALU.min))
            olink(dve.tensor_scalar(TRIG[:, :], angle, -3.1415925, None, ALU.max))
            dve.sem_inc(s_prod, 1)

            with dve.Fori(0, L) as l:
                chain = [0]

                def link(ins):
                    chain[0] += 1
                    ins.then_inc(s_dch, 1)
                    dve.wait_ge(s_dch, chain[0])

                def signal(ins, q, n=1):
                    link(ins)
                    dve.sem_inc(q, n)

                def acc_ready(name):
                    dve.wait_ge(s_acc, ACC[name] + 1)
                    return acc_bank(name)

                dve.wait_ge(s_ss1, 1)
                signal(dve.tensor_scalar(MS, SS, 1.0 / D, EPS, ALU.mult, ALU.add), s_ms)
                dve.wait_ge(s_rs, 1)
                for t in range(TT):
                    if t == 3:
                        dve.wait_ge(s_tr, TRN[("H", 0, 1)] + 1)
                    signal(dve.tensor_scalar(HR[t % 3], X[:, t, :], RS[:, t:t + 1], None, ALU.mult), s_hr)

                def ada_row(j):
                    bank, free, _ = acc_ready(("A", j))
                    row = MOD[:, j // 2, (j % 2) * CH:(j % 2 + 1) * CH]
                    signal(dve.tensor_tensor(row, bank[:, :], row, ALU.add), free)

                def in_low(u):
                    dve.wait_ge(s_inh, u + 1)
                    dve.tensor_tensor(in_half(W_L[in_slot(u)], u), in_half(SLOT[in_slot(u)], u), in_place(u).bitcast(F32),
                                      ALU.subtract).then_inc(s_inl, 1)

                turned_out(dve, "P")
                turned_out(dve, ("H", 3, 0))
                turned_out(dve, ("H", 3, 1))
                dve.wait_ge(s_mcol, 4)
                link(dve.tensor_tensor(MCOL[:, :], PS[4][:, 0:2 * KT], COLS[:, R_BADA:R_BADA + 2 * KT], ALU.add))
                shift, scale = MCOL[:, 0:KT], MCOL[:, KT:2 * KT]
                link(dve.scalar_tensor_tensor(scale, scale, 1.0, COLS[:, R_NW1:R_NW1 + KT], ALU.add, ALU.mult))

                def normed_low(k):
                    dve.wait_ge(s_hnh, k + 1)
                    dve.tensor_tensor(HN_L[:, k, :], HT[:, k, :], HN_H[:, k, :].bitcast(F32), ALU.subtract).then_inc(s_hnl, 1)

                for k in range(KT):
                    signal(dve.tensor_scalar(HT[:, k, :], HT[:, k, :], scale[:, k:k + 1], shift[:, k:k + 1], ALU.mult, ALU.add), s_hm)
                    if k == 1:
                        in_low(0)
                    if k:
                        normed_low(k - 1)
                normed_low(KT - 1)
                in_low(1)
                lam = BC[:, B_LAM:B_LAM + 256]
                for k in range(2):
                    link(dve.tensor_tensor(LPR[:, 64 * k:64 * k + 64], lam[:, 128 * k:128 * k + 64], lam[:, 128 * k + 64:128 * k + 128], ALU.mult))
                signal(dve.tensor_reduce(LT, LPR.rearrange("p (k d) -> p k d", k=2), AX, ALU.add), s_lam)
                for m in range(16):
                    bank, free, _ = acc_ready(("X", m))
                    if m >= 2:
                        dve.wait_ge(s_sx, m - 1)
                    w = lambda k: COLS[:, R_CW + 16 * k + m:R_CW + 16 * k + m + 1]
                    link(dve.tensor_scalar(CV[m % 2], bank[:, :], w(SC - 1), COLS[:, R_CB + m:R_CB + m + 1], ALU.mult, ALU.add))
                    for back in range(1, SC):
                        ins = dve.scalar_tensor_tensor(CV[m % 2][:, back:], bank[:, 0:T - back], w(SC - 1 - back), CV[m % 2][:, back:],
                                                       ALU.mult, ALU.add)
                        link(ins)
                    dve.sem_inc(free, 1)
                    dve.sem_inc(s_conv, 1)
                    if m % 2 == 0:
                        if m:
                            in_low(m // 2 + 1)
                in_low(9)
                in_low(10)
                in_low(11)
                def per_chunk(v):
                    return v.rearrange("p (a h) -> p a h", a=1).broadcast_to([P, TT, SH])

                bank, free, _ = acc_ready("DT")
                signal(dve.tensor_tensor(DTT, bank[:, 0:TT * SH].rearrange("p (t h) -> p t h", t=TT), per_chunk(BC[:, B_DTB:B_DTB + SH]), ALU.add), free)
                dve.sem_inc(s_dt1, 1)
                dve.wait_ge(s_dt2, 1)
                link(dve.scalar_tensor_tensor(flat(DTT), flat(DTT), 0.0, flat(EACS), ALU.max, ALU.add))
                signal(dve.scalar_tensor_tensor(ADT, DTT, -1.0, per_chunk(ANEG), ALU.mult, ALU.mult), s_adt)
                dve.wait_ge(s_dt2, 2)
                link(dve.tensor_tensor(LAM, LT[:, 0:1], LT[:, 1:2], ALU.subtract))
                link(dve.tensor_tensor(LAM, LAM, BC[:, B_LI:B_LI + 1], ALU.add))
                link(dve.tensor_tensor(SUBW, COLS[:, R_SUB:R_SUB + 1], BC[:, B_LI + 1:B_LI + 2], ALU.mult))
                bank, free, _ = acc_ready("AC")
                cs, tot = bank[:, 0:TT * SH], bank[:, TT * SH:2 * TT * SH]
                link(dve.tensor_copy(flat(ACS), cs))
                dve.tensor_scalar(flat(NACS), cs, -1.0, None, ALU.mult)
                dve.tensor_tensor(flat(STMP), tot, flat(ACS), ALU.subtract)
                signal(dve.tensor_copy(flat(ETOT), tot), free)
                dve.sem_inc(s_acs, 1)
                dve.wait_ge(s_dec, 1)
                turned_out(dve, ("T", 10))
                turned_out(dve, ("T", 11))
                dve.wait_ge(s_late, 32)

                def heads(v, n=SH):
                    return v.rearrange("p (h d) -> p h d", h=n)

                def each(v, n):
                    return v.rearrange("p (h a) -> p h a", a=1).broadcast_to([P, n, SP_])

                def norm_chunk(cc):
                    dve.wait_ge(s_ssg, 2 * cc + 2)
                    signal(dve.tensor_scalar(MSG[:, cc, :], SSG[:, cc, :], 1.0 / 256, EPS, ALU.mult, ALU.add), s_msg)
                    dve.wait_ge(s_rsg, cc + 1)
                    for g in range(SG):
                        zg = Z[:, cc, 256 * g:256 * g + 256]
                        ins = dve.scalar_tensor_tensor(zg, zg, RSG[:, cc, g:g + 1], SNW[:, 256 * g:256 * g + 256], ALU.mult, ALU.mult)
                    signal(ins, s_ynn)

                for cc in range(TT):
                    if cc >= 1:
                        dve.wait_ge(s_st, 2 * cc)
                    link(dve.tensor_tensor(heads(XW), heads(XS[:, cc, :]), each(DTT[:, cc, :], SH), ALU.mult))
                    if cc < TT - 1:
                        link(dve.tensor_tensor(heads(XD), heads(XW), each(DEND[:, cc, :], SH), ALU.mult))
                    dve.sem_inc(s_xw, 1)
                    for g in range(SG):
                        dve.wait_ge(s_cb, cc + 1)
                        dve.wait_ge(s_mx, 4 * cc + g + 1)
                        cb = PS[4][:, g * P:(g + 1) * P].rearrange("p (a l) -> p a l", a=1).broadcast_to([P, 4, P])
                        signal(dve.tensor_tensor(MT[g % 2], MT[g % 2], cb, ALU.mult), s_mt)
                        if g % 2 == 0:
                            continue
                        hf, hs = g // 2, slice(8 * (g // 2), 8 * (g // 2) + 8)
                        cols = slice(512 * hf, 512 * hf + 512)
                        link(dve.tensor_tensor(heads(YT2, 8), heads(XS[:, cc, cols], 8), each(BC[:, B_D + 8 * hf:B_D + 8 * hf + 8], 8), ALU.mult))
                        dve.wait_ge(s_st, 2 * cc + hf + 1)
                        if cc:
                            link(dve.tensor_tensor(heads(YT1, 8), heads(PS[6][:, :], 8), each(EACS[:, cc, hs], 8), ALU.mult))
                            link(dve.tensor_tensor(YT1, YT1, PS[5][:, :], ALU.add))
                        else:
                            link(dve.tensor_copy(YT1, PS[5][:, :]))
                        dve.sem_inc(s_ydf, 1)
                        link(dve.tensor_tensor(YT1, YT1, YT2, ALU.add))
                        signal(dve.tensor_tensor(Z[:, cc, cols], YT1, Z[:, cc, cols], ALU.mult), s_yn)
                        if cc < TT - 1:
                            if cc:
                                link(dve.tensor_tensor(heads(ST[:, cols], 8), heads(ST[:, cols], 8), each(ETOT[:, cc, hs], 8), ALU.mult))
                                link(dve.tensor_tensor(ST[:, cols], ST[:, cols], PS[7][:, :], ALU.add))
                            else:
                                link(dve.tensor_copy(ST[:, cols], PS[7][:, :]))
                            dve.sem_inc(s_ste, 1)
                        if hf == 0 and cc >= 1:
                            norm_chunk(cc - 1)
                norm_chunk(TT - 1)

                dve.wait_ge(s_pos, 16)
                posf = PB[1]
                link(dve.tensor_copy(posf, POSR.bitcast(I32)))
                for i in range(TT):
                    n = (i + 1) * P
                    link(dve.tensor_scalar(DIST[:, i, 0:n], posf[:, 0:n], POSQ[:, i:i + 1], None, ALU.subtract))
                    link(dve.scalar_tensor_tensor(DIST[:, i, 0:n], DIST[:, i, 0:n], -1.0, DIST[:, i, 0:n], ALU.mult, ALU.max))
                    link(dve.tensor_tensor(DIST[:, i, 0:n], DIST[:, i, 0:n], CON[:, C_CM + 512 - n:C_CM + 512], ALU.subtract))

                def maxima(b, n, scale, count):
                    link(dve.tensor_reduce(MX[:, b:b + 1], PB[b][:, 0:n], AX, ALU.max))
                    signal(dve.tensor_scalar(NB_[:, b:b + 1], MX[:, b:b + 1], -scale, None, ALU.mult), s_nb)

                def diff_scores(u):
                    h, i = u // 4, u % 4
                    n = (i + 1) * P
                    if u >= 2:
                        dve.wait_ge(s_tp, u - 1)
                    for m in range(2):
                        b = (2 * u + m) % 4
                        dve.wait_ge(s_sc, 2 * u + m + 1)
                        signal(dve.scalar_tensor_tensor(PB[b][:, 0:n], DIST[:, i, 0:n], -SLOPES[h] / DIFF_SCALE, PS[2 + b][:, 0:n],
                                                        ALU.mult, ALU.add), s_scf)
                        maxima(b, n, DIFF_SCALE, 2 * u + m)

                def diff_probs(u):
                    i, b = u % 4, 2 * (u % 2)
                    n = (i + 1) * P
                    dve.wait_ge(s_ex, 2 * u + 2)
                    link(dve.reciprocal(RR[:, b:b + 2], SE[:, b:b + 2]))
                    link(dve.tensor_tensor(RR[:, b + 1:b + 2], RR[:, b + 1:b + 2], LAM, ALU.mult))
                    link(dve.tensor_scalar(PB[b + 1][:, 0:n], PB[b + 1][:, 0:n], RR[:, b + 1:b + 2], None, ALU.mult))
                    signal(dve.scalar_tensor_tensor(PB[b][:, 0:n], PB[b][:, 0:n], RR[:, b:b + 1], PB[b + 1][:, 0:n], ALU.mult, ALU.subtract), s_at)

                def rotate(dst, bank, free, done):
                    link(dve.tensor_tensor(dst, bank[0:64, :], TRIG[0:64, :], ALU.mult))
                    signal(dve.tensor_tensor(ROT[0:64, :], bank[64:128, :], TRIG[64:128, :], ALU.mult), free)
                    signal(dve.tensor_tensor(dst, dst, ROT[0:64, :], ALU.add), done)

                def filled(name):
                    kind, m = name
                    if kind == "A":
                        ada_row(m)
                        return
                    bank, free, _ = acc_ready(name)
                    if m == 3:
                        rotate(KPE[0:64, :], bank, free, s_kpe)
                    else:
                        signal(dve.tensor_copy(CQT[:, m, :] if m < 2 else CKVT, bank[:, :]), free)

                dve.wait_ge(s_bada, 16)
                for u in range(19):
                    if u >= 6 and (u - 6) % 4 == 0:
                        h = (u - 6) // 4
                        dve.wait_ge(s_rst, h + 1)
                        signal(dve.scalar_tensor_tensor(YA[:, 1, h, :], PS[7][:, :], SUBW, RSB, ALU.mult, ALU.mult), s_ya)
                    if u < 16:
                        diff_scores(u)
                    if 1 <= u <= 16:
                        diff_probs(u - 1)
                    if u - 1 in DIFF_FILL:
                        filled(DIFF_FILL[u - 1])

                dve.wait_ge(s_crs, 1)
                for m in range(2):
                    link(dve.scalar_tensor_tensor(CQT[:, m, :], CQT[:, m, :], COLS[:, R_QN + m:R_QN + m + 1], RSB, ALU.mult, ALU.mult))
                dve.sem_inc(s_cn, 1)
                dve.wait_ge(s_crs, 2)
                signal(dve.scalar_tensor_tensor(CKVT, CKVT, COLS[:, R_KN:R_KN + 1], RSB, ALU.mult, ALU.mult), s_cn)
                for h in range(NH):
                    bank, free, _ = acc_ready(("QP", h))
                    rotate(QP[0:64, h, :], bank, free, s_qpr)

                def mla_scores(u):
                    b, n = u % 4, (u % 4 + 1) * P
                    if u >= 4:
                        dve.wait_ge(s_tp, 16 + u - 3)
                    dve.wait_ge(s_sc, 32 + u + 1)
                    signal(dve.tensor_tensor(PB[b][:, 0:n], PS[2 + b][:, 0:n], CON[:, C_CM + 512 - n:C_CM + 512], ALU.add), s_scf)
                    maxima(b, n, MLA_SCALE, 32 + u)

                def mla_probs(u):
                    b, n = u % 4, (u % 4 + 1) * P
                    dve.wait_ge(s_ex, 32 + u + 1)
                    link(dve.reciprocal(RR[:, b:b + 1], SE[:, b:b + 1]))
                    signal(dve.tensor_scalar(PB[b][:, 0:n], PB[b][:, 0:n], RR[:, b:b + 1], None, ALU.mult), s_at)

                for u in range(19):
                    if u >= 6 and (u - 6) % 4 == 0:
                        h = (u - 6) // 4
                        dve.wait_ge(s_pv, NH + h + 1)
                        signal(dve.tensor_copy(YA[:, 0, h, :], PS[7][:, :]), s_ya)
                    if u < 16:
                        mla_scores(u)
                    if 1 <= u <= 16:
                        mla_probs(u - 1)
                    if u - 1 in MLA_FILL:
                        filled(MLA_FILL[u - 1])
                link(dve.scalar_tensor_tensor(MOD[:, 4], MOD[:, 4], 1.0, NW2, ALU.add, ALU.mult))

                def residual(t):
                    if t >= 3:
                        dve.wait_ge(s_nt, t - 2)
                        dve.wait_ge(s_h2st, 16 * (t - 2))
                    dve.wait_ge(s_o, t + 1)
                    for q in range(2):
                        cols = slice(q * CH, (q + 1) * CH)
                        link(dve.tensor_tensor(H2R[t % 3][:, cols], PS[2 * t + q][:, :], MOD[:, 2, cols], ALU.mult))
                    signal(dve.tensor_tensor(X[:, t, :], X[:, t, :], H2R[t % 3], ALU.add), s_xr)

                def norm2(t):
                    dve.wait_ge(s_ss2, t + 1)
                    signal(dve.tensor_scalar(MS[:, t:t + 1], SS[:, t:t + 1], 1.0 / D, EPS, ALU.mult, ALU.add), s_ms)
                    dve.wait_ge(s_rs, t + 2)
                    link(dve.scalar_tensor_tensor(H2R[t % 3], X[:, t, :], RS[:, t:t + 1], MOD[:, 4], ALU.mult, ALU.mult))
                    signal(dve.tensor_tensor(H2R[t % 3], H2R[t % 3], MOD[:, 3], ALU.add), s_h2)

                residual(0)
                for t in range(TT):
                    norm2(t)
                    if t + 1 < TT:
                        residual(t + 1)

                for t in range(TT):
                    dve.wait_ge(s_lg, t + 1)
                    dve.tensor_tensor(GL[:, t, :], PS[2 * t][:, 0:NG], BC[:, B_RB:B_RB + NG], ALU.add)
                    link(dve.tensor_tensor(EL[:, t, :], PS[2 * t][:, NG:NG + NE], BC[:, B_RB + NG:B_RB + NG + NE], ALU.add))

                def per_token(v, n):
                    return v.rearrange("p (t a) -> p t a", a=1).broadcast_to([P, TT, n])

                def per_entry(v, n):
                    return v.rearrange("p (a e) -> p a e", a=1).broadcast_to([P, TT, n])

                def first_of_max(oh, v, best, order, n):
                    link(dve.tensor_reduce(best, v, AX, ALU.max))
                    link(dve.tensor_tensor(oh, v, per_token(best, n), ALU.is_equal))
                    link(dve.tensor_tensor(oh, oh, per_entry(order, n), ALU.mult))
                    link(dve.tensor_reduce(RV, oh, AX, ALU.max))
                    link(dve.tensor_tensor(oh, oh, per_token(RV, n), ALU.is_equal))

                first_of_max(PEN, GL, RM, CON[:, C_D4:C_D4 + 4], NG)
                signal(dve.tensor_tensor(GE, GL, per_token(RM, NG), ALU.subtract), s_ge)
                link(dve.tensor_scalar(flat(PEN), flat(PEN), -1.0, -NEG, ALU.add, ALU.mult))
                by_group = lambda v: v.rearrange("p t (g e) -> p (t g) e", g=NG)
                link(dve.tensor_tensor(by_group(LM), by_group(EL),
                                       flat(PEN).rearrange("p (a b) -> p a b", b=1).broadcast_to([P, TT * NG, NE_G]), ALU.add))
                first_of_max(OH1, LM, R1, CON[:, C_D32:C_D32 + 32], NE)
                link(dve.scalar_tensor_tensor(flat(LM), flat(OH1), 2 * NEG, flat(LM), ALU.mult, ALU.add))
                first_of_max(OH2, LM, R2, CON[:, C_D32:C_D32 + 32], NE)
                signal(dve.tensor_tensor(RW, R2, R1, ALU.subtract), s_ge)
                signal(dve.tensor_tensor(MM, OH1, OH2, ALU.add), s_oh)
                dve.wait_ge(s_gf, 2)
                link(dve.tensor_reduce(R3, GE, AX, ALU.add))
                link(dve.reciprocal(R3, R3))
                link(dve.tensor_scalar(R4, RW, 1.0, None, ALU.add))
                link(dve.reciprocal(R4, R4))
                link(dve.tensor_tensor(R3, R3, R4, ALU.mult))
                weight = PAY[:, :, :, :].bitcast(F32)
                link(dve.tensor_copy(weight[:, :, 0, 2], R3))
                link(dve.tensor_tensor(weight[:, :, 1, 2], R3, RW, ALU.mult))
                dve.wait_ge(s_pp, 1)
                cnt = PS[1][0:NE, 64:65]
                for k, limit in enumerate((P, 2 * P, 3 * P)):
                    link(dve.tensor_scalar(OVT[:, k:k + 1], cnt, float(limit), None, ALU.is_gt))
                link(dve.tensor_tensor(OVT[:, 0:1], OVT[:, 0:1], OVT[:, 1:2], ALU.add))
                link(dve.tensor_tensor(OVT[:, 0:1], OVT[:, 0:1], OVT[:, 2:3], ALU.add))
                signal(dve.tensor_scalar(OVR, ONE[0:NE, :], OVT[:, 0:1], None, ALU.mult), s_ovt)
                link(dve.tensor_copy(flat(POS), PS[0][:, 0:TT * NE]))
                link(dve.tensor_scalar(flat(BLK), flat(POS), float(P), None, ALU.is_ge))
                for limit in (2 * P, 3 * P):
                    link(dve.scalar_tensor_tensor(flat(BLK), flat(POS), float(limit), flat(BLK), ALU.is_ge, ALU.add))
                link(dve.scalar_tensor_tensor(flat(ROWF), flat(BLK), -float(P), flat(POS), ALU.mult, ALU.add))
                dve.wait_ge(s_ov2, 1)
                link(dve.tensor_copy(OVS, PS[2][:, 0:NE]))
                link(dve.tensor_copy(OVE, PS[2][:, 64:64 + NE]))
                row0 = lambda v, n: v.rearrange("p (a e) -> p a e", a=1).broadcast_to([1, 8, n])
                link(dve.tensor_tensor(KCMP, row0(OVE[0:1, :], NE),
                                       CON[0:1, C_K8:C_K8 + 8].rearrange("p (k a) -> p k a", a=1).broadcast_to([1, 8, NE]), ALU.is_le))
                link(dve.tensor_reduce(NPF[:, 0:8], KCMP, AX, ALU.add))
                link(dve.tensor_scalar(EID[0:1, 32:40], NPF[:, 0:8], float(NE - 1), None, ALU.min))
                over = PS[2][0:1, 128:129]
                link(dve.tensor_scalar(NPF[:, 8:9], over, 0.0, 16.0, ALU.is_gt, ALU.add))
                for limit in (2.0, 4.0, 6.0):
                    link(dve.scalar_tensor_tensor(NPF[:, 8:9], over, limit, NPF[:, 8:9], ALU.is_gt, ALU.add))
                link(dve.tensor_copy(EID[0:1, 40:41], NPF[:, 8:9]))
                signal(dve.tensor_scalar(EID[0:1, 41:42], NPF[:, 8:9], -1.0, None, ALU.add), s_eid)
                link(dve.tensor_tensor(TMPE, BLK, per_entry(OVS, NE), ALU.add))
                link(dve.tensor_scalar(flat(TMPE), flat(TMPE), float(NE - 1), None, ALU.add))
                e32 = per_entry(CON[:, C_E32:C_E32 + 32], NE)
                link(dve.tensor_tensor(TMPE, TMPE, e32, ALU.subtract))
                link(dve.scalar_tensor_tensor(flat(TMPE), flat(BLK), 0.0, flat(TMPE), ALU.is_gt, ALU.mult))
                link(dve.tensor_tensor(TMPE, TMPE, e32, ALU.add))
                link(dve.scalar_tensor_tensor(flat(ROWF), flat(ROWF), float(NB_MAX), flat(TMPE), ALU.mult, ALU.add))
                for s, oh in enumerate((OH1, OH2)):
                    link(dve.tensor_tensor(TMPE, oh, ROWF, ALU.mult))
                    link(dve.tensor_reduce(RV, TMPE, AX, ALU.add))
                    link(dve.tensor_copy(ROWI[:, s:8:2], RV))
                dve.sem_inc(s_row, 1)

                more = more_pairs(dve)
                dve.sem_inc(s_ye, 1)

                def low(i, v):
                    slot, half, kind = unit_matrix(v % UNITS)
                    dve.wait_ge(s_hi, i * UNITS + (v + 1))
                    dve.tensor_tensor(unit_of(W_L[slot], v, half), unit_of(SLOT[slot], v, half),
                                      unit_of(W_H[v % 4], v).bitcast(F32), ALU.subtract).then_inc(s_lo, 1)

                def rows_low(s, count):
                    dve.wait_ge(s_xh, count)
                    dve.tensor_tensor(XG_L[s][:, 0:4, :], tiles4(PS[0]), XG_H[s][:, 0:4, :].bitcast(F32), ALU.subtract)
                    dve.tensor_tensor(XG_L[s][:, 4:8, :], tiles4(PS[1]), XG_H[s][:, 4:8, :].bitcast(F32), ALU.subtract).then_inc(s_xl, 1)

                def hidden(i, s):
                    dve.wait_ge(s_gs, i * 2 + (s + 1))
                    dve.wait_ge(s_unit, i * UNITS + (4 * s + 4))
                    weight = TBL[:, bass.ds(i * 2 + s, 1), 2:3].rearrange("p a b -> p (a b)").bitcast(F32)
                    dve.scalar_tensor_tensor(HH, PS[3][:, :], weight, GS, ALU.mult, ALU.mult).then_inc(s_hh, 1)

                def hidden_low(s, count):
                    dve.wait_ge(s_hth, count)
                    dve.tensor_tensor(HH_L[s][:, :, :], tiles4(PS[4]), HH_H[s][:, :, :].bitcast(F32), ALU.subtract).then_inc(s_htl, 1)

                def output_half(i, v):
                    s, q = divmod(v - 8, 2)
                    if q == 0:
                        dve.wait_ge(s_slot[s], i + 1)
                    dve.wait_ge(s_unit, i * UNITS + (v + 1))
                    dve.tensor_copy(YB[s][:, q * CH:(q + 1) * CH], down_bank(v)[:, :]).then_inc(s_ye, 1)

                def pair(i, ahead):
                    low(i, 4)
                    rows_low(1, i * 2 + 2)
                    low(i, 5)
                    low(i, 6)
                    hidden(i, 0)
                    low(i, 7)
                    low(i, 8)
                    hidden_low(0, i * 2 + 1)
                    low(i, 9)
                    hidden(i, 1)
                    low(i, 10)
                    output_half(i, 8)
                    hidden_low(1, i * 2 + 2)
                    low(i, 11)
                    output_half(i, 9)
                    if ahead:
                        low(i, 12)
                        rows_low(0, i * 2 + 3)
                        low(i, 13)
                    output_half(i, 10)
                    if ahead:
                        low(i, 14)
                    output_half(i, 11)
                    if ahead:
                        low(i, 15)

                for v in range(4):
                    low(0, v)
                rows_low(0, 1)
                with dve.Fori(0, more) as i:
                    pair(i, True)
                pair(more, False)
                for t in range(TT):
                    dve.wait_ge(s_cmb[t], 16)
                    link(dve.tensor_tensor(CB[t][:, 0:D], CB[t][:, 0:D], CB[t][:, D:2 * D], ALU.add))
                    link(dve.tensor_tensor(CB[t][:, 0:D], CB[t][:, 0:D], MOD[:, 5], ALU.mult))
                    link(dve.tensor_tensor(X[:, t, :], X[:, t, :], CB[t][:, 0:D], ALU.add))
                dve.sem_inc(s_end, 1)
                dve.wait_ge(s_clr, l + 1)
                dve.sem_inc(s_seq, 1)
            dve.sem_inc(s_fss, 1)
            dve.wait_ge(s_prot, TT)
            olink(dve.tensor_scalar(MS, SS, 1.0 / D, EPS, ALU.mult, ALU.add))
            dve.sem_inc(s_fin, 1)
            dve.wait_ge(s_finr, 1)
            dve.wait_ge(s_fw, 16)
            for t in range(TT):
                dve.scalar_tensor_tensor(X[:, t, :], X[:, t, :], RS[:, t:t + 1], MOD[:, 0], ALU.mult, ALU.mult).then_inc(s_fout, 1)

        @block.tensor
        def _(pe):
            pe.wait_ge(s_con, 80)
            pe.transpose(PS[2][:, 0:KT], CROW, ID[0:KT, 0:KT]).then_inc(s_pro, 1)
            pe.wait_ge(s_proa, 2)
            ln = dict(start=True, stop=True)

            with pe.Fori(0, L) as l:
                def begin(name):
                    bank, free, k = acc_bank(name)
                    if k >= 2:
                        pe.wait_ge(free, k - 1)
                    return bank

                def begin_tr(name):
                    bank, free, k = tr_bank(name)
                    if k >= 2:
                        pe.wait_ge(free, k - 1)
                    return bank

                def chunk(name):
                    n = CHN[name]
                    pe.wait_ge(s_load[chunk_slot(n)], slot_count(n))
                    return SLOT[chunk_slot(n)]

                def tile_of(v, t):
                    return v[:, t * P:(t + 1) * P]

                def turn(bank, blocks, done):
                    for j, v in enumerate(blocks):
                        ins = pe.transpose(bank[:, j * P:(j + 1) * P], v, ID)
                    ins.then_inc(done, 1)

                def ada(j):
                    w = chunk(("A", j)).rearrange("p (k n) -> p k n", k=KT)
                    bank = begin(("A", j))
                    for k in range(KT):
                        ins = pe.matmul(bank[:, :], COND[:, k:k + 1].broadcast_to([P, P]), w[:, k, :], start=(k == 0), stop=(k == KT - 1))
                    ins.then_inc(s_acc, 1)

                def project(name, lhs, rhs):
                    bank = begin(name)
                    n = len(lhs)
                    for k in range(n):
                        ins = pe.matmul(bank[:, :], lhs[k], rhs[k], start=(k == 0), stop=(k == n - 1))
                    ins.then_inc(s_acc, 1)

                def in_feature(name, j, m):
                    w = chunk(("I", j)).rearrange("p (k n) -> p k n", k=KT)
                    project(name, [tile_of(w[:, k, :], m) for k in range(KT)], [HT[:, k, :] for k in range(KT)])

                def in_token(name, j, t):
                    w = chunk(("I", j)).rearrange("p (k n) -> p k n", k=KT)
                    project(name, [tile_of(HT[:, k, :], t) for k in range(KT)], [w[:, k, :] for k in range(KT)])

                for t in range(TT):
                    pe.wait_ge(s_hr, t + 1)
                    for q in range(2):
                        turn(begin_tr(("H", t, q)), [tile_of(HR[t % 3], 4 * q + k) for k in range(4)], s_tr)
                pe.wait_ge(s_par, N_PAR)
                bank = begin_tr("P")
                pe.transpose(bank[:, 0:R_N], ROWS, ID[0:R_N, 0:R_N]).then_inc(s_tr, 1)

                def ada_columns(j):
                    pe.wait_ge(s_mrow, j + 1)
                    for b in range(4):
                        col = 4 * j + b
                        ins = pe.matmul(PS[4][:, col:col + 1], MOD[:, j // 2, (j % 2) * CH + b * P:(j % 2) * CH + (b + 1) * P], ID[:, 0:1], **ln)
                    ins.then_inc(s_mcol, 1)

                for j in range(4):
                    ada(j)
                    if j:
                        ada_columns(j - 1)
                ada_columns(3)
                def token_major(m):
                    bank = begin_tr(("T", m))
                    pe.wait_ge(s_sx, m + 1)
                    src = SX[m % 2] if m < 8 else BT[:, m - 8, :]
                    turn(bank, [tile_of(src, t) for t in range(TT)], s_tr)

                def three(out_, k, a_h, a_l, b_h, b_l):
                    pe.matmul(out_, a_h, b_h, start=(k == 0), stop=False)
                    pe.matmul(out_, a_h, b_l, start=False, stop=False)
                    return pe.matmul(out_, a_l, b_h, start=False, stop=(k == KT - 1))

                for m in range(16):
                    u = m // 2
                    bank = begin(("X", m))
                    pe.wait_ge(s_inl, u + 1)
                    w_h, w_l = in_place(u), in_half(W_L[in_slot(u)], u)
                    for k in range(KT):
                        if m == 0:
                            pe.wait_ge(s_hnl, k + 1)
                        ins = three(bank[:, :], k, tile_of(w_h[:, k, :], m % 2), tile_of(w_l[:, k, :], m % 2), HN_H[:, k, :], HN_L[:, k, :])
                    ins.then_inc(s_acc, 1)
                    if 1 <= m <= 12:
                        token_major(m - 1)
                for m in range(16):
                    u = 8 + m // 4
                    bank = begin(("Z", m))
                    pe.wait_ge(s_inl, u + 1)
                    w_h, w_l = in_place(u), in_half(W_L[in_slot(u)], u)
                    for k in range(KT):
                        ins = three(bank[:, 0:256], k, tile_of(HN_H[:, k, :], m % 4), tile_of(HN_L[:, k, :], m % 4), w_h[:, k, :], w_l[:, k, :])
                    ins.then_inc(s_acc, 1)
                bank = begin("DT")
                for t in range(TT):
                    for k in range(KT):
                        ins = pe.matmul(bank[:, t * SH:(t + 1) * SH], tile_of(HT[:, k, :], t), WDT[:, k, :], start=(k == 0), stop=(k == KT - 1))
                ins.then_inc(s_acc, 1)
                bank = begin("AC")
                pe.wait_ge(s_adt, 1)
                pe.matmul(bank[:, 0:TT * SH], UU, flat(ADT), **ln)
                pe.matmul(bank[:, TT * SH:2 * TT * SH], ONE, flat(ADT), **ln).then_inc(s_acc, 1)
                bank = begin_tr("AT")
                pe.wait_ge(s_acs, 1)
                pe.transpose(bank[0:TT * SH, 0:P], flat(ACS), ID).then_inc(s_tr, 1)
                turned_out(pe, "AT")
                pe.wait_ge(s_sx, 16)

                def decay_rows(cc, g):
                    bank = begin(("R", cc, g))
                    pe.matmul(bank[:, :], IDB[:, :], CMB[:, :].rearrange("p (a l) -> p a l", a=1).broadcast_to([P, 4, P]), start=True, stop=False)
                    for h in range(4):
                        j = cc * SH + 4 * g + h
                        ins = pe.matmul(tile_of(bank, h), ID[0:TT * SH, j:j + 1].broadcast_to([TT * SH, P]), ACST,
                                        start=False, stop=(h == 3))
                    ins.then_inc(s_acc, 1)

                def ssd_group(cc, g):
                    hf = g // 2
                    pe.wait_ge(s_mt, 4 * cc + g + 1)
                    if g % 2 == 0 and cc + hf:
                        pe.wait_ge(s_ydf, 2 * cc + hf)
                    for h in range(4):
                        at = (4 * (g % 2) + h) * SP_
                        ins = pe.matmul(PS[5][:, at:at + SP_], MT[g % 2][:, h, :], XW[:, (4 * g + h) * SP_:(4 * g + h + 1) * SP_], **ln)
                    ins.then_inc(s_yd, 1)
                    half = slice((g % 2) * 256, (g % 2) * 256 + 256)
                    cols = slice(g * 256, g * 256 + 256)
                    last = g % 2 == 1
                    if cc:
                        if g % 2 == 0:
                            pe.wait_ge(s_ste, 2 * (cc - 1) + hf + 1)
                        ins = pe.matmul(PS[6][:, half], tile_of(CT[:, g, :], cc), ST[:, cols], **ln)
                        if last and cc == TT - 1:
                            ins.then_inc(s_st, 1)
                    if cc < TT - 1:
                        if g % 2 == 0 and cc + hf:
                            pe.wait_ge(s_ste, 2 * cc + hf)
                        ins = pe.matmul(PS[7][:, half], tile_of(BTOK[:, cc, :], g), XD[:, cols], **ln)
                        if last:
                            ins.then_inc(s_st, 1)

                def fill(name):
                    kind, m = name
                    if kind == "A":
                        ada(m)
                    elif kind == "DV":
                        in_token(name, 8, m)
                    else:
                        in_feature(name, {"DQ": 6, "DK": 7, "C": 9}[kind], m)

                for cc in range(TT):
                    if cc:
                        pe.wait_ge(s_mt, 4 * cc)
                    for g in range(SG):
                        ins = pe.matmul(tile_of(PS[4], g), tile_of(BT[:, g, :], cc), tile_of(CT[:, g, :], cc), **ln)
                    ins.then_inc(s_cb, 1)
                    decay_rows(cc, 0)
                    decay_rows(cc, 1)
                    fill(SSD_FILL[3 * cc])
                    pe.wait_ge(s_xw, cc + 1)
                    for g in range(SG):
                        ssd_group(cc, g)
                        if g < 2:
                            decay_rows(cc, g + 2)
                        if g % 2:
                            fill(SSD_FILL[3 * cc + 1 + g // 2])

                def transposed(k, buf):
                    pe.wait_ge(s_at, k + 1)
                    if k:
                        pe.wait_ge(s_pt, k)
                    turn(PS[6], [tile_of(buf, j) for j in range(k % 4 + 1)], s_tp)

                def values(h, v):
                    pe.wait_ge(s_pt, 4 * h + 4)
                    if h:
                        pe.wait_ge(s_ya, h)
                    for j in range(TT):
                        ins = pe.matmul(PS[7][:, j * P:T], v[j], PT[:, j, j * P:T], start=(j == 0), stop=(j == TT - 1))
                    ins.then_inc(s_pv, 1)

                def diff_scores(u):
                    h, i = u // 4, u % 4
                    for m in range(2):
                        k = 2 * u + m
                        b, rows = k % 4, slice(64 * m, 64 * m + 64)
                        if k >= 4:
                            pe.wait_ge(s_scf, k - 3)
                        pe.matmul(PS[2 + b][:, 0:(i + 1) * P], DQT[rows, h, i * P:(i + 1) * P], DKT[rows, h, 0:(i + 1) * P], **ln).then_inc(s_sc, 1)

                evacuated(pe, ("DV", 2))
                evacuated(pe, ("DV", 3))
                pe.wait_ge(s_ydf, 8)
                pe.wait_ge(s_ste, 6)
                for u in range(19):
                    if u < 16:
                        diff_scores(u)
                    if u >= 6 and (u - 6) % 4 == 0:
                        h = (u - 6) // 4
                        bank = begin(("DS", h))
                        pe.wait_ge(s_sq, h + 1)
                        pe.matmul(bank[:, :], ONE, SQB, **ln).then_inc(s_acc, 1)
                    if 2 <= u <= 17:
                        transposed(u - 2, PB[2 * (u % 2)])
                        if u % 4 == 1:
                            h = (u - 2) // 4
                            values(h, [DVT[:, j, h * P:(h + 1) * P] for j in range(TT)])
                    if u in DIFF_FILL:
                        fill(DIFF_FILL[u])
                bank = begin("SQ")
                pe.wait_ge(s_csq, 2)
                pe.matmul(bank[:, :], ONE, SQB, start=True, stop=False)
                pe.matmul(bank[:, :], ONE, PB[0], start=False, stop=True).then_inc(s_acc, 1)
                bank = begin("SK")
                pe.wait_ge(s_csq, 3)
                pe.matmul(bank[:, :], ONE, SQB, **ln).then_inc(s_acc, 1)
                pe.wait_ge(s_scf, 32)
                for cc in range(TT):
                    pe.wait_ge(s_ynn, cc + 1)
                    for q in range(2):
                        turn(begin_tr(("Y", cc, q)), [tile_of(Z[:, cc, :], 4 * q + k) for k in range(4)], s_tr)
                w = chunk("U")
                uq = w[:, 0:2048].rearrange("p (k h n) -> p k h n", k=2, h=NH)
                ukv = w[:, 2048:3072].rearrange("p (h n) -> p h n", h=NH)
                pe.wait_ge(s_cn, 1)
                for h in range(NH):
                    project(("QN", h), [uq[:, k, h, 0:P] for k in range(2)], [CQT[:, k, :] for k in range(2)])
                for h in range(NH):
                    project(("QP", h), [uq[:, k, h, P:2 * P] for k in range(2)], [CQT[:, k, :] for k in range(2)])
                pe.wait_ge(s_cn, 2)
                for h in range(NH):
                    project(("KN", h), [ukv[:, h, 0:P]], [CKVT])
                for t in range(TT):
                    bank = begin(("V", t))
                    pe.matmul(bank[:, :].rearrange("p (h n) -> p h n", h=NH), tile_of(CKVT, t), ukv[:, :, P:2 * P], **ln).then_inc(s_acc, 1)

                def mla_scores(u):
                    h, i, b = u // 4, u % 4, u % 4
                    if u >= 4:
                        pe.wait_ge(s_scf, 32 + u - 3)
                    out_, n = PS[2 + b], (i + 1) * P
                    pe.matmul(out_[:, 0:n], tile_of(QN[:, h, :], i), KN[:, h, 0:n], start=True, stop=False)
                    pe.matmul(out_[:, 0:n], tile_of(QP[0:64, h, :], i), KPE[0:64, 0:n], start=False, stop=True).then_inc(s_sc, 1)

                turned_out(pe, ("Y", 3, 0))
                turned_out(pe, ("Y", 3, 1))
                evacuated(pe, ("V", 2))
                evacuated(pe, ("V", 3))
                pe.wait_ge(s_kpe, 1)
                pe.wait_ge(s_qpr, NH)
                for u in range(18):
                    if u < 16:
                        mla_scores(u)
                    if u >= 2:
                        transposed(16 + u - 2, PB[(u - 2) % 4])
                        if u % 4 == 1:
                            h = (u - 2) // 4
                            values(NH + h, [VT[:, j, h * P:(h + 1) * P] for j in range(TT)])
                    if u in MLA_FILL:
                        fill(MLA_FILL[u])
                def turn_normed(t):
                    pe.wait_ge(s_h2, t + 1)
                    for q in range(2):
                        for k in range(4):
                            ins = pe.transpose(tile_of(PS[2 * t + q], k), tile_of(H2R[t % 3], 4 * q + k), ID)
                    ins.then_inc(s_nt, 1)

                evacuated(pe, ("A", 10))
                evacuated(pe, ("A", 11))
                pe.wait_ge(s_scf, 48)
                pe.wait_ge(s_pt, 32)
                pe.wait_ge(s_ya, 2 * NH)
                for j in range(4):
                    w = chunk(("O", j)).rearrange("p (f n) -> p f n", f=4)
                    src = (YA[:, 0], YA[:, 1], HT[:, 0:4], HT[:, 4:8])[j]
                    for t in range(TT):
                        for q in range(2):
                            for f in range(4):
                                ins = pe.matmul(PS[2 * t + q][:, :], tile_of(src[:, f, :], t), w[:, f, q * CH:(q + 1) * CH],
                                                start=(j == 0 and f == 0), stop=(j == 3 and f == 3))
                        if j == 3:
                            ins.then_inc(s_o, 1)
                            if t >= 2:
                                turn_normed(t - 2)
                    if j < 3:
                        ins.then_inc(s_oc, 1)
                def logits(t):
                    pe.wait_ge(s_ntf, t + 1)
                    for k in range(KT):
                        ins = pe.matmul(PS[2 * t][:, 0:NG + NE], tile_of(H2T[:, k, :], t), WR[:, k, :], start=(k == 0), stop=(k == KT - 1))
                    ins.then_inc(s_lg, 1)

                logits(0)
                for t in range(2, TT):
                    turn_normed(t)
                    logits(t - 1)
                logits(TT - 1)
                pe.wait_ge(s_oh, 1)
                for t in range(TT):
                    for before in range(t):
                        pe.matmul(PS[0][:, t * NE:(t + 1) * NE], ONE, MM[:, before, :], start=(before == 0), stop=False)
                    pe.matmul(PS[0][:, t * NE:(t + 1) * NE], SU, MM[:, t, :], start=(t == 0), stop=True)
                for t in range(TT):
                    ins = pe.matmul(PS[1][0:NE, 64:65], MM[:, t, :], ONE[:, 0:1], start=(t == 0), stop=(t == TT - 1))
                ins.then_inc(s_pp, 1)
                pe.wait_ge(s_ovt, 1)
                pe.matmul(PS[2][:, 0:NE], OVR, SU[0:NE, 0:NE], **ln)
                pe.matmul(PS[2][:, 64:64 + NE], OVR, UU[0:NE, 0:NE], **ln)
                pe.matmul(PS[2][:, 128:129], OVR, ONE[0:NE, 0:1], **ln).then_inc(s_ov2, 1)

                more = more_pairs(pe)

                def turn_rows(i, s):
                    pe.wait_ge(s_gd[s], i * 16 + 16)
                    for q in range(2):
                        for k in range(4):
                            ins = pe.transpose(tile_of(PS[q], k), tile_of(XG[s], 4 * q + k), ID)
                    ins.then_inc(s_xt, 1)

                def unit(i, v):
                    slot, half, kind = unit_matrix(v)
                    s = v // 4 % 2 if kind == "in" else (v - 8) // 2
                    pe.wait_ge(s_lo, i * UNITS + (v + 1))
                    w_h, w_l = unit_of(W_H[v % 4], v), unit_of(W_L[slot], v, half)
                    if kind == "in":
                        bank, t_h, t_l = PS[2 + v // 2 % 2], XG_H[s][:, 4 * half:4 * half + 4, :], XG_L[s][:, 4 * half:4 * half + 4, :]
                        first, last = half == 0, half == 1
                    else:
                        bank, t_h, t_l, first, last = down_bank(v), HH_H[s], HH_L[s], True, True
                    for k in range(4):
                        pe.matmul(bank[:, :], t_h[:, k, :], w_h[:, k, :], start=(first and k == 0), stop=False)
                        pe.matmul(bank[:, :], t_h[:, k, :], w_l[:, k, :], start=False, stop=False)
                        ins = pe.matmul(bank[:, :], t_l[:, k, :], w_h[:, k, :], start=False, stop=(last and k == 3))
                    ins.then_inc(s_unit, 1)

                def turn_hidden(i, s):
                    pe.wait_ge(s_hh, i * 2 + (s + 1))
                    for k in range(4):
                        ins = pe.transpose(tile_of(PS[4], k), tile_of(HH, k), ID)
                    ins.then_inc(s_htp, 1)

                def pair(i, ahead):
                    pe.wait_ge(s_xl, i * 2 + 1)
                    unit(i, 0)
                    unit(i, 1)
                    turn_rows(i, 1)
                    unit(i, 2)
                    unit(i, 3)
                    pe.wait_ge(s_xl, i * 2 + 2)
                    pe.wait_ge(s_gs, i * 2 + 1)
                    unit(i, 4)
                    unit(i, 5)
                    turn_hidden(i, 0)
                    unit(i, 6)
                    unit(i, 7)
                    pe.wait_ge(s_htl, i * 2 + 1)
                    pe.wait_ge(s_ye, i * 4 + 1)
                    unit(i, 8)
                    turn_hidden(i, 1)
                    unit(i, 9)
                    if ahead:
                        turn_rows(i + 1, 0)
                    pe.wait_ge(s_htl, i * 2 + 2)
                    unit(i, 10)
                    pe.wait_ge(s_ye, i * 4 + 2)
                    unit(i, 11)

                turn_rows(0, 0)
                with pe.Fori(0, more) as i:
                    pair(i, True)
                pair(more, False)
                pe.sem_inc(s_end, 1)
                pe.wait_ge(s_clr, l + 1)
                pe.sem_inc(s_seq, 1)


INS = ["x", "c", "positions", "w_ada", "b_ada", "norm1_w", "w_in", "mla_q_norm_w", "mla_w_uq", "mla_kv_norm_w", "mla_w_ukv",
       "diff_lambda", "diff_subln_w", "ssd_conv_w", "ssd_conv_b", "ssd_dt_bias", "ssd_a_log", "ssd_d", "ssd_norm_w",
       "w_out", "norm2_w", "router_w_group", "router_b_group", "router_w_expert", "router_b_expert",
       "exp_w_gate", "exp_w_up", "exp_w_down", "final_norm_w"]


def kernel(**inputs):
    import concourse.bacc as bacc
    from concourse.bass_utils import run_bass_kernel_spmd

    nc = bacc.Bacc("TRN2", target_bir_lowering=False, num_devices=1)
    arrays = {f"in_{name}": np.ascontiguousarray(inputs[name]) for name in INS}
    arrays.update({f"in_{name}": a for name, a in shape_constants().items()})
    args = [nc.dram_tensor(n, a.shape, mybir.dt.from_np(a.dtype), kind="ExternalInput").ap() for n, a in arrays.items()]
    out = nc.dram_tensor("out", (1, T, D), F32, kind="ExternalOutput").ap()
    h2_rows = nc.dram_tensor("h2_rows", (T, D), F32, kind="Internal").ap()
    expert_rows = nc.dram_tensor("expert_rows", (2 * T, D), F32, kind="Internal").ap()
    slot_table = nc.dram_tensor("slot_table", (P * NB_MAX, 4), I32, kind="Internal").ap()
    hybrid_kernel(nc, *args, out, h2_rows, expert_rows, slot_table)
    r = run_bass_kernel_spmd(nc, [arrays], core_ids=[0])
    return r.results[0]["out"]
```

```python
import math
from contextlib import ExitStack

import numpy as np
import concourse.bass as bass
from concourse import mybir

F32 = mybir.dt.float32
F32R = mybir.dt.float32r
BF16 = mybir.dt.bfloat16
I32 = mybir.dt.int32
U32 = mybir.dt.uint32
ALU = mybir.AluOpType
ACT = mybir.ActivationFunctionType
AX = mybir.AxisListType.X

P = 128
T, D, L = 512, 1024, 2
TT, KT = T // P, D // P
NH = 4
MQ, MKV, DN, DR, DV = 256, 128, 128, 64, 128
DQK = 64
SH, SP_, SG, SN_, SC = 16, 64, 4, 128, 4
DI = SH * SP_
NG, NE_G = 4, 8
NE = NG * NE_G
FE = 512
O_CQ, O_CKV, O_KPE, O_DQ, O_DK, O_DV, O_Z, O_XBC, O_DT = 0, 256, 384, 448, 960, 1472, 1984, 3008, 5056
N_IN = 5072
EPS, SUBEPS = 1e-6, 1e-5
NEG = -1.0e30
MLA_SCALE = (DN + DR) ** -0.5
DIFF_SCALE = DQK ** -0.5
SLOPES = [2.0 ** (-8.0 / NH * (h + 1)) for h in range(NH)]
NB_MAX = 42
PAIRS_MAX = 20
NEXT_LAYER = 44
CH = 512
CHE = KT * CH

C_ID, C_U, C_SU, C_ONE, C_CM = 0, 128, 256, 384, 512
C_D4, C_D32, C_E32, C_K8, C_INV, C_PH, C_HALF = 1024, 1028, 1060, 1092, 1100, 1101, 1102
C_N = 1104 + 2
B_DTB, B_ALOG, B_D, B_RB, B_LAM, B_LI = 0, 16, 32, 48, 84, 340
B_N = 342
R_CW, R_CB, R_QN, R_KN, R_SUB, R_NW1, R_BADA, R_N = 0, 64, 80, 82, 83, 84, 92, 108


def shape_constants():
    c = np.zeros((P, C_N), np.float32)
    i = np.arange(P)
    c[:, C_ID:C_ID + P] = np.eye(P)
    c[:, C_U:C_U + P] = i[:, None] <= i[None, :]
    c[:, C_SU:C_SU + P] = i[:, None] < i[None, :]
    c[:, C_ONE:C_ONE + P] = 1.0
    c[:, C_CM + 384:C_CM + 512] = np.where(i[:, None] >= i[None, :], 0.0, NEG)
    c[:, C_D4:C_D4 + 4] = 4.0 - np.arange(4)
    c[:, C_D32:C_D32 + 32] = 32.0 - np.arange(32)
    c[:, C_E32:C_E32 + 32] = np.arange(32)
    c[:, C_K8:C_K8 + 8] = np.arange(8)
    inv = (1.0 / (np.float32(10000.0) ** (np.arange(0, DR, 2, dtype=np.float32) / np.float32(DR)))).astype(np.float32)
    c[:, C_INV] = np.tile(inv, 4)
    c[0:64, C_PH], c[64:96, C_PH], c[96:128, C_PH] = 0.25, 0.5, 0.0
    c[:, C_HALF] = -0.5
    pay = np.zeros((P, TT, 2, 4), np.int32)
    tok = np.arange(TT)[None, :] * P + i[:, None]
    for s in range(2):
        pay[:, :, s, 0] = tok
        pay[:, :, s, 1] = 2 * tok + s
    table = np.zeros((P, NB_MAX, 4), np.int32)
    table[:, :, 0:2] = 1 << 20
    lam = np.array([[0.8 - 0.6 * math.exp(-0.3 * l), 1.0 - (0.8 - 0.6 * math.exp(-0.3 * l))] for l in range(L)], np.float32)
    eids = (np.arange(48, dtype=np.int32) % NE)[None, :]
    eids[0, NEXT_LAYER:NEXT_LAYER + L] = [min(l + 1, L - 1) for l in range(L)]
    return {"k_const": c, "k_pay": pay.reshape(P, -1), "k_table": table.reshape(P, -1), "k_lam": lam, "k_eid": eids}


def numbered(names):
    return {n: k for k, n in enumerate(names)}


SSD_FILL = [(n, m) for n in ("DQ", "DK", "DV") for m in range(4)]
DIFF_FILL = dict(zip((0, 2, 3, 5, 7, 9, 11, 13, 15), [("C", m) for m in range(4)] + [("A", j) for j in range(4, 9)]))
MLA_FILL = dict(zip((6, 10, 15), [("A", j) for j in range(9, 12)]))


OUT_ROWS = (2, 3, 1, 0)


def head_ends(u):
    return u >= 7 and (u - 7) % 4 == 0


ACC = numbered(
    [("A", 0), ("A", 2)] + [("X", m) for m in range(16)] + ["DT", "AC"]
    + [n for c in range(TT) for n in (("R", c, 0), ("R", c, 1), SSD_FILL[3 * c], ("R", c, 2), ("R", c, 3), *SSD_FILL[3 * c + 1:3 * c + 3])]
    + [n for u in range(20) for n in ([("DS", (u - 7) // 4)] if head_ends(u) else []) + ([DIFF_FILL[u]] if u in DIFF_FILL else [])]
    + ["SQ", "SK"]
    + [("QN", h) for h in range(NH)] + [("QP", h) for h in range(NH)] + [("KN", h) for h in range(NH)]
    + [("V", t) for t in range(TT)] + list(MLA_FILL.values()))
TRN = numbered([("H", t, q) for t in range(TT) for q in range(2)] + ["P"] + [("T", m) for m in range(12)] + ["AT"]
               + [("Y", c, q) for c in range(TT) for q in range(2)])
X_UNITS = 8

CHUNKS = [("A", j) for j in range(4)] + [("I", j) for j in range(10)] + [("A", j) for j in range(4, 9)] + ["U"] + [("A", j) for j in range(9, 12)] \
    + [("O", j) for j in range(4)]
CHN = numbered(CHUNKS)
NCH = len(CHUNKS)
CHUNK_DMAS = {("I", 9): 3, "U": 7}
IN_COLS = [O_XBC, O_XBC + 512, O_XBC + 1024, O_XBC + 1536, O_Z, O_Z + 512, O_DQ, O_DK, O_DV, O_CQ]


def chunk_slot(n):
    return n + 2 if n < 4 else n % 2


def slot_count(n):
    return sum(16 * CHUNK_DMAS.get(CHUNKS[m], 1) for m in range(2, n + 1) if chunk_slot(m) == chunk_slot(n))


UNITS = 12


def unit_matrix(v):
    return (v // 2 + 2) % 6, v % 2, ("in", "out")[v >= 8]


SLOT_BASE = [slot_count(max(m for m in range(NCH) if chunk_slot(m) == s)) for s in range(6)]


def hybrid_kernel(nc, x, c, positions, w_ada, b_ada, norm1_w, w_in, mla_q_norm_w, mla_w_uq, mla_kv_norm_w, mla_w_ukv,
                  diff_lambda, diff_subln_w, ssd_conv_w, ssd_conv_b, ssd_dt_bias, ssd_a_log, ssd_d, ssd_norm_w,
                  w_out, norm2_w, router_w_group, router_b_group, router_w_expert, router_b_expert,
                  exp_w_gate, exp_w_up, exp_w_down, final_norm_w,
                  k_const, k_pay, k_table, k_lam, k_eid, out, h2_rows, expert_rows, slot_table):
    with ExitStack() as ctx:
        at = {}

        def sb(name, shape, dt=F32):
            at[name] = (nc.sbuf_base + 31) // 32 * 32
            return ctx.enter_context(nc.sbuf_tensor(name, shape, dt))

        def sem(name):
            s = ctx.enter_context(nc.semaphore(name))
            layer_sems.append(s)
            return s

        def kept_sem(name):
            return ctx.enter_context(nc.semaphore(name))

        layer_sems = []

        RING = sb("ring", [P, 2, CHE])
        OV = sb("ov", [P, 4 * CHE])
        X = sb("x_sb", [P, TT, D])
        HT = sb("ht", [P, KT, T])
        MOD = sb("mod", [P, 6, D])
        YA = sb("ya", [P, 2, NH, T])
        F = sb("f_area", [P, 6144])
        TRIG = sb("trig", [P, T])
        CON = sb("con", [P, C_N])
        IDB = sb("ident_bf", [P, P], BF16)
        CMB = sb("causal_bf", [P, P], BF16)
        BC = sb("bc", [P, B_N])
        COLS = sb("cols", [P, R_N])
        MCOL = sb("mod_cols", [P, 2 * KT])
        COND = sb("cond", [P, KT])
        SM = sb("small", [P, 832])
        WDT = sb("w_dt", [P, KT, SH])
        WR = sb("w_router", [P, KT, NG + NE])
        PAY = sb("pay", [P, TT, 2, 4], I32)
        TBL = sb("tbl", [P, NB_MAX, 4], I32)
        EID = sb("eid", [1, 48], I32)
        ROWI = sb("row_idx", [P, 8], U32)
        GIDX = [sb(f"gidx{s}", [P, 1], U32) for s in range(2)]
        SIDX = [sb(f"sidx{s}", [P, 4], U32) for s in range(2)]
        SLOT = [RING[:, 0, :], RING[:, 1, :]] + [OV[:, j * CHE:(j + 1) * CHE] for j in range(4)]

        def ov(at, *shape):
            n = int(np.prod(shape))
            v = OV[:, at:at + n]
            return v if len(shape) == 1 else v.rearrange("p (a b) -> p a b", a=shape[0])

        def fa(at, *shape):
            n = int(np.prod(shape))
            v = F[:, at:at + n]
            return v if len(shape) == 1 else v.rearrange("p (a b) -> p a b", a=shape[0])

        XS, Z, BTOK, BT, CT = ov(0, TT, DI), ov(4096, TT, DI), ov(8192, TT, T), ov(10240, SG, T), ov(12288, SG, T)
        CV = [ov(14336, T), ov(14848, T)]
        SX = [ov(15360, T), ov(15872, T)]
        ST, XW, XD = fa(0, DI), fa(1024, DI), fa(2048, DI)
        MT = [fa(3072, 4, P), fa(3584, 4, P)]
        DQT, DKT = YA[:, 1], ov(14336, NH, T)
        DVT = YA[:, 0]
        CQT, CKVT, KPE, QN, QP, KN, VT = ov(0, 2, T), ov(1024, T), ov(1536, T), ov(2048, NH, T), ov(4096, NH, T), \
            ov(6144, NH, T), ov(8192, TT, T)
        PB = [ov(10240 + 512 * j, T) for j in range(4)]
        PT = ov(12288, TT, T)
        YT1, YT2, JSS = fa(4096, 512), fa(4608, 512), fa(5120, 256)
        ROT = fa(3072, T)
        DIST = fa(0, TT, T)
        SQB, RSB = fa(2048, T), fa(2560, T)
        POSR = fa(5632, T)
        ADS = [fa(3072, CH), fa(3584, CH)]
        HR = [fa(0, D), fa(1024, D), fa(2048, D)]
        JUNK1 = fa(3072, D)
        H2T, H2R = HT, [fa(4096, D), fa(5120, D), MOD[:, 1]]
        JUNK2 = MOD[:, 0]
        NW2, SNW = MOD[:, 0], MOD[:, 1]
        def rounded(name, region, first, *shape):
            return nc.alloc_sbuf_tensor_at(name, [P, *shape], F32R, offset=at[region] + 4 * first)

        def at_slot(j):
            return ("ring", j * CHE) if j < 2 else ("ov", (j - 2) * CHE)

        W_L = [rounded(f"w_low{j}", *at_slot(j), CHE) for j in range(6)]
        W_H = [rounded(f"w_high{k}", *(("f_area", 2048 * k) if k < 3 else ("mod", 0)), 2048) for k in range(4)]
        yaf = YA[:, :, :, :].rearrange("p a h t -> p (a h t)")
        htf = HT[:, :, :].rearrange("p k t -> p (k t)")
        HN_H, HN_L = rounded("hn_high", "ya", 0, KT, T), rounded("hn_low", "mod", 2 * D, KT, T)
        IN_H = [rounded(f"in_high{k}", "ov", 4096 + 2048 * k, 2048) for k in range(2)] + W_H[0:2]
        OUT_H = [rounded(f"out_high{k}", "ov", a, 4, CH) for k, a in enumerate((14336, 12288))]
        Y = [HT[:, 0:4], HT[:, 4:8], YA[:, 1], YA[:, 0]]
        Y_H = [rounded(f"y_high{k}", "f_area", 2048 * k, 4, T) for k in range(2)]
        Y_L = [rounded(f"y_low{k}", a, b, 4, T) for k, (a, b) in enumerate((("ht", 0), ("ht", 2048), ("ya", 2048), ("ya", 0)))]
        XG, YB = [MOD[:, 2], MOD[:, 3]], [htf[:, 3072:4096], MOD[:, 4]]
        GS, HH = htf[:, 2048:2560], htf[:, 2560:3072]
        XG_H, XG_L = ([rounded(f"x_{part}{s}", "ya", 2048 * s + 1024 * k, KT, P) for s in range(2)]
                      for k, part in enumerate(("high", "low")))
        HH_H, HH_L = ([rounded(f"h_{part}{s}", "ht", 1024 * s + 512 * k, 4, P) for s in range(2)]
                      for k, part in enumerate(("high", "low")))
        CB = [yaf[:, 0:2048], yaf[:, 2048:4096], htf[:, 0:2048], htf[:, 2048:4096]]

        ID, UU, SU, ONE = (CON[:, a:a + P] for a in (C_ID, C_U, C_SU, C_ONE))

        def sm(at, *shape):
            n = int(np.prod(shape))
            v = SM[:, at:at + n]
            if len(shape) == 2:
                v = v.rearrange("p (a b) -> p a b", a=shape[0])
            return v
        SS, MS, RS = sm(0, TT), sm(4, TT), sm(8, TT)
        DTT, ADT, ACS, NACS, EACS, DEND, ETOT, STMP = (sm(16 + 64 * k, TT, SH) for k in range(8))
        ANEG = sm(528, SH)
        MX, NB_, SE, RR = sm(544, 4), sm(548, 4), sm(552, 4), sm(556, 4)
        LAM, LT, SUBW = sm(560, 1), sm(561, 2), sm(563, 1)
        SSG, MSG, RSG = (sm(768 + 16 * k, TT, SG) for k in range(3))
        POSQ = sm(816, TT)
        ACST = F[0:TT * SH, 5376:5504]
        LPR = F[:, 5120:5248]
        ROWS = F[0:R_N, 5504:5632]
        CROW = F[0:KT, 4096:4224]
        RM, RV, RW, R1, R2, R3, R4 = (sm(576 + 4 * k, TT) for k in range(7))
        GL, GE, PEN = sm(608, TT, NG), sm(624, TT, NG), sm(640, TT, NG)
        RROW = sm(656, 2 * TT)
        EL, LM, OH1, OH2, MM, POS, BLK, TMPE, ROWF = (YA[:, 1, k // 4, 128 * (k % 4):128 * (k % 4) + 128]
                                                      .rearrange("p (t e) -> p t e", t=TT) for k in range(9))
        OVE = YA[:, 1, 3, 32:64]
        OVR = YA[0:32, 1, 3, 128:256]
        OVT = YA[0:32, 1, 3, 256:260]
        NPF = YA[0:1, 1, 3, 264:280]
        KCMP = YA[0:1, 1, 2, 256:512].rearrange("p (k e) -> p k e", k=8)

        PS = [ctx.enter_context(nc.psum_tensor(f"bank{b}", [P, 512], F32)) for b in range(8)]

        s_load = [sem(f"s_load{j}") for j in range(6)]
        s_par = sem("s_par")
        s_par2 = sem("s_par2")
        s_bada = sem("s_bada")
        s_mrow = sem("s_mrow")
        s_msum = sem("s_msum")
        s_mcol = sem("s_mcol")
        s_hm = sem("s_hm")
        s_hnl = sem("s_hnl")
        s_late = sem("s_late")
        s_tblini = sem("s_tblini")
        s_acc = sem("s_acc")
        s_accf = [sem("s_accf0"), sem("s_accf1")]
        s_tr = sem("s_tr")
        s_trf = [sem("s_trf0"), sem("s_trf1")]
        s_dch = sem("s_dch")
        s_ach = sem("s_ach")
        s_pch = sem("s_pch")
        s_ms = sem("s_ms")
        s_rs = sem("s_rs")
        s_hr = sem("s_hr")
        s_conv = sem("s_conv")
        s_sx = sem("s_sx")
        s_dt1 = sem("s_dt1")
        s_dt2 = sem("s_dt2")
        s_lam = sem("s_lam")
        s_adt = sem("s_adt")
        s_acs = sem("s_acs")
        s_dec = sem("s_dec")
        s_xw = sem("s_xw")
        s_cb = sem("s_cb")
        s_mx = sem("s_mx")
        s_mt = sem("s_mt")
        s_yd = sem("s_yd")
        s_st = sem("s_st")
        s_ydf = sem("s_ydf")
        s_ste = sem("s_ste")
        s_yn = sem("s_yn")
        s_ssg = sem("s_ssg")
        s_msg = sem("s_msg")
        s_rsg = sem("s_rsg")
        s_ynn = sem("s_ynn")
        s_pos = sem("s_pos")
        s_sc = sem("s_sc")
        s_scf = sem("s_scf")
        s_nb = sem("s_nb")
        s_ex = sem("s_ex")
        s_at = sem("s_at")
        s_tp = sem("s_tp")
        s_pt = sem("s_pt")
        s_pv = sem("s_pv")
        s_sq = sem("s_sq")
        s_rst = sem("s_rst")
        s_ya = sem("s_ya")
        s_csq = sem("s_csq")
        s_crs = sem("s_crs")
        s_cn = sem("s_cn")
        s_kpe = sem("s_kpe")
        s_qpr = sem("s_qpr")
        s_yh = sem("s_yh")
        s_yl = sem("s_yl")
        s_wh = sem("s_wh")
        s_wl = sem("s_wl")
        s_ou = sem("s_ou")
        s_o = sem("s_o")
        s_xr = sem("s_xr")
        s_res = sem("s_res")
        s_ss2 = sem("s_ss2")
        s_h2 = sem("s_h2")
        s_h2st = sem("s_h2st")
        s_nt = sem("s_nt")
        s_ntf = sem("s_ntf")
        s_lg = sem("s_lg")
        s_ge = sem("s_ge")
        s_gf = sem("s_gf")
        s_oh = sem("s_oh")
        s_pp = sem("s_pp")
        s_ovt = sem("s_ovt")
        s_ov2 = sem("s_ov2")
        s_eid = sem("s_eid")
        s_row = sem("s_row")
        s_tbl = sem("s_tbl")
        s_xt = sem("s_xt")
        s_xh = sem("s_xh")
        s_xl = sem("s_xl")
        s_unit = sem("s_unit")
        s_hi = sem("s_hi")
        s_lo = sem("s_lo")
        s_zu = sem("s_zu")
        s_z = sem("s_z")
        s_zf = sem("s_zf")
        s_hnh = sem("s_hnh")
        s_inh = sem("s_inh")
        s_inl = sem("s_inl")
        s_gs = sem("s_gs")
        s_hh = sem("s_hh")
        s_htp = sem("s_htp")
        s_hth = sem("s_hth")
        s_htl = sem("s_htl")
        s_ye = sem("s_ye")
        s_slot = [sem("s_slot0"), sem("s_slot1")]
        s_all = sem("s_all")
        s_cmb = [sem(f"s_cmb{t}") for t in range(TT)]
        s_gd = [kept_sem("s_gd0"), kept_sem("s_gd1")]
        s_sd = [kept_sem("s_sd0"), kept_sem("s_sd1")]
        s_disp = [kept_sem(f"s_disp{k}") for k in range(8)]
        s_end = kept_sem("s_end")
        s_clr = kept_sem("s_clr")
        s_con = kept_sem("s_con")
        s_x0 = kept_sem("s_x0")
        s_pro = kept_sem("s_pro")
        s_proa = kept_sem("s_proa")
        s_prod = kept_sem("s_prod")
        s_ada = [kept_sem(f"s_ada{j}") for j in range(2)]
        s_ssx = kept_sem("s_ssx")
        s_msx = kept_sem("s_msx")
        s_rsx = kept_sem("s_rsx")
        s_prov = kept_sem("s_prov")
        s_fout = kept_sem("s_fout")
        s_fw = kept_sem("s_fw")
        s_fst = kept_sem("s_fst")
        s_tick = kept_sem("s_tick")

        block = ctx.enter_context(nc.Block())

        N_PAR, N_PAR2 = 16 * 7, 16 * 10

        def acc_bank(name):
            n = ACC[name]
            return PS[n % 2], s_accf[n % 2], n // 2 + 1

        def tr_bank(name):
            n = TRN[name]
            return PS[2 + n % 2], s_trf[n % 2], n // 2 + 1

        def evacuated(eng, name):
            _, free, k = acc_bank(name)
            eng.wait_ge(free, k)

        def turned_out(eng, name):
            _, free, k = tr_bank(name)
            eng.wait_ge(free, k)

        def flat(v):
            return v.rearrange("p a b -> p (a b)")

        def last_group(n):
            name = CHUNKS[n]
            if name == "U":
                return s_acc, ACC[("V", 3)] + 1
            if name[0] == "A":
                return s_acc, ACC[name] + 1
            if name[0] == "O":
                return (s_ou, 2 * name[1] + 2) if name[1] < 3 else (s_o, TT)
            j = name[1]
            if j in (4, 5):
                return s_z, 4 * (j - 3)
            tile = (("X", 4 * j + 3) if j < 4 else
                    (("DQ", "DK", "DV")[j - 6], 3) if j < 9 else ("C", 3))
            return s_acc, ACC[tile] + 1

        def tiles4(bank):
            return bank[:, :].rearrange("p (k j) -> p k j", k=4)

        def unit_of(buf, v, half=None):
            if half is None:
                return buf[:, :].rearrange("p (k n) -> p k n", k=4)
            if v % UNITS < 8:
                return buf[:, half * 2048:(half + 1) * 2048].rearrange("p (k n) -> p k n", k=4)
            return buf[:, :].rearrange("p (k n) -> p k n", k=4)[:, :, half * CH:(half + 1) * CH]

        def out_half(buf, v):
            return buf[:, :].rearrange("p (f n) -> p f n", f=4)[:, :, (v % 2) * CH:(v % 2 + 1) * CH]

        def in_half(buf, u):
            if u >= X_UNITS:
                return buf[:, (u % 2) * 2048:(u % 2 + 1) * 2048].rearrange("p (k n) -> p k n", k=4)
            return buf[:, :].rearrange("p (k n) -> p k n", k=KT)[:, :, (u % 2) * 256:(u % 2) * 256 + 256]

        def in_place(u):
            if u >= X_UNITS:
                return IN_H[2 + u % 2][:, :].rearrange("p (k n) -> p k n", k=4)
            return IN_H[u % 2][:, :].rearrange("p (k n) -> p k n", k=KT)

        def in_slot(u):
            return chunk_slot(CHN[("I", u // 2)])

        def down_bank(v):
            return PS[(5, 6, 7, 5)[v - 8]]

        def more_pairs(eng):
            eng.wait_ge(s_eid, 1)
            return eng.value_load(EID[0:1, 41:42], min_val=15, max_val=PAIRS_MAX - 1)

        @block.sync
        def _(sp):
            sp.dma_start(CON[:, :], k_const).then_inc(s_con, 16)
            sp.dma_start(CROW, c.rearrange("a (k p) -> (a k) p", p=P)).then_inc(s_con, 16)
            sp.dma_start(EID[:, :], k_eid).then_inc(s_con, 16)
            sp.dma_start(PAY[:, :, :, :].rearrange("p t s w -> p (t s w)"), k_pay).then_inc(s_con, 16)
            sp.dma_start(SM[:, 304:816].bitcast(I32), positions.partition_broadcast(P)).then_inc(s_con, 16)
            sp.dma_start(X[:, :, :], x.rearrange("a (t p) d -> p (a t) d", p=P)).then_inc(s_x0, 16)

            def load_ada(layer, j):
                sp.dma_start(SLOT[2 + j].rearrange("p (k n) -> p k n", k=KT),
                             w_ada[layer, :, j * CH:(j + 1) * CH].rearrange("a (k p) n -> p (a k) n", p=P)).then_inc(s_ada[j], 16)

            for j in range(2):
                load_ada(slice(0, 1), j)
            sp.wait_ge(s_prod, 1)

            with sp.Fori(0, L) as l:
                def rows(w, o, n):
                    return w[bass.ds(l, 1), :, o:o + n].rearrange("a (k p) n -> p (a k) n", p=P)

                def load_chunk(n):
                    name, dst, landed = CHUNKS[n], SLOT[chunk_slot(n)], s_load[chunk_slot(n)]
                    if n >= 6:
                        sp.wait_ge(*last_group(n - 2))
                    tiles = dst.rearrange("p (k n) -> p k n", k=KT)
                    if name[0] == "A":
                        sp.dma_start(tiles, rows(w_ada, name[1] * CH, CH)).then_inc(landed, 16)
                    elif name == ("I", 9):
                        for a, b, o in ((0, 448, 0), (448, 480, 416), (480, 512, 384)):
                            sp.dma_start(tiles[:, :, a:b], rows(w_in, o, b - a)).then_inc(landed, 16)
                    elif name[0] == "I":
                        sp.dma_start(tiles, rows(w_in, IN_COLS[name[1]], CH)).then_inc(landed, 16)
                    elif name == "U":
                        uq = dst[:, 0:2048].rearrange("p (k h n) -> p k h n", k=2, h=NH)
                        for k in range(2):
                            src = mla_w_uq[bass.ds(l, 1), k * P:(k + 1) * P, :].rearrange("a p (h n) -> (a p) h n", h=NH)
                            for a, b, o in ((0, 192, 0), (192, 224, 160), (224, 256, 128)):
                                sp.dma_start(uq[:, k, :, a:b], src[:, :, o:o + b - a]).then_inc(landed, 16)
                        sp.dma_start(dst[:, 2048:3072],
                                     mla_w_ukv[bass.ds(l, 1)].rearrange("a p n -> (a p) n")).then_inc(landed, 16)
                    else:
                        j = name[1]
                        sp.dma_start(dst.rearrange("p (f n) -> p f n", f=4),
                                     w_out[bass.ds(l, 1), OUT_ROWS[j] * 512:(OUT_ROWS[j] + 1) * 512, :]
                                     .rearrange("a (f p) n -> p (a f) n", p=P)).then_inc(landed, 16)

                small = [(ROWS[R_NW1:R_NW1 + 8, :], norm1_w[bass.ds(l, 1)].rearrange("a (m p) -> (a m) p", p=P)),
                         (ROWS[R_BADA:R_BADA + 16, :], b_ada[bass.ds(l, 1), 0:2 * D].rearrange("a (m p) -> (a m) p", p=P)),
                         (ROWS[R_CW:R_CW + 64, :], ssd_conv_w[bass.ds(l, 1)].rearrange("a k (m p) -> (a k m) p", p=P)),
                         (ROWS[R_CB:R_CB + 16, :], ssd_conv_b[bass.ds(l, 1)].rearrange("a (m p) -> (a m) p", p=P)),
                         (ROWS[R_QN:R_QN + 2, :], mla_q_norm_w[bass.ds(l, 1)].rearrange("a (m p) -> (a m) p", p=P)),
                         (ROWS[R_KN:R_KN + 1, :], mla_kv_norm_w[bass.ds(l, 1)]),
                         (ROWS[R_SUB:R_SUB + 1, :], diff_subln_w[bass.ds(l, 1)]),
                         (BC[:, B_LAM:B_LAM + 256], diff_lambda[bass.ds(l, 1)].rearrange("a k d -> a (k d)").partition_broadcast(P)),
                         (WDT[:, :, :], rows(w_in, O_DT, SH)),
                         (WR[:, :, 0:NG], rows(router_w_group, 0, NG)),
                         (WR[:, :, NG:], rows(router_w_expert, 0, NE))]
                for at, n, w in ((B_DTB, SH, ssd_dt_bias), (B_ALOG, SH, ssd_a_log), (B_D, SH, ssd_d),
                                 (B_RB, NG, router_b_group), (B_RB + NG, NE, router_b_expert), (B_LI, 2, k_lam)):
                    small.append((BC[:, at:at + n], w[bass.ds(l, 1)].partition_broadcast(P)))
                assert 16 * len(small) == N_PAR + N_PAR2
                load_chunk(2)
                load_chunk(3)
                for k, (dst, src) in enumerate(small):
                    if 16 * k == N_PAR:
                        load_chunk(4)
                        load_chunk(5)
                    sp.dma_start(dst, src).then_inc(s_par if 16 * k < N_PAR else s_par2, 16)
                def load_bias(a, b):
                    sp.dma_start(MOD[:, a:b, :].rearrange("p a n -> p (a n)"),
                                 b_ada[bass.ds(l, 1), a * D:b * D].partition_broadcast(P)).then_inc(s_bada, 16)

                sp.dma_start(POSR.bitcast(I32), positions.partition_broadcast(P)).then_inc(s_pos, 16)
                sp.dma_start(TBL[:, :, :].rearrange("p k w -> p (k w)"), k_table).then_inc(s_tblini, 16)
                sp.wait_ge(s_tblini, 16)
                sp.dma_start(slot_table.rearrange("(p k) w -> p (k w)", p=P),
                             TBL[:, :, :].rearrange("p k w -> p (k w)")).then_inc(s_tblini, 16)
                for n in range(6, 8):
                    load_chunk(n)
                sp.wait_ge(s_mcol, 4)
                sp.dma_start(NW2, norm2_w[bass.ds(l, 1)].partition_broadcast(P)).then_inc(s_late, 16)
                sp.dma_start(SNW, ssd_norm_w[bass.ds(l, 1)].partition_broadcast(P)).then_inc(s_late, 16)
                for n in range(8, NCH):
                    load_chunk(n)
                    if n == CHN[("I", 7)]:
                        load_bias(2, 6)

                def load_expert(m, e):
                    slot, kind = (m + 2) % 6, (0, 1, 0, 1, 2, 2)[m]
                    w = (exp_w_gate, exp_w_up, exp_w_down)[kind][bass.ds(l, 1), bass.ds(e, 1)]
                    sp.dma_start(SLOT[slot].rearrange("p (k n) -> p k n", k=4 if kind == 2 else KT),
                                 w.rearrange("a b (k p) n -> p (a b k) n", p=P)).then_inc(s_load[slot], 16)

                sp.wait_ge(s_ya, 2 * NH)
                for m in range(3):
                    load_expert(m, (0, 0, 1)[m])
                for t in range(TT):
                    sp.wait_ge(s_h2, t + 1)
                    sp.dma_start(h2_rows[t * P:(t + 1) * P, :], H2R[t % 3]).then_inc(s_h2st, 16)
                    sp.wait_ge(s_h2st, 16 * (t + 1))
                for m in (4, 5, 3):
                    load_expert(m, (0, 1, 1)[(4, 5, 3).index(m)])
                for q in s_disp:
                    sp.wait_ge(q, 16)
                sp.dma_start(TBL[:, :, :].rearrange("p k w -> p (k w)"),
                             slot_table.rearrange("(p k) w -> p (k w)", p=P)).then_inc(s_tbl, 16)
                more = more_pairs(sp)
                with sp.Fori(0, more) as i:
                    e = [sp.value_load(EID[0:1, bass.ds(i * 2 + (2 + s), 1)], min_val=0, max_val=NE - 1) for s in range(2)]
                    for m in range(6):
                        s = (0, 0, 1, 1, 0, 1)[m]
                        sp.wait_ge(s_unit, i * UNITS + (2 * m + 2))
                        load_expert(m, e[s])
                sp.wait_ge(s_all, 1)
                for t in range(TT):
                    sp.dma_start(CB[t], expert_rows[t * 2 * P:(t + 1) * 2 * P, :].rearrange("(p s) d -> p (s d)", s=2)).then_inc(s_cmb[t], 16)
                following = sp.value_load(EID[0:1, bass.ds(l + NEXT_LAYER, 1)], min_val=0, max_val=L - 1)
                for j in range(2):
                    load_ada(bass.ds(following, 1), j)
                sp.sem_inc(s_end, 1)
                sp.wait_ge(s_end, l * 5 + 5)
                sp.sem_inc(s_tick, 1)
                for q in layer_sems:
                    sp.sem_clear(q)
                sp.sem_inc(s_clr, 1)
            sp.dma_start(MOD[:, 0], final_norm_w.rearrange("(a d) -> a d", a=1).partition_broadcast(P)).then_inc(s_fw, 16)
            for t in range(TT):
                sp.wait_ge(s_fout, t + 1)
                sp.dma_start(out[0, t * P:(t + 1) * P, :], X[:, t, :]).then_inc(s_fst, 16)
            sp.wait_ge(s_fst, 16 * TT)
            for q in s_ada:
                sp.wait_ge(q, 16 * (L + 1))

        @block.gpsimd
        def _(pool):
            pool.wait_ge(s_con, 80)
            half = CON[:, C_HALF:C_HALF + 1]

            def rstd(dst, src, n, done):
                pool.tensor_tensor(dst, src, half.broadcast_to([P, n]), ALU.pow).then_inc(done, 1)

            pool.wait_ge(s_msx, 1)
            rstd(RS, MS, TT, s_rsx)
            with pool.Fori(0, L) as l:
                for cc in range(TT):
                    pool.wait_ge(s_msg, cc + 1)
                    rstd(RSG[:, cc, :], MSG[:, cc, :], SG, s_rsg)
                for t in range(TT):
                    pool.wait_ge(s_ms, t + 1)
                    rstd(RS[:, t:t + 1], MS[:, t:t + 1], 1, s_rs)
                pool.wait_ge(s_tblini, 32)
                pool.wait_ge(s_oh, 1)
                for s in range(2):
                    pool.memset(XG[s], 0.0).then_inc(s_pch, 1)
                pool.wait_ge(s_pch, 2)
                pool.wait_ge(s_row, 1)
                for t in range(TT):
                    for s in range(2):
                        k = 2 * t + s
                        pool.indirect_dma_start(slot_table, bass.IndirectOffsetOnAxis(ap=ROWI[:, k:k + 1], axis=0), PAY[:, t, s, :], None,
                                                bounds_check=P * NB_MAX - 1, oob_is_err=False).then_inc(s_disp[k], 16)
                pool.wait_ge(s_tbl, 16)
                pool.wait_ge(s_h2st, 16 * TT)

                def gather(s):
                    pool.indirect_dma_start(XG[s], None, h2_rows, bass.IndirectOffsetOnAxis(ap=GIDX[s][:, 0:1], axis=0),
                                            bounds_check=T - 1, oob_is_err=False).then_inc(s_gd[s], 16)

                for s in range(2):
                    pool.tensor_copy(GIDX[s][:, :], TBL[:, s, 0:1].bitcast(U32)).then_inc(s_pch, 1)
                    pool.tensor_copy(SIDX[s][:, 0:3], TBL[:, s, 0:3].bitcast(U32)).then_inc(s_slot[s], 1)
                for s in range(2):
                    pool.wait_ge(s_pch, 3 + s)
                    gather(s)
                more = more_pairs(pool)

                def after(q, value):
                    pool.wait_ge(q, value)
                    pool.sem_inc(s_tick, 1)

                def gather_next(s, col, count):
                    pool.tensor_copy(GIDX[s][:, :], TBL[:, bass.ds(col, 1), 0:1].rearrange("p a b -> p (a b)").bitcast(U32)).then_inc(s_pch, 1)
                    after(s_pch, count + 1)
                    gather(s)

                def scatter(i, s):
                    after(s_ye, i * 4 + (2 * s + 3))
                    pool.indirect_dma_start(expert_rows, bass.IndirectOffsetOnAxis(ap=SIDX[s][:, 1:2], axis=0), YB[s], None,
                                            bounds_check=2 * T - 1, oob_is_err=False).then_inc(s_sd[s], 16)

                for s in range(2):
                    pool.wait_ge(s_xt, s + 1)
                    pool.tensor_copy(GIDX[s][:, :], TBL[:, 2 + s, 0:1].bitcast(U32)).then_inc(s_pch, 1)
                    pool.wait_ge(s_pch, 5 + s)
                    gather(s)
                with pool.Fori(0, more) as i:
                    after(s_xt, i * 2 + 3)
                    gather_next(0, i * 2 + 4, i * 2 + 6)
                    scatter(i, 0)
                    scatter(i, 1)
                    after(s_xt, i * 2 + 4)
                    gather_next(1, i * 2 + 5, i * 2 + 7)
                    for s in range(2):
                        after(s_sd[s], i * 16 + 16)
                        pool.tensor_copy(SIDX[s][:, 0:3], TBL[:, bass.ds(i * 2 + (2 + s), 1), 0:3]
                                         .rearrange("p a b -> p (a b)").bitcast(U32)).then_inc(s_slot[s], 1)
                for s in range(2):
                    after(s_slot[s], more + 1)
                    scatter(more, s)
                for s in range(2):
                    after(s_sd[s], more * 16 + 16)
                    after(s_gd[s], more * 16 + 32)
                pool.sem_inc(s_all, 1)
                for q in (*s_gd, *s_sd, *s_disp):
                    pool.dma_reset(range(q.num, q.num + 1))
                    pool.sem_clear(q)
                after(s_msx, l + 2)
                rstd(RS, MS, TT, s_rsx)
                pool.sem_inc(s_end, 1)
                after(s_clr, l + 1)

        @block.scalar
        def _(act):
            act.wait_ge(s_pro, 1)
            act.activation(COND[:, :], PS[2][:, 0:KT], ACT.Silu).then_inc(s_proa, 1)
            act.wait_ge(s_x0, 16)
            for t in range(TT):
                if t:
                    act.wait_ge(s_ssx, t)
                act.activation(JUNK1, X[:, t, :], ACT.Square, accum_out=SS[:, t:t + 1]).then_inc(s_ssx, 1)
            act.wait_ge(s_prod, 1)
            act.activation(TRIG[:, :], TRIG[:, :], ACT.Sin).then_inc(s_proa, 1)


            with act.Fori(0, L) as l:
                chain = [0]

                def link(ins):
                    chain[0] += 1
                    ins.then_inc(s_ach, 1)
                    act.wait_ge(s_ach, chain[0])

                def acc_ready(name):
                    act.wait_ge(s_acc, ACC[name] + 1)
                    return acc_bank(name)

                def tr_ready(name):
                    act.wait_ge(s_tr, TRN[name] + 1)
                    return tr_bank(name)

                for t in range(TT):
                    for q in range(2):
                        bank, free, _ = tr_ready(("H", t, q))
                        act.activation(HT[:, 4 * q:4 * q + 4, t * P:(t + 1) * P], tiles4(bank), ACT.Copy).then_inc(free, 1)
                for j in (0, 2):
                    bank, free, k = acc_ready(("A", j))
                    act.activation(MOD[:, j // 2, (j % 2) * CH:(j % 2 + 1) * CH], bank[:, :], ACT.Copy).then_inc(free, 1)
                    act.wait_ge(free, k)
                    act.sem_inc(s_mrow, 1)
                bank, free, _ = tr_ready("P")
                act.activation(COLS[:, :], bank[:, 0:R_N], ACT.Copy).then_inc(free, 1)

                def in_high(u):
                    if u % 2 == 0:
                        n = CHN[("I", u // 2)]
                        act.wait_ge(s_load[chunk_slot(n)], slot_count(n))
                    if 2 <= u < X_UNITS:
                        act.wait_ge(s_acc, ACC[("X", 2 * u - 3)] + 1)
                    elif u == 10:
                        act.wait_ge(s_zu, 1)
                    elif u == 11:
                        act.wait_ge(s_z, TT)
                    act.activation(in_place(u), in_half(SLOT[in_slot(u)], u), ACT.Copy).then_inc(s_inh, 1)

                act.wait_ge(s_mcol, 4)
                in_high(0)
                for k in range(KT):
                    act.wait_ge(s_hm, k + 1)
                    act.activation(HN_H[:, k, :], HT[:, k, :], ACT.Copy).then_inc(s_hnh, 1)
                in_high(1)
                for m in range(16):
                    if 1 <= m <= 12:
                        bank, free, _ = tr_ready(("T", m - 1))
                        dst = XS[:, :, (m - 1) * P:m * P] if m <= 8 else BTOK[:, :, (m - 9) * P:(m - 8) * P]
                        act.activation(dst, bank[:, :].rearrange("p (t n) -> p t n", t=TT), ACT.Copy).then_inc(free, 1)
                    act.wait_ge(s_conv, m + 1)
                    dst = SX[m % 2] if m < 8 else (BT, CT)[m // 12][:, m % 4, :]
                    act.activation(dst, CV[m % 2], ACT.Silu).then_inc(s_sx, 1)
                    if m % 2:
                        in_high(m // 2 + 2)
                in_high(10)
                for m in range(8):
                    act.wait_ge(s_z, m + 1)
                    act.activation(Z[:, m % 4, (m // 4) * CH:(m // 4 + 1) * CH], PS[4 + m % 4][:, :], ACT.Silu).then_inc(s_zf, 1)
                    if m == 3:
                        in_high(11)
                act.preload_act_table_set("natural_log_exp_and_others")
                act.wait_ge(s_dt1, 1)
                act.activation(ANEG, BC[:, B_ALOG:B_ALOG + SH], ACT.Exp)
                link(act.activation(flat(ACS), flat(DTT), ACT.Abs))
                link(act.activation(flat(NACS), flat(ACS), ACT.Exp, scale=-1.0))
                act.activation(flat(EACS), flat(NACS), ACT.Ln, bias=1.0).then_inc(s_dt2, 1)
                act.wait_ge(s_lam, 1)
                act.activation(LT, LT, ACT.Exp).then_inc(s_dt2, 1)
                act.wait_ge(s_acs, 1)
                act.activation(flat(EACS), flat(ACS), ACT.Exp)
                act.activation(flat(DEND), flat(STMP), ACT.Exp)
                act.activation(flat(ETOT), flat(ETOT), ACT.Exp).then_inc(s_dec, 1)
                bank, free, _ = tr_ready("AT")
                act.activation(ACST, bank[0:TT * SH, 0:P], ACT.Copy).then_inc(free, 1)

                def squares(cc, hf):
                    act.wait_ge(s_yn, 2 * cc + hf + 1)
                    for q in range(2):
                        g = 2 * hf + q
                        link(act.activation(JSS, Z[:, cc, 256 * g:256 * g + 256], ACT.Square, accum_out=SSG[:, cc, g:g + 1]))
                    act.sem_inc(s_ssg, 1)

                def fill_out(k):
                    name, m = SSD_FILL[k]
                    bank, free, _ = acc_ready((name, m))
                    act.activation({"DQ": DQT, "DK": DKT, "DV": DVT}[name][:, m, :], bank[:, :], ACT.Copy).then_inc(free, 1)

                for cc in range(TT):
                    for g in range(SG):
                        n = 4 * cc + g
                        bank, free, k = acc_ready(("R", cc, g))
                        if n >= 2:
                            act.wait_ge(s_yd, n - 1)
                        for h in range(4):
                            ins = act.activation(MT[g % 2][:, h, :], bank[:, h * P:(h + 1) * P], ACT.Exp,
                                                 bias=NACS[:, cc, 4 * g + h:4 * g + h + 1])
                        ins.then_inc(free, 1)
                        act.wait_ge(free, k)
                        act.sem_inc(s_mx, 1)
                        if g in (1, 3):
                            fill_out(3 * cc + g // 2)
                        if n >= 2 and g == 3:
                            squares(cc, 0)
                        if cc >= 1 and g == 1:
                            squares(cc - 1, 1)
                    fill_out(3 * cc + 2)
                squares(TT - 1, 1)

                def exps(base, u, width, scale):
                    for m in range(width):
                        b, n = (width * u + m) % 4, (u % 4 + 1) * P
                        act.wait_ge(s_nb, base + width * u + m + 1)
                        link(act.activation(PB[b][:, 0:n], PB[b][:, 0:n], ACT.Exp, bias=NB_[:, b:b + 1], scale=scale,
                                            accum_out=SE[:, b:b + 1]))
                        act.sem_inc(s_ex, 1)

                def turned(k):
                    i = k % 4
                    act.wait_ge(s_tp, k + 1)
                    if i == 0 and k >= 4:
                        act.wait_ge(s_pv, k // 4)
                    act.activation(PT[:, 0:i + 1, i * P:(i + 1) * P],
                                   PS[6][:, 0:(i + 1) * P].rearrange("p (j q) -> p j q", j=i + 1), ACT.Copy).then_inc(s_pt, 1)

                def rms_rows(name, n, eps, done):
                    bank, free, k = acc_ready(name)
                    act.activation(RSB, bank[:, :], ACT.Ln, scale=1.0 / n, bias=eps).then_inc(free, 1)
                    act.wait_ge(free, k)
                    act.activation(RSB, RSB, ACT.Exp, scale=-0.5).then_inc(done, 1)

                for u in range(20):
                    if u < 16:
                        exps(0, u, 2, DIFF_SCALE)
                    if 2 <= u < 18:
                        turned(u - 2)
                    if u >= 6 and u % 4 == 2:
                        act.wait_ge(s_pv, (u - 2) // 4)
                        act.activation(SQB, PS[7][:, :], ACT.Square).then_inc(s_sq, 1)
                    if head_ends(u):
                        h = (u - 7) // 4
                        if h >= 1:
                            act.wait_ge(s_ya, h)
                        rms_rows(("DS", h), DV, SUBEPS, s_rst)
                def ssd_output(cc):
                    for q in range(2):
                        bank, free, _ = tr_ready(("Y", cc, q))
                        act.activation(HT[:, 4 * q:4 * q + 4, cc * P:(cc + 1) * P], tiles4(bank), ACT.Copy).then_inc(free, 1)

                act.wait_ge(s_ya, NH)
                for m, dst in ((0, SQB), (1, PB[0])):
                    evacuated(act, ("C", m))
                    act.activation(dst, CQT[:, m, :], ACT.Square).then_inc(s_csq, 1)
                ssd_output(0)
                rms_rows("SQ", MQ, EPS, s_crs)
                evacuated(act, ("C", 2))
                act.activation(SQB, CKVT, ACT.Square).then_inc(s_csq, 1)
                ssd_output(1)
                act.wait_ge(s_cn, 1)
                rms_rows("SK", MKV, EPS, s_crs)
                ssd_output(2)
                ssd_output(3)
                for name, dst in (("QN", QN), ("KN", KN), ("V", VT)):
                    for m in range(4):
                        bank, free, _ = acc_ready((name, m))
                        act.activation(dst[:, m, :], bank[:, :], ACT.Copy).then_inc(free, 1)
                def inputs_high(j):
                    if j >= 2:
                        act.wait_ge(s_ou, 2 * j - 2)
                        act.wait_ge(s_ya, 2 * NH)
                    act.activation(Y_H[j % 2][:, :, :], Y[j], ACT.Copy).then_inc(s_yh, 1)

                def out_high(v):
                    n = CHN[("O", v // 2)]
                    if v % 2 == 0:
                        act.wait_ge(s_load[n % 2], slot_count(n))
                    if v >= 2:
                        act.wait_ge(s_ou, v - 1)
                    act.activation(OUT_H[v % 2][:, :, :], out_half(SLOT[n % 2], v), ACT.Copy).then_inc(s_wh, 1)

                for u in range(18):
                    if u < 16:
                        exps(32, u, 1, MLA_SCALE)
                    if u >= 2:
                        turned(16 + u - 2)
                    if u == 15:
                        inputs_high(0)
                    if u == 16:
                        out_high(0)
                act.wait_ge(s_pv, 2 * NH)
                out_high(1)
                inputs_high(1)
                for j in range(1, 4):
                    out_high(2 * j)
                    out_high(2 * j + 1)
                    if j < 3:
                        inputs_high(j + 1)
                def feature_major2(t):
                    act.wait_ge(s_nt, t + 1)
                    for q in range(2):
                        ins = act.activation(H2T[:, 4 * q:4 * q + 4, t * P:(t + 1) * P],
                                             PS[2 * t + q][:, :].rearrange("p (k t) -> p k t", k=4), ACT.Copy)
                    ins.then_inc(s_ntf, 1)

                for t in range(TT):
                    act.wait_ge(s_xr, t + 1)
                    link(act.activation(JUNK2, X[:, t, :], ACT.Square, accum_out=SS[:, t:t + 1]))
                    act.sem_inc(s_ss2, 1)
                    if t >= 1:
                        feature_major2(t - 1)
                feature_major2(TT - 1)
                act.wait_ge(s_ge, 1)
                act.activation(flat(GE), flat(GE), ACT.Exp).then_inc(s_gf, 1)
                act.wait_ge(s_ge, 2)
                act.activation(RW, RW, ACT.Exp).then_inc(s_gf, 1)
                def high(i, v):
                    slot, half, kind = unit_matrix(v % UNITS)
                    if half == 0:
                        act.wait_ge(s_load[slot], i * 16 + (SLOT_BASE[slot] + 16 * (1 + v // UNITS)))
                    if v >= 4:
                        act.wait_ge(s_unit, i * UNITS + (v - 3))
                    act.activation(unit_of(W_H[v % 4], v), unit_of(SLOT[slot], v, half), ACT.Copy).then_inc(s_hi, 1)

                def rows_high(s, count):
                    act.wait_ge(s_xt, count)
                    act.activation(XG_H[s][:, 0:4, :], tiles4(PS[0]), ACT.Copy)
                    act.activation(XG_H[s][:, 4:8, :], tiles4(PS[1]), ACT.Copy).then_inc(s_xh, 1)

                def hidden_high(s, count):
                    act.wait_ge(s_htp, count)
                    act.activation(HH_H[s][:, :, :], tiles4(PS[4]), ACT.Copy).then_inc(s_hth, 1)

                def gate(i, s):
                    act.wait_ge(s_unit, i * UNITS + (4 * s + 2))
                    act.activation(GS, PS[2][:, :], ACT.Silu).then_inc(s_gs, 1)

                def pair(i, ahead):
                    high(i, 4)
                    gate(i, 0)
                    rows_high(1, i * 2 + 2)
                    for v in (5, 6, 7, 8):
                        high(i, v)
                    hidden_high(0, i * 2 + 1)
                    gate(i, 1)
                    for v in (9, 10, 11):
                        high(i, v)
                    hidden_high(1, i * 2 + 2)
                    if ahead:
                        high(i, 12)
                        rows_high(0, i * 2 + 3)
                        for v in (13, 14, 15):
                            high(i, v)

                act.wait_ge(s_h2st, 16 * TT)
                for v in range(4):
                    high(0, v)
                more = more_pairs(act)
                rows_high(0, 1)
                with act.Fori(0, more) as i:
                    pair(i, True)
                pair(more, False)
                for t in range(TT):
                    act.wait_ge(s_res, t + 1)
                    act.wait_ge(s_ssx, l * TT + (TT + t))
                    act.activation(JUNK1, X[:, t, :], ACT.Square, accum_out=SS[:, t:t + 1]).then_inc(s_ssx, 1)
                act.sem_inc(s_end, 1)
                act.wait_ge(s_clr, l + 1)
                act.sem_inc(s_tick, 1)

        @block.vector
        def _(dve):
            own = [0]

            def olink(ins):
                own[0] += 1
                ins.then_inc(s_prov, 1)
                dve.wait_ge(s_prov, own[0])

            dve.wait_ge(s_con, 80)
            dve.tensor_copy(IDB[:, :], ID)
            dve.tensor_scalar(CMB[:, :], UU, -1.0, -NEG, ALU.add, ALU.mult)
            angle, turns, posf = F[:, 0:T], F[:, T:2 * T], F[:, 2 * T:3 * T]
            olink(dve.tensor_copy(posf, SM[:, 304:816].bitcast(I32)))
            for t in range(TT):
                dve.tensor_tensor(F[:, 3 * T + t * P:3 * T + (t + 1) * P], posf[:, t * P:(t + 1) * P], ID, ALU.mult)
            olink(dve.tensor_scalar(angle, posf, CON[:, C_INV:C_INV + 1], None, ALU.mult))
            dve.tensor_reduce(POSQ, F[:, 3 * T:4 * T].rearrange("p (t q) -> p t q", t=TT), AX, ALU.add)
            olink(dve.tensor_scalar(turns, angle, 1.0 / (2 * math.pi), CON[:, C_PH:C_PH + 1], ALU.mult, ALU.add))
            olink(dve.tensor_scalar(turns, turns, 12582912.0, None, ALU.add))
            olink(dve.tensor_scalar(turns, turns, -12582912.0, None, ALU.add))
            c1 = 6.28125
            c2 = float(np.float32(np.round((2 * math.pi - c1) * 2 ** 22) / 2 ** 22))
            c3 = 2 * math.pi - c1 - c2
            for part in (c1, c2, c3):
                olink(dve.scalar_tensor_tensor(angle, turns, -part, angle, ALU.mult, ALU.add))
            olink(dve.tensor_scalar(turns[:, 0:1], CON[:, C_PH:C_PH + 1], 2 * math.pi, None, ALU.mult))
            olink(dve.tensor_scalar(angle, angle, turns[:, 0:1], 3.1415925, ALU.add, ALU.min))
            olink(dve.tensor_scalar(TRIG[:, :], angle, -3.1415925, None, ALU.max))
            dve.sem_inc(s_prod, 1)
            dve.wait_ge(s_ssx, TT)
            dve.tensor_scalar(MS, SS, 1.0 / D, EPS, ALU.mult, ALU.add).then_inc(s_msx, 1)

            with dve.Fori(0, L) as l:
                chain = [0]

                def link(ins):
                    chain[0] += 1
                    ins.then_inc(s_dch, 1)
                    dve.wait_ge(s_dch, chain[0])

                def signal(ins, q, n=1):
                    link(ins)
                    dve.sem_inc(q, n)

                def acc_ready(name):
                    dve.wait_ge(s_acc, ACC[name] + 1)
                    return acc_bank(name)

                dve.wait_ge(s_rsx, l + 1)
                dve.sem_inc(s_tick, 1)
                for t in range(TT):
                    if t == 3:
                        dve.wait_ge(s_tr, TRN[("H", 0, 1)] + 1)
                    signal(dve.tensor_scalar(HR[t % 3], X[:, t, :], RS[:, t:t + 1], None, ALU.mult), s_hr)

                def ada_row(j):
                    bank, free, _ = acc_ready(("A", j))
                    row = MOD[:, j // 2, (j % 2) * CH:(j % 2 + 1) * CH]
                    signal(dve.tensor_tensor(row, bank[:, :], row, ALU.add), free)

                def in_low(u):
                    dve.wait_ge(s_inh, u + 1)
                    dve.tensor_tensor(in_half(W_L[in_slot(u)], u), in_half(SLOT[in_slot(u)], u), in_place(u).bitcast(F32),
                                      ALU.subtract).then_inc(s_inl, 1)

                for h, j in enumerate((1, 3)):
                    if j < 2:
                        dve.wait_ge(s_ada[j], l * 16 + 16)
                        dve.sem_inc(s_tick, 1)
                    else:
                        dve.wait_ge(s_load[chunk_slot(j)], slot_count(j))
                    w = SLOT[2 + j].rearrange("p (k n) -> p k n", k=KT)
                    link(dve.tensor_scalar(ADS[h], w[:, 0, :], COND[:, 0:1], None, ALU.mult))
                    for k in range(1, KT):
                        link(dve.scalar_tensor_tensor(ADS[h], w[:, k, :], COND[:, k:k + 1], ADS[h], ALU.mult, ALU.add))
                    dve.sem_inc(s_msum, 1)

                turned_out(dve, "P")
                turned_out(dve, ("H", 3, 0))
                turned_out(dve, ("H", 3, 1))
                dve.wait_ge(s_mcol, 4)
                link(dve.tensor_tensor(MCOL[:, :], PS[4][:, 0:2 * KT], COLS[:, R_BADA:R_BADA + 2 * KT], ALU.add))
                shift, scale = MCOL[:, 0:KT], MCOL[:, KT:2 * KT]
                link(dve.scalar_tensor_tensor(scale, scale, 1.0, COLS[:, R_NW1:R_NW1 + KT], ALU.add, ALU.mult))

                def normed_low(k):
                    dve.wait_ge(s_hnh, k + 1)
                    dve.tensor_tensor(HN_L[:, k, :], HT[:, k, :], HN_H[:, k, :].bitcast(F32), ALU.subtract).then_inc(s_hnl, 1)

                for k in range(KT):
                    signal(dve.tensor_scalar(HT[:, k, :], HT[:, k, :], scale[:, k:k + 1], shift[:, k:k + 1], ALU.mult, ALU.add), s_hm)
                    if k == 1:
                        in_low(0)
                    if k:
                        normed_low(k - 1)
                normed_low(KT - 1)
                in_low(1)
                dve.wait_ge(s_par2, N_PAR2)
                lam = BC[:, B_LAM:B_LAM + 256]
                for k in range(2):
                    link(dve.tensor_tensor(LPR[:, 64 * k:64 * k + 64], lam[:, 128 * k:128 * k + 64], lam[:, 128 * k + 64:128 * k + 128], ALU.mult))
                signal(dve.tensor_reduce(LT, LPR.rearrange("p (k d) -> p k d", k=2), AX, ALU.add), s_lam)
                for m in range(16):
                    bank, free, _ = acc_ready(("X", m))
                    if m >= 2:
                        dve.wait_ge(s_sx, m - 1)
                    w = lambda k: COLS[:, R_CW + 16 * k + m:R_CW + 16 * k + m + 1]
                    link(dve.tensor_scalar(CV[m % 2], bank[:, :], w(SC - 1), COLS[:, R_CB + m:R_CB + m + 1], ALU.mult, ALU.add))
                    for back in range(1, SC):
                        ins = dve.scalar_tensor_tensor(CV[m % 2][:, back:], bank[:, 0:T - back], w(SC - 1 - back), CV[m % 2][:, back:],
                                                       ALU.mult, ALU.add)
                        link(ins)
                    dve.sem_inc(free, 1)
                    dve.sem_inc(s_conv, 1)
                    if m % 2 == 0:
                        if m:
                            in_low(m // 2 + 1)
                in_low(9)
                in_low(10)
                in_low(11)
                def per_chunk(v):
                    return v.rearrange("p (a h) -> p a h", a=1).broadcast_to([P, TT, SH])

                bank, free, _ = acc_ready("DT")
                signal(dve.tensor_tensor(DTT, bank[:, 0:TT * SH].rearrange("p (t h) -> p t h", t=TT), per_chunk(BC[:, B_DTB:B_DTB + SH]), ALU.add), free)
                dve.sem_inc(s_dt1, 1)
                dve.wait_ge(s_dt2, 1)
                link(dve.scalar_tensor_tensor(flat(DTT), flat(DTT), 0.0, flat(EACS), ALU.max, ALU.add))
                signal(dve.scalar_tensor_tensor(ADT, DTT, -1.0, per_chunk(ANEG), ALU.mult, ALU.mult), s_adt)
                dve.wait_ge(s_dt2, 2)
                link(dve.tensor_tensor(LAM, LT[:, 0:1], LT[:, 1:2], ALU.subtract))
                link(dve.tensor_tensor(LAM, LAM, BC[:, B_LI:B_LI + 1], ALU.add))
                link(dve.tensor_tensor(SUBW, COLS[:, R_SUB:R_SUB + 1], BC[:, B_LI + 1:B_LI + 2], ALU.mult))
                bank, free, _ = acc_ready("AC")
                cs, tot = bank[:, 0:TT * SH], bank[:, TT * SH:2 * TT * SH]
                link(dve.tensor_copy(flat(ACS), cs))
                dve.tensor_scalar(flat(NACS), cs, -1.0, None, ALU.mult)
                dve.tensor_tensor(flat(STMP), tot, flat(ACS), ALU.subtract)
                signal(dve.tensor_copy(flat(ETOT), tot), free)
                dve.sem_inc(s_acs, 1)
                dve.wait_ge(s_dec, 1)
                turned_out(dve, ("T", 10))
                turned_out(dve, ("T", 11))
                dve.wait_ge(s_late, 32)

                def heads(v, n=SH):
                    return v.rearrange("p (h d) -> p h d", h=n)

                def each(v, n):
                    return v.rearrange("p (h a) -> p h a", a=1).broadcast_to([P, n, SP_])

                def norm_chunk(cc):
                    dve.wait_ge(s_ssg, 2 * cc + 2)
                    signal(dve.tensor_scalar(MSG[:, cc, :], SSG[:, cc, :], 1.0 / 256, EPS, ALU.mult, ALU.add), s_msg)
                    dve.wait_ge(s_rsg, cc + 1)
                    for g in range(SG):
                        zg = Z[:, cc, 256 * g:256 * g + 256]
                        ins = dve.scalar_tensor_tensor(zg, zg, RSG[:, cc, g:g + 1], SNW[:, 256 * g:256 * g + 256], ALU.mult, ALU.mult)
                    signal(ins, s_ynn)

                for cc in range(TT):
                    if cc >= 1:
                        dve.wait_ge(s_st, 2 * cc)
                    link(dve.tensor_tensor(heads(XW), heads(XS[:, cc, :]), each(DTT[:, cc, :], SH), ALU.mult))
                    if cc < TT - 1:
                        link(dve.tensor_tensor(heads(XD), heads(XW), each(DEND[:, cc, :], SH), ALU.mult))
                    dve.sem_inc(s_xw, 1)
                    for g in range(SG):
                        dve.wait_ge(s_cb, cc + 1)
                        dve.wait_ge(s_mx, 4 * cc + g + 1)
                        cb = PS[4][:, g * P:(g + 1) * P].rearrange("p (a l) -> p a l", a=1).broadcast_to([P, 4, P])
                        signal(dve.tensor_tensor(MT[g % 2], MT[g % 2], cb, ALU.mult), s_mt)
                        if g % 2 == 0:
                            continue
                        hf, hs = g // 2, slice(8 * (g // 2), 8 * (g // 2) + 8)
                        cols = slice(512 * hf, 512 * hf + 512)
                        link(dve.tensor_tensor(heads(YT2, 8), heads(XS[:, cc, cols], 8), each(BC[:, B_D + 8 * hf:B_D + 8 * hf + 8], 8), ALU.mult))
                        dve.wait_ge(s_st, 2 * cc + hf + 1)
                        if cc:
                            link(dve.tensor_tensor(heads(YT1, 8), heads(PS[6][:, :], 8), each(EACS[:, cc, hs], 8), ALU.mult))
                            link(dve.tensor_tensor(YT1, YT1, PS[5][:, :], ALU.add))
                        else:
                            link(dve.tensor_copy(YT1, PS[5][:, :]))
                        dve.sem_inc(s_ydf, 1)
                        link(dve.tensor_tensor(YT1, YT1, YT2, ALU.add))
                        signal(dve.tensor_tensor(Z[:, cc, cols], YT1, Z[:, cc, cols], ALU.mult), s_yn)
                        if cc < TT - 1:
                            if cc:
                                link(dve.tensor_tensor(heads(ST[:, cols], 8), heads(ST[:, cols], 8), each(ETOT[:, cc, hs], 8), ALU.mult))
                                link(dve.tensor_tensor(ST[:, cols], ST[:, cols], PS[7][:, :], ALU.add))
                            else:
                                link(dve.tensor_copy(ST[:, cols], PS[7][:, :]))
                            dve.sem_inc(s_ste, 1)
                        if hf == 0 and cc >= 1:
                            norm_chunk(cc - 1)
                norm_chunk(TT - 1)

                dve.wait_ge(s_pos, 16)
                posf = PB[1]
                link(dve.tensor_copy(posf, POSR.bitcast(I32)))
                for i in range(TT):
                    n = (i + 1) * P
                    link(dve.tensor_scalar(DIST[:, i, 0:n], posf[:, 0:n], POSQ[:, i:i + 1], None, ALU.subtract))
                    link(dve.scalar_tensor_tensor(DIST[:, i, 0:n], DIST[:, i, 0:n], -1.0, DIST[:, i, 0:n], ALU.mult, ALU.max))
                    link(dve.tensor_tensor(DIST[:, i, 0:n], DIST[:, i, 0:n], CON[:, C_CM + 512 - n:C_CM + 512], ALU.subtract))

                def maxima(b, n, scale, count):
                    link(dve.tensor_reduce(MX[:, b:b + 1], PB[b][:, 0:n], AX, ALU.max))
                    signal(dve.tensor_scalar(NB_[:, b:b + 1], MX[:, b:b + 1], -scale, None, ALU.mult), s_nb)

                def diff_scores(u):
                    h, i = u // 4, u % 4
                    n = (i + 1) * P
                    if u >= 2:
                        dve.wait_ge(s_tp, u - 1)
                    for m in range(2):
                        b = (2 * u + m) % 4
                        dve.wait_ge(s_sc, 2 * u + m + 1)
                        signal(dve.scalar_tensor_tensor(PB[b][:, 0:n], DIST[:, i, 0:n], -SLOPES[h] / DIFF_SCALE, PS[2 + b][:, 0:n],
                                                        ALU.mult, ALU.add), s_scf)
                        maxima(b, n, DIFF_SCALE, 2 * u + m)

                def diff_probs(u):
                    i, b = u % 4, 2 * (u % 2)
                    n = (i + 1) * P
                    dve.wait_ge(s_ex, 2 * u + 2)
                    link(dve.reciprocal(RR[:, b:b + 2], SE[:, b:b + 2]))
                    link(dve.tensor_tensor(RR[:, b + 1:b + 2], RR[:, b + 1:b + 2], LAM, ALU.mult))
                    link(dve.tensor_scalar(PB[b + 1][:, 0:n], PB[b + 1][:, 0:n], RR[:, b + 1:b + 2], None, ALU.mult))
                    signal(dve.scalar_tensor_tensor(PB[b][:, 0:n], PB[b][:, 0:n], RR[:, b:b + 1], PB[b + 1][:, 0:n], ALU.mult, ALU.subtract), s_at)

                def rotate(dst, bank, free, done):
                    link(dve.tensor_tensor(dst, bank[0:64, :], TRIG[0:64, :], ALU.mult))
                    signal(dve.tensor_tensor(ROT[0:64, :], bank[64:128, :], TRIG[64:128, :], ALU.mult), free)
                    signal(dve.tensor_tensor(dst, dst, ROT[0:64, :], ALU.add), done)

                def filled(name):
                    kind, m = name
                    if kind == "A":
                        ada_row(m)
                        return
                    bank, free, _ = acc_ready(name)
                    if m == 3:
                        rotate(KPE[0:64, :], bank, free, s_kpe)
                    else:
                        signal(dve.tensor_copy(CQT[:, m, :] if m < 2 else CKVT, bank[:, :]), free)

                dve.wait_ge(s_bada, 16)
                for u in range(21):
                    if u < 16:
                        diff_scores(u)
                    if head_ends(u - 1):
                        h = (u - 8) // 4
                        dve.wait_ge(s_rst, h + 1)
                        signal(dve.scalar_tensor_tensor(YA[:, 1, h, :], PS[7][:, :], SUBW, RSB, ALU.mult, ALU.mult), s_ya)
                    if 1 <= u <= 16:
                        diff_probs(u - 1)
                    if u - 1 in DIFF_FILL:
                        filled(DIFF_FILL[u - 1])

                dve.wait_ge(s_crs, 1)
                for m in range(2):
                    link(dve.scalar_tensor_tensor(CQT[:, m, :], CQT[:, m, :], COLS[:, R_QN + m:R_QN + m + 1], RSB, ALU.mult, ALU.mult))
                dve.sem_inc(s_cn, 1)
                dve.wait_ge(s_crs, 2)
                signal(dve.scalar_tensor_tensor(CKVT, CKVT, COLS[:, R_KN:R_KN + 1], RSB, ALU.mult, ALU.mult), s_cn)
                for h in range(NH):
                    bank, free, _ = acc_ready(("QP", h))
                    rotate(QP[0:64, h, :], bank, free, s_qpr)

                def mla_scores(u):
                    b, n = u % 4, (u % 4 + 1) * P
                    if u >= 4:
                        dve.wait_ge(s_tp, 16 + u - 3)
                    dve.wait_ge(s_sc, 32 + u + 1)
                    signal(dve.tensor_tensor(PB[b][:, 0:n], PS[2 + b][:, 0:n], CON[:, C_CM + 512 - n:C_CM + 512], ALU.add), s_scf)
                    maxima(b, n, MLA_SCALE, 32 + u)

                def mla_probs(u):
                    b, n = u % 4, (u % 4 + 1) * P
                    dve.wait_ge(s_ex, 32 + u + 1)
                    link(dve.reciprocal(RR[:, b:b + 1], SE[:, b:b + 1]))
                    signal(dve.tensor_scalar(PB[b][:, 0:n], PB[b][:, 0:n], RR[:, b:b + 1], None, ALU.mult), s_at)

                def inputs_low(j):
                    dve.wait_ge(s_yh, j + 1)
                    dve.tensor_tensor(Y_L[j][:, :, :], Y[j], Y_H[j % 2][:, :, :].bitcast(F32), ALU.subtract).then_inc(s_yl, 1)

                def out_low(v):
                    slot = CHN[("O", v // 2)] % 2
                    dve.wait_ge(s_wh, v + 1)
                    dve.tensor_tensor(out_half(W_L[slot], v), out_half(SLOT[slot], v), OUT_H[v % 2][:, :, :].bitcast(F32), ALU.subtract).then_inc(s_wl, 1)

                for u in range(19):
                    if u < 16:
                        mla_scores(u)
                    if 1 <= u <= 16:
                        mla_probs(u - 1)
                    if u - 1 in MLA_FILL:
                        filled(MLA_FILL[u - 1])
                    if u >= 6 and (u - 6) % 4 == 0:
                        h = (u - 6) // 4
                        dve.wait_ge(s_pv, NH + h + 1)
                        signal(dve.tensor_copy(YA[:, 0, h, :], PS[7][:, :]), s_ya)
                    if u == 17:
                        inputs_low(0)
                        out_low(0)
                out_low(1)
                inputs_low(1)
                link(dve.scalar_tensor_tensor(MOD[:, 4], MOD[:, 4], 1.0, NW2, ALU.add, ALU.mult))

                for j in range(1, 4):
                    out_low(2 * j)
                    out_low(2 * j + 1)
                    if j < 3:
                        inputs_low(j + 1)

                def residual(t):
                    if t >= 3:
                        dve.wait_ge(s_nt, t - 2)
                        dve.wait_ge(s_h2st, 16 * (t - 2))
                    dve.wait_ge(s_o, t + 1)
                    for q in range(2):
                        cols = slice(q * CH, (q + 1) * CH)
                        link(dve.tensor_tensor(H2R[t % 3][:, cols], PS[2 * t + q][:, :], MOD[:, 2, cols], ALU.mult))
                    signal(dve.tensor_tensor(X[:, t, :], X[:, t, :], H2R[t % 3], ALU.add), s_xr)

                def norm2(t):
                    dve.wait_ge(s_ss2, t + 1)
                    signal(dve.tensor_scalar(MS[:, t:t + 1], SS[:, t:t + 1], 1.0 / D, EPS, ALU.mult, ALU.add), s_ms)
                    dve.wait_ge(s_rs, t + 1)
                    link(dve.scalar_tensor_tensor(H2R[t % 3], X[:, t, :], RS[:, t:t + 1], MOD[:, 4], ALU.mult, ALU.mult))
                    signal(dve.tensor_tensor(H2R[t % 3], H2R[t % 3], MOD[:, 3], ALU.add), s_h2)

                residual(0)
                for t in range(TT):
                    norm2(t)
                    if t + 1 < TT:
                        residual(t + 1)

                for t in range(TT):
                    dve.wait_ge(s_lg, t + 1)
                    dve.tensor_tensor(GL[:, t, :], PS[2 * t][:, 0:NG], BC[:, B_RB:B_RB + NG], ALU.add)
                    link(dve.tensor_tensor(EL[:, t, :], PS[2 * t][:, NG:NG + NE], BC[:, B_RB + NG:B_RB + NG + NE], ALU.add))

                def per_token(v, n):
                    return v.rearrange("p (t a) -> p t a", a=1).broadcast_to([P, TT, n])

                def per_entry(v, n):
                    return v.rearrange("p (a e) -> p a e", a=1).broadcast_to([P, TT, n])

                def first_of_max(oh, v, best, order, n):
                    link(dve.tensor_reduce(best, v, AX, ALU.max))
                    link(dve.tensor_tensor(oh, v, per_token(best, n), ALU.is_equal))
                    link(dve.tensor_tensor(oh, oh, per_entry(order, n), ALU.mult))
                    link(dve.tensor_reduce(RV, oh, AX, ALU.max))
                    link(dve.tensor_tensor(oh, oh, per_token(RV, n), ALU.is_equal))

                first_of_max(PEN, GL, RM, CON[:, C_D4:C_D4 + 4], NG)
                signal(dve.tensor_tensor(GE, GL, per_token(RM, NG), ALU.subtract), s_ge)
                link(dve.tensor_scalar(flat(PEN), flat(PEN), -1.0, -NEG, ALU.add, ALU.mult))
                by_group = lambda v: v.rearrange("p t (g e) -> p (t g) e", g=NG)
                link(dve.tensor_tensor(by_group(LM), by_group(EL),
                                       flat(PEN).rearrange("p (a b) -> p a b", b=1).broadcast_to([P, TT * NG, NE_G]), ALU.add))
                first_of_max(OH1, LM, R1, CON[:, C_D32:C_D32 + 32], NE)
                link(dve.scalar_tensor_tensor(flat(LM), flat(OH1), 2 * NEG, flat(LM), ALU.mult, ALU.add))
                first_of_max(OH2, LM, R2, CON[:, C_D32:C_D32 + 32], NE)
                signal(dve.tensor_tensor(RW, R2, R1, ALU.subtract), s_ge)
                signal(dve.tensor_tensor(MM, OH1, OH2, ALU.add), s_oh)
                dve.wait_ge(s_gf, 2)
                link(dve.tensor_reduce(R3, GE, AX, ALU.add))
                link(dve.reciprocal(R3, R3))
                link(dve.tensor_scalar(R4, RW, 1.0, None, ALU.add))
                link(dve.reciprocal(R4, R4))
                link(dve.tensor_tensor(R3, R3, R4, ALU.mult))
                weight = PAY[:, :, :, :].bitcast(F32)
                link(dve.tensor_copy(weight[:, :, 0, 2], R3))
                link(dve.tensor_tensor(weight[:, :, 1, 2], R3, RW, ALU.mult))
                dve.wait_ge(s_pp, 1)
                cnt = PS[1][0:NE, 64:65]
                for k, limit in enumerate((P, 2 * P, 3 * P)):
                    link(dve.tensor_scalar(OVT[:, k:k + 1], cnt, float(limit), None, ALU.is_gt))
                link(dve.tensor_tensor(OVT[:, 0:1], OVT[:, 0:1], OVT[:, 1:2], ALU.add))
                link(dve.tensor_tensor(OVT[:, 0:1], OVT[:, 0:1], OVT[:, 2:3], ALU.add))
                signal(dve.tensor_scalar(OVR, ONE[0:NE, :], OVT[:, 0:1], None, ALU.mult), s_ovt)
                link(dve.tensor_copy(flat(POS), PS[0][:, 0:TT * NE]))
                link(dve.tensor_scalar(flat(BLK), flat(POS), float(P), None, ALU.is_ge))
                for limit in (2 * P, 3 * P):
                    link(dve.scalar_tensor_tensor(flat(BLK), flat(POS), float(limit), flat(BLK), ALU.is_ge, ALU.add))
                link(dve.scalar_tensor_tensor(flat(ROWF), flat(BLK), -float(P), flat(POS), ALU.mult, ALU.add))
                e32 = per_entry(CON[:, C_E32:C_E32 + 32], NE)
                link(dve.tensor_tensor(TMPE, BLK, e32, ALU.subtract))
                dve.wait_ge(s_ov2, 1)
                link(dve.scalar_tensor_tensor(TMPE, TMPE, float(NE - 1), per_entry(PS[2][:, 0:NE], NE), ALU.add, ALU.add))
                link(dve.scalar_tensor_tensor(flat(TMPE), flat(BLK), 0.0, flat(TMPE), ALU.is_gt, ALU.mult))
                link(dve.tensor_tensor(TMPE, TMPE, e32, ALU.add))
                link(dve.scalar_tensor_tensor(flat(ROWF), flat(ROWF), float(NB_MAX), flat(TMPE), ALU.mult, ALU.add))
                chosen = YA[:, 1, 0, 256:512].rearrange("p (s n) -> p s n", s=2)
                picked = YA[:, 1, 2, 256:512]
                link(dve.tensor_tensor(picked.rearrange("p (s n) -> p s n", s=2), chosen,
                                       flat(ROWF).rearrange("p (a n) -> p a n", a=1).broadcast_to([P, 2, TT * NE]), ALU.mult))
                link(dve.tensor_reduce(RROW, picked.rearrange("p (k e) -> p k e", e=NE), AX, ALU.add))
                signal(dve.tensor_copy(ROWI[:, :].rearrange("p (t s) -> p s t", s=2), RROW.rearrange("p (s t) -> p s t", s=2)), s_row)
                link(dve.tensor_copy(OVE, PS[2][:, 64:64 + NE]))
                row0 = lambda v, n: v.rearrange("p (a e) -> p a e", a=1).broadcast_to([1, 8, n])
                link(dve.tensor_tensor(KCMP, row0(OVE[0:1, :], NE),
                                       CON[0:1, C_K8:C_K8 + 8].rearrange("p (k a) -> p k a", a=1).broadcast_to([1, 8, NE]), ALU.is_le))
                link(dve.tensor_reduce(NPF[:, 0:8], KCMP, AX, ALU.add))
                link(dve.tensor_scalar(EID[0:1, 32:40], NPF[:, 0:8], float(NE - 1), None, ALU.min))
                over = PS[2][0:1, 128:129]
                link(dve.tensor_scalar(NPF[:, 8:9], over, 0.0, 15.0, ALU.is_gt, ALU.add))
                for limit in (2.0, 4.0, 6.0):
                    link(dve.scalar_tensor_tensor(NPF[:, 8:9], over, limit, NPF[:, 8:9], ALU.is_gt, ALU.add))
                signal(dve.tensor_copy(EID[0:1, 41:42], NPF[:, 8:9]), s_eid)

                more = more_pairs(dve)
                dve.sem_inc(s_ye, 1)

                def low(i, v):
                    slot, half, kind = unit_matrix(v % UNITS)
                    dve.wait_ge(s_hi, i * UNITS + (v + 1))
                    dve.tensor_tensor(unit_of(W_L[slot], v, half), unit_of(SLOT[slot], v, half),
                                      unit_of(W_H[v % 4], v).bitcast(F32), ALU.subtract).then_inc(s_lo, 1)

                def rows_low(s, count):
                    dve.wait_ge(s_xh, count)
                    dve.tensor_tensor(XG_L[s][:, 0:4, :], tiles4(PS[0]), XG_H[s][:, 0:4, :].bitcast(F32), ALU.subtract)
                    dve.tensor_tensor(XG_L[s][:, 4:8, :], tiles4(PS[1]), XG_H[s][:, 4:8, :].bitcast(F32), ALU.subtract).then_inc(s_xl, 1)

                def hidden(i, s):
                    dve.wait_ge(s_gs, i * 2 + (s + 1))
                    dve.wait_ge(s_unit, i * UNITS + (4 * s + 4))
                    weight = TBL[:, bass.ds(i * 2 + s, 1), 2:3].rearrange("p a b -> p (a b)").bitcast(F32)
                    dve.scalar_tensor_tensor(HH, PS[3][:, :], weight, GS, ALU.mult, ALU.mult).then_inc(s_hh, 1)

                def hidden_low(s, count):
                    dve.wait_ge(s_hth, count)
                    dve.tensor_tensor(HH_L[s][:, :, :], tiles4(PS[4]), HH_H[s][:, :, :].bitcast(F32), ALU.subtract).then_inc(s_htl, 1)

                def output_half(i, v):
                    s, q = divmod(v - 8, 2)
                    if q == 0:
                        dve.wait_ge(s_slot[s], i + 1)
                    dve.wait_ge(s_unit, i * UNITS + (v + 1))
                    cols = slice(q * CH, (q + 1) * CH)
                    dve.tensor_tensor(YB[s][:, cols], down_bank(v)[:, :], MOD[:, 5, cols], ALU.mult).then_inc(s_ye, 1)

                def pair(i, ahead):
                    low(i, 4)
                    rows_low(1, i * 2 + 2)
                    low(i, 5)
                    low(i, 6)
                    hidden(i, 0)
                    low(i, 7)
                    low(i, 8)
                    hidden_low(0, i * 2 + 1)
                    low(i, 9)
                    hidden(i, 1)
                    low(i, 10)
                    output_half(i, 8)
                    hidden_low(1, i * 2 + 2)
                    low(i, 11)
                    output_half(i, 9)
                    if ahead:
                        low(i, 12)
                        rows_low(0, i * 2 + 3)
                        low(i, 13)
                    output_half(i, 10)
                    if ahead:
                        low(i, 14)
                    output_half(i, 11)
                    if ahead:
                        low(i, 15)

                for v in range(4):
                    low(0, v)
                rows_low(0, 1)
                with dve.Fori(0, more) as i:
                    pair(i, True)
                pair(more, False)
                for t in range(TT):
                    dve.wait_ge(s_cmb[t], 16)
                    link(dve.tensor_tensor(CB[t][:, 0:D], CB[t][:, 0:D], CB[t][:, D:2 * D], ALU.add))
                    signal(dve.tensor_tensor(X[:, t, :], X[:, t, :], CB[t][:, 0:D], ALU.add), s_res)
                dve.wait_ge(s_ssx, l * TT + 2 * TT)
                dve.tensor_scalar(MS, SS, 1.0 / D, EPS, ALU.mult, ALU.add).then_inc(s_msx, 1)
                dve.sem_inc(s_end, 1)
                dve.wait_ge(s_clr, l + 1)
                dve.sem_inc(s_tick, 1)
            dve.wait_ge(s_rsx, L + 1)
            dve.wait_ge(s_fw, 16)
            for t in range(TT):
                dve.scalar_tensor_tensor(X[:, t, :], X[:, t, :], RS[:, t:t + 1], MOD[:, 0], ALU.mult, ALU.mult).then_inc(s_fout, 1)

        @block.tensor
        def _(pe):
            pe.wait_ge(s_con, 80)
            pe.transpose(PS[2][:, 0:KT], CROW, ID[0:KT, 0:KT]).then_inc(s_pro, 1)
            pe.wait_ge(s_proa, 2)
            ln = dict(start=True, stop=True)

            with pe.Fori(0, L) as l:
                def begin(name):
                    bank, free, k = acc_bank(name)
                    if k >= 2:
                        pe.wait_ge(free, k - 1)
                    return bank

                def begin_tr(name):
                    bank, free, k = tr_bank(name)
                    if k >= 2:
                        pe.wait_ge(free, k - 1)
                    return bank

                def chunk(name):
                    n = CHN[name]
                    if n < 2:
                        pe.wait_ge(s_ada[n], l * 16 + 16)
                        return SLOT[chunk_slot(n)]
                    pe.wait_ge(s_load[chunk_slot(n)], slot_count(n))
                    return SLOT[chunk_slot(n)]

                def tile_of(v, t):
                    return v[:, t * P:(t + 1) * P]

                def turn(bank, blocks, done):
                    for j, v in enumerate(blocks):
                        ins = pe.transpose(bank[:, j * P:(j + 1) * P], v, ID)
                    ins.then_inc(done, 1)

                def ada(j):
                    w = chunk(("A", j)).rearrange("p (k n) -> p k n", k=KT)
                    bank = begin(("A", j))
                    for k in range(KT):
                        ins = pe.matmul(bank[:, :], COND[:, k:k + 1].broadcast_to([P, P]), w[:, k, :], start=(k == 0), stop=(k == KT - 1))
                    ins.then_inc(s_acc, 1)

                def project(name, lhs, rhs):
                    bank = begin(name)
                    n = len(lhs)
                    for k in range(n):
                        ins = pe.matmul(bank[:, :], lhs[k], rhs[k], start=(k == 0), stop=(k == n - 1))
                    ins.then_inc(s_acc, 1)

                def in_feature(name, j, m):
                    w = chunk(("I", j)).rearrange("p (k n) -> p k n", k=KT)
                    project(name, [tile_of(w[:, k, :], m) for k in range(KT)], [HT[:, k, :] for k in range(KT)])

                def in_token(name, j, t):
                    w = chunk(("I", j)).rearrange("p (k n) -> p k n", k=KT)
                    project(name, [tile_of(HT[:, k, :], t) for k in range(KT)], [w[:, k, :] for k in range(KT)])

                for t in range(TT):
                    pe.wait_ge(s_hr, t + 1)
                    for q in range(2):
                        turn(begin_tr(("H", t, q)), [tile_of(HR[t % 3], 4 * q + k) for k in range(4)], s_tr)

                def ada_columns(j):
                    if j % 2:
                        pe.wait_ge(s_msum, j // 2 + 1)
                        src, pick = ADS[j // 2], ONE[:, 0:1]
                    else:
                        pe.wait_ge(s_mrow, j // 2 + 1)
                        src, pick = MOD[:, j // 2, 0:CH], ID[:, 0:1]
                    for b in range(4):
                        ins = pe.matmul(PS[4][:, 4 * j + b:4 * j + b + 1], tile_of(src, b), pick, **ln)
                    ins.then_inc(s_mcol, 1)

                ada(0)
                ada_columns(0)
                ada_columns(1)
                ada(2)
                pe.wait_ge(s_par, N_PAR)
                bank = begin_tr("P")
                pe.transpose(bank[:, 0:R_N], ROWS, ID[0:R_N, 0:R_N]).then_inc(s_tr, 1)
                ada_columns(2)
                ada_columns(3)
                def token_major(m):
                    bank = begin_tr(("T", m))
                    pe.wait_ge(s_sx, m + 1)
                    src = SX[m % 2] if m < 8 else BT[:, m - 8, :]
                    turn(bank, [tile_of(src, t) for t in range(TT)], s_tr)

                def three(out_, k, a_h, a_l, b_h, b_l):
                    pe.matmul(out_, a_h, b_h, start=(k == 0), stop=False)
                    pe.matmul(out_, a_h, b_l, start=False, stop=False)
                    return pe.matmul(out_, a_l, b_h, start=False, stop=(k == KT - 1))

                for m in range(16):
                    u = m // 2
                    bank = begin(("X", m))
                    pe.wait_ge(s_inl, u + 1)
                    w_h, w_l = in_place(u), in_half(W_L[in_slot(u)], u)
                    for k in range(KT):
                        if m == 0:
                            pe.wait_ge(s_hnl, k + 1)
                        ins = three(bank[:, :], k, tile_of(w_h[:, k, :], m % 2), tile_of(w_l[:, k, :], m % 2), HN_H[:, k, :], HN_L[:, k, :])
                    ins.then_inc(s_acc, 1)
                    if 1 <= m <= 12:
                        token_major(m - 1)
                for u in range(X_UNITS, X_UNITS + 4):
                    c, half = u // 2 - 4, u % 2
                    pe.wait_ge(s_inl, u + 1)
                    w_h, w_l = in_place(u), in_half(W_L[in_slot(u)], u)
                    for t in range(TT):
                        if c and not half:
                            pe.wait_ge(s_zf, t + 1)
                        for k in range(4):
                            at = 4 * half + k
                            ins = three(PS[4 + t][:, :], at, tile_of(HN_H[:, at, :], t), tile_of(HN_L[:, at, :], t), w_h[:, k, :], w_l[:, k, :])
                        if half:
                            ins.then_inc(s_z, 1)
                    if not half:
                        ins.then_inc(s_zu, 1)
                pe.wait_ge(s_zf, 2 * TT)
                pe.wait_ge(s_par2, N_PAR2)
                bank = begin("DT")
                for t in range(TT):
                    for k in range(KT):
                        ins = pe.matmul(bank[:, t * SH:(t + 1) * SH], tile_of(HT[:, k, :], t), WDT[:, k, :], start=(k == 0), stop=(k == KT - 1))
                ins.then_inc(s_acc, 1)
                bank = begin("AC")
                pe.wait_ge(s_adt, 1)
                pe.matmul(bank[:, 0:TT * SH], UU, flat(ADT), **ln)
                pe.matmul(bank[:, TT * SH:2 * TT * SH], ONE, flat(ADT), **ln).then_inc(s_acc, 1)
                bank = begin_tr("AT")
                pe.wait_ge(s_acs, 1)
                pe.transpose(bank[0:TT * SH, 0:P], flat(ACS), ID).then_inc(s_tr, 1)
                turned_out(pe, "AT")
                pe.wait_ge(s_sx, 16)

                def decay_rows(cc, g):
                    bank = begin(("R", cc, g))
                    pe.matmul(bank[:, :], IDB[:, :], CMB[:, :].rearrange("p (a l) -> p a l", a=1).broadcast_to([P, 4, P]), start=True, stop=False)
                    for h in range(4):
                        j = cc * SH + 4 * g + h
                        ins = pe.matmul(tile_of(bank, h), ID[0:TT * SH, j:j + 1].broadcast_to([TT * SH, P]), ACST,
                                        start=False, stop=(h == 3))
                    ins.then_inc(s_acc, 1)

                def ssd_group(cc, g):
                    hf = g // 2
                    pe.wait_ge(s_mt, 4 * cc + g + 1)
                    if g % 2 == 0 and cc + hf:
                        pe.wait_ge(s_ydf, 2 * cc + hf)
                    for h in range(4):
                        at = (4 * (g % 2) + h) * SP_
                        ins = pe.matmul(PS[5][:, at:at + SP_], MT[g % 2][:, h, :], XW[:, (4 * g + h) * SP_:(4 * g + h + 1) * SP_], **ln)
                    ins.then_inc(s_yd, 1)
                    half = slice((g % 2) * 256, (g % 2) * 256 + 256)
                    cols = slice(g * 256, g * 256 + 256)
                    last = g % 2 == 1
                    if cc:
                        if g % 2 == 0:
                            pe.wait_ge(s_ste, 2 * (cc - 1) + hf + 1)
                        ins = pe.matmul(PS[6][:, half], tile_of(CT[:, g, :], cc), ST[:, cols], **ln)
                        if last and cc == TT - 1:
                            ins.then_inc(s_st, 1)
                    if cc < TT - 1:
                        if g % 2 == 0 and cc + hf:
                            pe.wait_ge(s_ste, 2 * cc + hf)
                        ins = pe.matmul(PS[7][:, half], tile_of(BTOK[:, cc, :], g), XD[:, cols], **ln)
                        if last:
                            ins.then_inc(s_st, 1)

                def fill(name):
                    kind, m = name
                    if kind == "A":
                        ada(m)
                    elif kind == "DV":
                        in_token(name, 8, m)
                    else:
                        in_feature(name, {"DQ": 6, "DK": 7, "C": 9}[kind], m)

                for cc in range(TT):
                    if cc:
                        pe.wait_ge(s_mt, 4 * cc)
                    for g in range(SG):
                        ins = pe.matmul(tile_of(PS[4], g), tile_of(BT[:, g, :], cc), tile_of(CT[:, g, :], cc), **ln)
                    ins.then_inc(s_cb, 1)
                    decay_rows(cc, 0)
                    decay_rows(cc, 1)
                    fill(SSD_FILL[3 * cc])
                    pe.wait_ge(s_xw, cc + 1)
                    for g in range(SG):
                        ssd_group(cc, g)
                        if g < 2:
                            decay_rows(cc, g + 2)
                        if g % 2:
                            fill(SSD_FILL[3 * cc + 1 + g // 2])

                def transposed(k, buf):
                    pe.wait_ge(s_at, k + 1)
                    if k:
                        pe.wait_ge(s_pt, k)
                    turn(PS[6], [tile_of(buf, j) for j in range(k % 4 + 1)], s_tp)

                def values(h, v):
                    pe.wait_ge(s_pt, 4 * h + 4)
                    if h:
                        pe.wait_ge(s_ya, h)
                    for j in range(TT):
                        ins = pe.matmul(PS[7][:, j * P:T], v[j], PT[:, j, j * P:T], start=(j == 0), stop=(j == TT - 1))
                    ins.then_inc(s_pv, 1)

                def diff_scores(u):
                    h, i = u // 4, u % 4
                    for m in range(2):
                        k = 2 * u + m
                        b, rows = k % 4, slice(64 * m, 64 * m + 64)
                        if k >= 4:
                            pe.wait_ge(s_scf, k - 3)
                        pe.matmul(PS[2 + b][:, 0:(i + 1) * P], DQT[rows, h, i * P:(i + 1) * P], DKT[rows, h, 0:(i + 1) * P], **ln).then_inc(s_sc, 1)

                evacuated(pe, ("DV", 2))
                evacuated(pe, ("DV", 3))
                pe.wait_ge(s_ydf, 8)
                pe.wait_ge(s_ste, 6)
                diff_scores(0)
                for u in range(20):
                    if u < 15:
                        diff_scores(u + 1)
                    if head_ends(u):
                        h = (u - 7) // 4
                        bank = begin(("DS", h))
                        pe.wait_ge(s_sq, h + 1)
                        pe.matmul(bank[:, :], ONE, SQB, **ln).then_inc(s_acc, 1)
                    if u >= 6 and u % 4 == 2:
                        h = (u - 6) // 4
                        values(h, [DVT[:, j, h * P:(h + 1) * P] for j in range(TT)])
                    if 2 <= u <= 17:
                        transposed(u - 2, PB[2 * (u % 2)])
                    if u in DIFF_FILL:
                        fill(DIFF_FILL[u])
                def turn_output(cc):
                    pe.wait_ge(s_ynn, cc + 1)
                    for q in range(2):
                        turn(begin_tr(("Y", cc, q)), [tile_of(Z[:, cc, :], 4 * q + k) for k in range(4)], s_tr)

                pe.wait_ge(s_scf, 32)
                turn_output(0)
                bank = begin("SQ")
                pe.wait_ge(s_csq, 2)
                pe.matmul(bank[:, :], ONE, SQB, start=True, stop=False)
                pe.matmul(bank[:, :], ONE, PB[0], start=False, stop=True).then_inc(s_acc, 1)
                turn_output(1)
                bank = begin("SK")
                pe.wait_ge(s_csq, 3)
                pe.matmul(bank[:, :], ONE, SQB, **ln).then_inc(s_acc, 1)
                turn_output(2)
                turn_output(3)
                w = chunk("U")
                uq = w[:, 0:2048].rearrange("p (k h n) -> p k h n", k=2, h=NH)
                ukv = w[:, 2048:3072].rearrange("p (h n) -> p h n", h=NH)
                pe.wait_ge(s_cn, 1)
                for h in range(NH):
                    project(("QN", h), [uq[:, k, h, 0:P] for k in range(2)], [CQT[:, k, :] for k in range(2)])
                for h in range(NH):
                    project(("QP", h), [uq[:, k, h, P:2 * P] for k in range(2)], [CQT[:, k, :] for k in range(2)])
                pe.wait_ge(s_cn, 2)
                for h in range(NH):
                    project(("KN", h), [ukv[:, h, 0:P]], [CKVT])
                for t in range(TT):
                    bank = begin(("V", t))
                    pe.matmul(bank[:, :].rearrange("p (h n) -> p h n", h=NH), tile_of(CKVT, t), ukv[:, :, P:2 * P], **ln).then_inc(s_acc, 1)

                def mla_scores(u):
                    h, i, b = u // 4, u % 4, u % 4
                    if u >= 4:
                        pe.wait_ge(s_scf, 32 + u - 3)
                    out_, n = PS[2 + b], (i + 1) * P
                    pe.matmul(out_[:, 0:n], tile_of(QN[:, h, :], i), KN[:, h, 0:n], start=True, stop=False)
                    pe.matmul(out_[:, 0:n], tile_of(QP[0:64, h, :], i), KPE[0:64, 0:n], start=False, stop=True).then_inc(s_sc, 1)

                turned_out(pe, ("Y", 3, 0))
                turned_out(pe, ("Y", 3, 1))
                evacuated(pe, ("V", 2))
                evacuated(pe, ("V", 3))
                pe.wait_ge(s_kpe, 1)
                pe.wait_ge(s_qpr, NH)
                mla_scores(0)
                mla_scores(1)
                for u in range(19):
                    if u < 14:
                        mla_scores(u + 2)
                    if u >= 6 and u % 4 == 2:
                        h = (u - 6) // 4
                        values(NH + h, [VT[:, j, h * P:(h + 1) * P] for j in range(TT)])
                    if 2 <= u < 18:
                        transposed(16 + u - 2, PB[(u - 2) % 4])
                    if u in MLA_FILL:
                        fill(MLA_FILL[u])
                def turn_normed(t):
                    pe.wait_ge(s_h2, t + 1)
                    for q in range(2):
                        for k in range(4):
                            ins = pe.transpose(tile_of(PS[2 * t + q], k), tile_of(H2R[t % 3], 4 * q + k), ID)
                    ins.then_inc(s_nt, 1)

                evacuated(pe, ("A", 10))
                evacuated(pe, ("A", 11))
                pe.wait_ge(s_scf, 48)
                pe.wait_ge(s_pt, 32)
                pe.wait_ge(s_ya, 2 * NH)
                def out_group(j, t, q):
                    slot = CHN[("O", j)] % 2
                    w_h, w_l = OUT_H[q], out_half(W_L[slot], q)
                    for f in range(4):
                        first, last = j == 0 and f == 0, j == 3 and f == 3
                        y_h, y_l = (tile_of(v[:, f, :], t) for v in (Y_H[j % 2], Y_L[j]))
                        pe.matmul(PS[2 * t + q][:, :], y_h, w_h[:, f, :], start=first, stop=False)
                        pe.matmul(PS[2 * t + q][:, :], y_h, w_l[:, f, :], start=False, stop=False)
                        ins = pe.matmul(PS[2 * t + q][:, :], y_l, w_h[:, f, :], start=False, stop=last)
                    return ins

                for j in range(3):
                    pe.wait_ge(s_yl, j + 1)
                    for q in range(2):
                        pe.wait_ge(s_wl, 2 * j + q + 1)
                        for t in range(TT):
                            ins = out_group(j, t, q)
                        ins.then_inc(s_ou, 1)
                pe.wait_ge(s_yl, 4)
                pe.wait_ge(s_wl, 7)
                out_group(3, 0, 0)
                out_group(3, 1, 0)
                pe.wait_ge(s_wl, 8)
                out_group(3, 0, 1).then_inc(s_o, 1)
                out_group(3, 1, 1).then_inc(s_o, 1)
                for t in range(2, TT):
                    out_group(3, t, 0)
                    out_group(3, t, 1).then_inc(s_o, 1)
                    turn_normed(t - 2)
                def logits(t):
                    pe.wait_ge(s_ntf, t + 1)
                    for k in range(KT):
                        ins = pe.matmul(PS[2 * t][:, 0:NG + NE], tile_of(H2T[:, k, :], t), WR[:, k, :], start=(k == 0), stop=(k == KT - 1))
                    ins.then_inc(s_lg, 1)

                logits(0)
                for t in range(2, TT):
                    turn_normed(t)
                    logits(t - 1)
                logits(TT - 1)
                pe.wait_ge(s_oh, 1)
                for t in range(TT):
                    for before in range(t):
                        pe.matmul(PS[0][:, t * NE:(t + 1) * NE], ONE, MM[:, before, :], start=(before == 0), stop=False)
                    pe.matmul(PS[0][:, t * NE:(t + 1) * NE], SU, MM[:, t, :], start=(t == 0), stop=True)
                for t in range(TT):
                    ins = pe.matmul(PS[1][0:NE, 64:65], MM[:, t, :], ONE[:, 0:1], start=(t == 0), stop=(t == TT - 1))
                ins.then_inc(s_pp, 1)
                pe.wait_ge(s_ovt, 1)
                pe.matmul(PS[2][:, 0:NE], OVR, SU[0:NE, 0:NE], **ln)
                pe.matmul(PS[2][:, 64:64 + NE], OVR, UU[0:NE, 0:NE], **ln)
                pe.matmul(PS[2][:, 128:129], OVR, ONE[0:NE, 0:1], **ln).then_inc(s_ov2, 1)

                more = more_pairs(pe)

                def turn_rows(i, s):
                    pe.wait_ge(s_gd[s], i * 16 + 16)
                    for q in range(2):
                        for k in range(4):
                            ins = pe.transpose(tile_of(PS[q], k), tile_of(XG[s], 4 * q + k), ID)
                    ins.then_inc(s_xt, 1)

                def unit(i, v):
                    slot, half, kind = unit_matrix(v)
                    s = v // 4 % 2 if kind == "in" else (v - 8) // 2
                    pe.wait_ge(s_lo, i * UNITS + (v + 1))
                    w_h, w_l = unit_of(W_H[v % 4], v), unit_of(W_L[slot], v, half)
                    if kind == "in":
                        bank, t_h, t_l = PS[2 + v // 2 % 2], XG_H[s][:, 4 * half:4 * half + 4, :], XG_L[s][:, 4 * half:4 * half + 4, :]
                        first, last = half == 0, half == 1
                    else:
                        bank, t_h, t_l, first, last = down_bank(v), HH_H[s], HH_L[s], True, True
                    for k in range(4):
                        pe.matmul(bank[:, :], t_h[:, k, :], w_h[:, k, :], start=(first and k == 0), stop=False)
                        pe.matmul(bank[:, :], t_h[:, k, :], w_l[:, k, :], start=False, stop=False)
                        ins = pe.matmul(bank[:, :], t_l[:, k, :], w_h[:, k, :], start=False, stop=(last and k == 3))
                    ins.then_inc(s_unit, 1)

                def turn_hidden(i, s):
                    pe.wait_ge(s_hh, i * 2 + (s + 1))
                    for k in range(4):
                        ins = pe.transpose(tile_of(PS[4], k), tile_of(HH, k), ID)
                    ins.then_inc(s_htp, 1)

                def pair(i, ahead):
                    pe.wait_ge(s_xl, i * 2 + 1)
                    unit(i, 0)
                    unit(i, 1)
                    turn_rows(i, 1)
                    unit(i, 2)
                    unit(i, 3)
                    pe.wait_ge(s_xl, i * 2 + 2)
                    pe.wait_ge(s_gs, i * 2 + 1)
                    unit(i, 4)
                    unit(i, 5)
                    turn_hidden(i, 0)
                    unit(i, 6)
                    unit(i, 7)
                    pe.wait_ge(s_htl, i * 2 + 1)
                    pe.wait_ge(s_ye, i * 4 + 1)
                    unit(i, 8)
                    turn_hidden(i, 1)
                    unit(i, 9)
                    if ahead:
                        turn_rows(i + 1, 0)
                    pe.wait_ge(s_htl, i * 2 + 2)
                    unit(i, 10)
                    pe.wait_ge(s_ye, i * 4 + 2)
                    unit(i, 11)

                turn_rows(0, 0)
                with pe.Fori(0, more) as i:
                    pair(i, True)
                pair(more, False)
                pe.sem_inc(s_end, 1)
                pe.wait_ge(s_clr, l + 1)
                pe.sem_inc(s_tick, 1)


INS = ["x", "c", "positions", "w_ada", "b_ada", "norm1_w", "w_in", "mla_q_norm_w", "mla_w_uq", "mla_kv_norm_w", "mla_w_ukv",
       "diff_lambda", "diff_subln_w", "ssd_conv_w", "ssd_conv_b", "ssd_dt_bias", "ssd_a_log", "ssd_d", "ssd_norm_w",
       "w_out", "norm2_w", "router_w_group", "router_b_group", "router_w_expert", "router_b_expert",
       "exp_w_gate", "exp_w_up", "exp_w_down", "final_norm_w"]


def kernel(**inputs):
    import concourse.bacc as bacc
    from concourse.bass_utils import run_bass_kernel_spmd

    nc = bacc.Bacc("TRN2", target_bir_lowering=False, num_devices=1)
    arrays = {f"in_{name}": np.ascontiguousarray(inputs[name]) for name in INS}
    arrays.update({f"in_{name}": a for name, a in shape_constants().items()})
    args = [nc.dram_tensor(n, a.shape, mybir.dt.from_np(a.dtype), kind="ExternalInput").ap() for n, a in arrays.items()]
    out = nc.dram_tensor("out", (1, T, D), F32, kind="ExternalOutput").ap()
    h2_rows = nc.dram_tensor("h2_rows", (T, D), F32, kind="Internal").ap()
    expert_rows = nc.dram_tensor("expert_rows", (2 * T, D), F32, kind="Internal").ap()
    slot_table = nc.dram_tensor("slot_table", (P * NB_MAX, 4), I32, kind="Internal").ap()
    hybrid_kernel(nc, *args, out, h2_rows, expert_rows, slot_table)
    r = run_bass_kernel_spmd(nc, [arrays], core_ids=[0])
    return r.results[0]["out"]
```
